# Optimizing a Trainium2 kernel written in Bass

```python
import math
import jax, jax.numpy as jnp
from jax import lax
import numpy as np

D_MODEL = 1024
BATCH = 1
SEQ = 512
DEPTH = 1

LRU_WIDTH = 512
LRU_HEADS = 8
LRU_HEAD_DIM = LRU_WIDTH // LRU_HEADS
LRU_CONV = 4
LRU_C = 8.0
MOBA_HEADS = 8
MOBA_HEAD_DIM = 64
MOBA_WIDTH = MOBA_HEADS * MOBA_HEAD_DIM
MOBA_BLOCK = 256
MOBA_TOPK = 3
MOBA_Q_CHUNK = 16
MEM_LEN = 256
XATTN_HEADS = 4
XATTN_HEAD_DIM = 128
XATTN_WIDTH = XATTN_HEADS * XATTN_HEAD_DIM
N_BRANCH = 3
IN_COLS = 2 * LRU_WIDTH + 3 * MOBA_WIDTH + XATTN_WIDTH + N_BRANCH * D_MODEL
D_FF = 3 * D_MODEL
FFN_CONV = 3
NORM_EPS = 1e-6


def rms_norm(x, g):
    x32 = x.astype(jnp.float32)
    y = x32 * lax.rsqrt(jnp.mean(x32 * x32, axis=-1, keepdims=True) + NORM_EPS)
    return (y * g.astype(jnp.float32)).astype(x.dtype)

def causal_dwconv(x, w, b):
    k, c = w.shape
    y = lax.conv_general_dilated(x, w[:, None, :].astype(x.dtype), (1,), [(k - 1, 0)],
                                 dimension_numbers=("NWC", "WIO", "NWC"),
                                 feature_group_count=c)
    return y + b.astype(x.dtype)

def rg_lru(x, w_a, b_a, w_x, b_x, lam):
    bsz, s, w = x.shape
    xh = x.reshape(bsz, s, LRU_HEADS, LRU_HEAD_DIM)
    r = jax.nn.sigmoid((jnp.einsum("bshi,hij->bshj", xh, w_a) + b_a).reshape(bsz, s, w).astype(jnp.float32))
    i = jax.nn.sigmoid((jnp.einsum("bshi,hij->bshj", xh, w_x) + b_x).reshape(bsz, s, w).astype(jnp.float32))
    log_a = -LRU_C * r * jax.nn.softplus(-lam.astype(jnp.float32))
    a = jnp.exp(log_a)
    mult = jnp.sqrt(-jnp.expm1(2.0 * log_a))
    u = mult * i * x.astype(jnp.float32)

    def combine(lhs, rhs):
        a1, b1 = lhs
        a2, b2 = rhs
        return a1 * a2, a2 * b1 + b2

    _, h = lax.associative_scan(combine, (a, u), axis=1)
    return h.astype(x.dtype)

def alibi_slopes(n_heads):
    return jnp.exp2(-8.0 * jnp.arange(1, n_heads + 1, dtype=jnp.float32) / n_heads)

def moba_attention(q, k, v):
    bsz, nh, s, dh = q.shape
    nb = -(-s // MOBA_BLOCK)
    sp = nb * MOBA_BLOCK
    pad = ((0, 0), (0, 0), (0, sp - s), (0, 0))
    q, k, v = jnp.pad(q, pad), jnp.pad(k, pad), jnp.pad(v, pad)
    kb = k.reshape(bsz, nh, nb, MOBA_BLOCK, dh)
    vb = v.reshape(bsz, nh, nb, MOBA_BLOCK, dh)
    kmean = jnp.mean(kb.astype(jnp.float32), axis=3)
    n_sel = min(MOBA_TOPK, nb - 1)
    slopes = alibi_slopes(nh)[None, :, None]
    scale = dh ** -0.5
    nq = sp // MOBA_Q_CHUNK
    qc = q.reshape(bsz, nh, nq, MOBA_Q_CHUNK, dh).transpose(2, 0, 1, 3, 4)
    bi = jnp.arange(bsz)[:, None, None, None]
    hi = jnp.arange(nh)[None, :, None, None]
    blk_pos = jnp.arange(MOBA_BLOCK)

    def attend_chunk(args):
        qi, c = args
        t = c * MOBA_Q_CHUNK + jnp.arange(MOBA_Q_CHUNK)
        own = (c * MOBA_Q_CHUNK) // MOBA_BLOCK
        k_own = lax.dynamic_index_in_dim(kb, own, axis=2, keepdims=False)
        v_own = lax.dynamic_index_in_dim(vb, own, axis=2, keepdims=False)
        dist_own = (t[:, None] - (own * MOBA_BLOCK + blk_pos)[None, :]).astype(jnp.float32)
        s_own = (jnp.einsum("bhqd,bhkd->bhqk", qi, k_own, preferred_element_type=jnp.float32) * scale
                 - slopes[..., None] * dist_own)
        s_own = jnp.where(dist_own >= 0, s_own, -jnp.inf)
        if n_sel == 0:
            p = jax.nn.softmax(s_own, axis=-1).astype(v.dtype)
            return jnp.einsum("bhqk,bhkd->bhqd", p, v_own)
        gate = jnp.einsum("bhqd,bhnd->bhqn", qi.astype(jnp.float32), kmean)
        gate = jnp.where(jnp.arange(nb) < own, gate, -jnp.inf)
        _, sel = lax.top_k(gate, n_sel)
        valid = sel < own
        ks = kb[bi, hi, sel]
        vs = vb[bi, hi, sel]
        kpos_sel = sel[..., None] * MOBA_BLOCK + blk_pos
        dist_sel = (t[None, None, :, None, None] - kpos_sel).astype(jnp.float32)
        s_sel = (jnp.einsum("bhqd,bhqnkd->bhqnk", qi, ks, preferred_element_type=jnp.float32) * scale
                 - slopes[..., None, None] * dist_sel)
        s_sel = jnp.where(valid[..., None], s_sel, -jnp.inf)
        nsk = n_sel * MOBA_BLOCK
        scores = jnp.concatenate([s_sel.reshape(bsz, nh, MOBA_Q_CHUNK, nsk), s_own], axis=-1)
        p = jax.nn.softmax(scores, axis=-1).astype(v.dtype)
        p_sel = p[..., :nsk].reshape(bsz, nh, MOBA_Q_CHUNK, n_sel, MOBA_BLOCK)
        p_own = p[..., nsk:]
        return (jnp.einsum("bhqnk,bhqnkd->bhqd", p_sel, vs)
                + jnp.einsum("bhqk,bhkd->bhqd", p_own, v_own))

    out = lax.map(attend_chunk, (qc, jnp.arange(nq)))
    out = out.transpose(1, 2, 0, 3, 4).reshape(bsz, nh, sp, dh)
    return out[:, :, :s]

def memory_cross_attention(q, mem_k, mem_v):
    scores = jnp.einsum("bshd,bmhd->bhsm", q, mem_k, preferred_element_type=jnp.float32) * (XATTN_HEAD_DIM ** -0.5)
    p = jax.nn.softmax(scores, axis=-1).astype(mem_v.dtype)
    o = jnp.einsum("bhsm,bmhd->bshd", p, mem_v)
    return o.reshape(q.shape[0], q.shape[1], XATTN_WIDTH)

def first_inputs(seed: int = 0) -> dict:
    key = jax.random.key(seed)
    ks = jax.random.split(key, 32)
    f32 = jnp.float32

    def nrm(k, shape, scale):
        return jax.random.normal(k, shape, f32) * scale

    def gain(k, shape):
        return 1.0 + 0.02 * jax.random.normal(k, shape, f32)

    u = jax.random.uniform(ks[8], (DEPTH, LRU_WIDTH), f32, 0.9, 0.999)
    sa = u ** (1.0 / LRU_C)
    lru_lambda = jnp.log(sa) - jnp.log1p(-sa)
    return {
        "x": nrm(ks[0], (BATCH, SEQ, D_MODEL), 1.0),
        "mem": nrm(ks[1], (BATCH, MEM_LEN, D_MODEL), 1.0),
        "mix_norm_gain": gain(ks[2], (DEPTH, D_MODEL)),
        "w_in": nrm(ks[3], (DEPTH, D_MODEL, IN_COLS), D_MODEL ** -0.5),
        "lru_conv_w": nrm(ks[4], (DEPTH, LRU_CONV, LRU_WIDTH), LRU_CONV ** -0.5),
        "lru_conv_b": nrm(ks[5], (DEPTH, LRU_WIDTH), 0.02),
        "lru_w_a": nrm(ks[6], (DEPTH, LRU_HEADS, LRU_HEAD_DIM, LRU_HEAD_DIM), LRU_HEAD_DIM ** -0.5),
        "lru_b_a": nrm(ks[7], (DEPTH, LRU_HEADS, LRU_HEAD_DIM), 0.02),
        "lru_w_x": nrm(ks[9], (DEPTH, LRU_HEADS, LRU_HEAD_DIM, LRU_HEAD_DIM), LRU_HEAD_DIM ** -0.5),
        "lru_b_x": nrm(ks[10], (DEPTH, LRU_HEADS, LRU_HEAD_DIM), 0.02),
        "lru_lambda": lru_lambda,
        "mem_norm_gain": gain(ks[11], (DEPTH, D_MODEL)),
        "w_mem_kv": nrm(ks[12], (DEPTH, D_MODEL, 2 * XATTN_WIDTH), D_MODEL ** -0.5),
        "w_branch": nrm(ks[13], (DEPTH, N_BRANCH, LRU_WIDTH, D_MODEL), LRU_WIDTH ** -0.5),
        "w_out": nrm(ks[14], (DEPTH, D_MODEL, D_MODEL), D_MODEL ** -0.5),
        "ffn_norm_gain": gain(ks[15], (DEPTH, D_MODEL)),
        "w_ffn_gate": nrm(ks[16], (DEPTH, D_MODEL, D_FF), D_MODEL ** -0.5),
        "w_ffn_up": nrm(ks[17], (DEPTH, D_MODEL, D_FF), D_MODEL ** -0.5),
        "ffn_conv_w": nrm(ks[18], (DEPTH, FFN_CONV, D_FF), FFN_CONV ** -0.5),
        "ffn_conv_b": nrm(ks[19], (DEPTH, D_FF), 0.02),
        "w_ffn_down": nrm(ks[20], (DEPTH, D_FF, D_MODEL), D_FF ** -0.5),
        "final_norm_gain": gain(ks[21], (D_MODEL,)),
    }

def first_block(x, mem, mix_norm_gain, w_in, lru_conv_w, lru_conv_b, lru_w_a, lru_b_a, lru_w_x, lru_b_x,
              lru_lambda, mem_norm_gain, w_mem_kv, w_branch, w_out, ffn_norm_gain, w_ffn_gate, w_ffn_up,
              ffn_conv_w, ffn_conv_b, w_ffn_down, final_norm_gain):
    bsz, s, d = x.shape
    m = mem.shape[1]
    splits = list(np.cumsum([LRU_WIDTH, LRU_WIDTH, MOBA_WIDTH, MOBA_WIDTH, MOBA_WIDTH, XATTN_WIDTH]))
    for l in range(DEPTH):
        h = rms_norm(x, mix_norm_gain[l])
        proj = h @ w_in[l]
        xa, ga, qm, km, vm, qx, g_logits = jnp.split(proj, splits, axis=-1)
        xa = causal_dwconv(xa, lru_conv_w[l], lru_conv_b[l])
        y_a = rg_lru(xa, lru_w_a[l], lru_b_a[l], lru_w_x[l], lru_b_x[l], lru_lambda[l]) * jax.nn.gelu(ga)
        to_heads = lambda t_: t_.reshape(bsz, s, MOBA_HEADS, MOBA_HEAD_DIM).transpose(0, 2, 1, 3)
        y_b = moba_attention(to_heads(qm), to_heads(km), to_heads(vm))
        y_b = y_b.transpose(0, 2, 1, 3).reshape(bsz, s, MOBA_WIDTH)
        mkv = rms_norm(mem, mem_norm_gain[l]) @ w_mem_kv[l]
        mk, mv = jnp.split(mkv.reshape(bsz, m, 2, XATTN_HEADS, XATTN_HEAD_DIM), 2, axis=2)
        y_c = memory_cross_attention(qx.reshape(bsz, s, XATTN_HEADS, XATTN_HEAD_DIM), mk[:, :, 0], mv[:, :, 0])
        ys = jnp.stack([y_a, y_b, y_c], axis=2)
        branch_out = jnp.einsum("bsnw,nwd->bsnd", ys, w_branch[l])
        gates = jax.nn.sigmoid(g_logits.astype(jnp.float32)).astype(x.dtype).reshape(bsz, s, N_BRANCH, d)
        merged = jnp.sum(gates * branch_out, axis=2)
        x = x + merged @ w_out[l]
        h = rms_norm(x, ffn_norm_gain[l])
        g = causal_dwconv(h @ w_ffn_gate[l], ffn_conv_w[l], ffn_conv_b[l])
        x = x + (jax.nn.gelu(g) * (h @ w_ffn_up[l])) @ w_ffn_down[l]
    return rms_norm(x, final_norm_gain)


RET_HEADS = 8
RET_DK = 64
RET_DV = 128
RET_CHUNK = 128
DIFF_HEADS = 8
DIFF_DK = 64
DIFF_DV = 2 * DIFF_DK
Q_BLOCK = 128
EPS = 1e-6

RET_QK = RET_HEADS * RET_DK
RET_V = RET_HEADS * RET_DV
DIFF_QK = DIFF_HEADS * 2 * DIFF_DK
DIFF_V = DIFF_HEADS * DIFF_DV
IN_SPLITS = (RET_QK, RET_QK, RET_V, RET_V, DIFF_QK, DIFF_QK, DIFF_V, DIFF_V, D_MODEL, D_MODEL)
N_IN = 2 * RET_QK + 2 * RET_V + 2 * DIFF_QK + 2 * DIFF_V + 2 * D_MODEL


def rms_norm_2(x, g):
    xf = x.astype(jnp.float32)
    xf = xf * lax.rsqrt(jnp.mean(xf * xf, axis=-1, keepdims=True) + EPS)
    return xf * g.astype(jnp.float32)

def retention(q, k, v):
    B, S, H, dk = q.shape
    dv = v.shape[-1]
    C = RET_CHUNK
    n = S // C
    log_gamma = jnp.log1p(-jnp.exp2(-5.0 - jnp.arange(H, dtype=jnp.float32)))
    pos = jnp.arange(C, dtype=jnp.float32)
    rel = pos[:, None] - pos[None, :]
    inner_decay = jnp.where(rel >= 0, jnp.exp(jnp.maximum(rel, 0.0)[None] * log_gamma[:, None, None]), 0.0)
    q_decay = jnp.exp((pos + 1.0)[None] * log_gamma[:, None])
    k_decay = jnp.exp((C - 1.0 - pos)[None] * log_gamma[:, None])
    chunk_decay = jnp.exp(C * log_gamma)

    def to_chunks(t):
        return t.astype(jnp.float32).reshape(B, n, C, H, t.shape[-1]).transpose(1, 0, 3, 2, 4)

    qc = to_chunks(q)
    kc = to_chunks(k) * (dk ** -0.5)
    vc = to_chunks(v)

    def step(state, inp):
        qi, ki, vi = inp
        scores = jnp.einsum('bhnd,bhmd->bhnm', qi, ki) * inner_decay
        out = (jnp.einsum('bhnm,bhme->bhne', scores, vi)
               + jnp.einsum('bhnd,bhde->bhne', qi, state) * q_decay[..., None])
        state = (state * chunk_decay[:, None, None]
                 + jnp.einsum('bhmd,bhme->bhde', ki * k_decay[..., None], vi))
        return state, out

    state0 = jnp.zeros((B, H, dk, dv), jnp.float32)
    _, out = lax.scan(step, state0, (qc, kc, vc))
    return out.transpose(1, 0, 3, 2, 4).reshape(B, S, H, dv)

def diff_attention(q, k, v, lam):
    B, S, H, _, dk = q.shape
    slopes = jnp.exp2(-8.0 * jnp.arange(1, H + 1, dtype=jnp.float32) / H)
    q = q.astype(jnp.float32) * (dk ** -0.5)
    k = k.astype(jnp.float32)
    v = v.astype(jnp.float32)
    outs = []
    for i in range(S // Q_BLOCK):
        start, end = i * Q_BLOCK, (i + 1) * Q_BLOCK
        qb = q[:, start:end]
        kb = k[:, :end]
        vb = v[:, :end]
        dist = (jnp.arange(start, end)[:, None] - jnp.arange(end)[None, :]).astype(jnp.float32)
        s = jnp.einsum('bqhjd,bkhjd->bhjqk', qb, kb) - slopes[None, :, None, None, None] * dist
        s = jnp.where(dist >= 0, s, -jnp.inf)
        p = jax.nn.softmax(s, axis=-1)
        a = p[:, :, 0] - lam * p[:, :, 1]
        outs.append(jnp.einsum('bhqk,bkhe->bqhe', a, vb))
    return jnp.concatenate(outs, axis=1)

def second_inputs(seed: int = 0) -> dict:
    key = jax.random.key(seed)
    ks = jax.random.split(key, 15)
    f32 = jnp.float32
    n = lambda k, s: jax.random.normal(k, s, f32)
    return {
        "x": n(ks[0], (BATCH, SEQ, D_MODEL)),
        "norm_g": 1.0 + 0.02 * n(ks[1], (DEPTH, D_MODEL)),
        "w_in": n(ks[2], (DEPTH, D_MODEL, N_IN)) * D_MODEL ** -0.5,
        "ret_norm_g": 1.0 + 0.02 * n(ks[3], (DEPTH, RET_V)),
        "ret_w_o": n(ks[4], (DEPTH, RET_V, D_MODEL)) * RET_V ** -0.5,
        "diff_q_norm_g": 1.0 + 0.02 * n(ks[5], (DEPTH, DIFF_DK)),
        "diff_k_norm_g": 1.0 + 0.02 * n(ks[6], (DEPTH, DIFF_DK)),
        "diff_lq1": 0.1 * n(ks[7], (DEPTH, DIFF_DK)),
        "diff_lk1": 0.1 * n(ks[8], (DEPTH, DIFF_DK)),
        "diff_lq2": 0.1 * n(ks[9], (DEPTH, DIFF_DK)),
        "diff_lk2": 0.1 * n(ks[10], (DEPTH, DIFF_DK)),
        "diff_sub_norm_g": 1.0 + 0.02 * n(ks[11], (DEPTH, DIFF_V)),
        "diff_w_o": n(ks[12], (DEPTH, DIFF_V, D_MODEL)) * DIFF_V ** -0.5,
        "w_out": n(ks[13], (DEPTH, D_MODEL, D_MODEL)) * D_MODEL ** -0.5,
    }

def second_block(x, norm_g, w_in, ret_norm_g, ret_w_o, diff_q_norm_g, diff_k_norm_g,
              diff_lq1, diff_lk1, diff_lq2, diff_lk2, diff_sub_norm_g, diff_w_o, w_out):
    B, S, _ = x.shape
    split_idx = [int(v) for v in np.cumsum(IN_SPLITS)[:-1]]
    for l in range(DEPTH):
        h = rms_norm_2(x, norm_g[l]).astype(x.dtype)
        z = jnp.einsum('bsd,dn->bsn', h, w_in[l])
        (q_r, k_r, v_r, gate_r, q_d, k_d, v_d, gate_d,
         mg_r, mg_d) = jnp.split(z, split_idx, axis=-1)

        o_r = retention(q_r.reshape(B, S, RET_HEADS, RET_DK),
                        k_r.reshape(B, S, RET_HEADS, RET_DK),
                        v_r.reshape(B, S, RET_HEADS, RET_DV))
        o_r = rms_norm_2(o_r, ret_norm_g[l].reshape(RET_HEADS, RET_DV)).reshape(B, S, RET_V)
        o_r = (o_r * jax.nn.silu(gate_r.astype(jnp.float32))).astype(x.dtype)
        y_r = jnp.einsum('bse,ed->bsd', o_r, ret_w_o[l])

        lam_init = 0.8 - 0.6 * math.exp(-0.3 * l)
        lam = (jnp.exp(jnp.sum(diff_lq1[l].astype(jnp.float32) * diff_lk1[l].astype(jnp.float32)))
               - jnp.exp(jnp.sum(diff_lq2[l].astype(jnp.float32) * diff_lk2[l].astype(jnp.float32)))
               + lam_init)
        qd = rms_norm_2(q_d.reshape(B, S, DIFF_HEADS, 2, DIFF_DK), diff_q_norm_g[l])
        kd = rms_norm_2(k_d.reshape(B, S, DIFF_HEADS, 2, DIFF_DK), diff_k_norm_g[l])
        o_d = diff_attention(qd, kd, v_d.reshape(B, S, DIFF_HEADS, DIFF_DV), lam)
        o_d = rms_norm_2(o_d, diff_sub_norm_g[l].reshape(DIFF_HEADS, DIFF_DV)) * (1.0 - lam_init)
        o_d = (o_d.reshape(B, S, DIFF_V) * jax.nn.silu(gate_d.astype(jnp.float32))).astype(x.dtype)
        y_d = jnp.einsum('bse,ed->bsd', o_d, diff_w_o[l])

        m = jax.nn.sigmoid(mg_r) * y_r + jax.nn.sigmoid(mg_d) * y_d
        x = (x + jnp.einsum('bsd,de->bse', m, w_out[l])).astype(x.dtype)
    return x


def setup_inputs(seed=0):
    out = dict(first_inputs(seed))
    for name, value in second_inputs(seed + 1).items():
        if name != "x":
            out[name + "_2"] = value
    return out


def reference(
    x, mem, mix_norm_gain, w_in, lru_conv_w, lru_conv_b, lru_w_a, lru_b_a, lru_w_x, lru_b_x,
    lru_lambda, mem_norm_gain, w_mem_kv, w_branch, w_out, ffn_norm_gain, w_ffn_gate, w_ffn_up,
    ffn_conv_w, ffn_conv_b, w_ffn_down, final_norm_gain, norm_g_2, w_in_2, ret_norm_g_2,
    ret_w_o_2, diff_q_norm_g_2, diff_k_norm_g_2, diff_lq1_2, diff_lk1_2, diff_lq2_2, diff_lk2_2,
    diff_sub_norm_g_2, diff_w_o_2, w_out_2,
):
    x = first_block(
        x, mem, mix_norm_gain, w_in, lru_conv_w, lru_conv_b, lru_w_a, lru_b_a, lru_w_x, lru_b_x,
        lru_lambda, mem_norm_gain, w_mem_kv, w_branch, w_out, ffn_norm_gain, w_ffn_gate,
        w_ffn_up, ffn_conv_w, ffn_conv_b, w_ffn_down, final_norm_gain,
    )
    return second_block(
        x, norm_g_2, w_in_2, ret_norm_g_2, ret_w_o_2, diff_q_norm_g_2, diff_k_norm_g_2,
        diff_lq1_2, diff_lk1_2, diff_lq2_2, diff_lk2_2, diff_sub_norm_g_2, diff_w_o_2, w_out_2,
    )


_drawn_inputs = setup_inputs


def setup_inputs(seed=0):
    import zlib

    import numpy as np

    out = dict(_drawn_inputs(seed))
    spreads = {}
    factors = {'mix_norm_gain': 4.939,
     'lru_b_a': 8.0,
     'lru_b_x': 8.0,
     'mem_norm_gain': 8.0,
     'ffn_norm_gain': 3.144,
     'ffn_conv_b': 4.576,
     'norm_g_2': 3.197,
     'ret_norm_g_2': 8.0,
     'diff_q_norm_g_2': 8.0,
     'diff_k_norm_g_2': 8.0,
     'diff_lq1_2': 5.902,
     'diff_lk1_2': 4.622,
     'diff_lq2_2': 4.205,
     'diff_lk2_2': 8.0,
     'diff_sub_norm_g_2': 8.0}
    for name, (base, spread) in spreads.items():
        noise = np.random.default_rng([zlib.crc32(name.encode()), seed]).standard_normal(out[name].shape)
        drawn = base * np.exp(spread * noise) if base else spread * noise
        out[name] = __import__('jax').numpy.asarray(drawn.astype(out[name].dtype))
    for name, factor in factors.items():
        out[name] = (out[name] * factor).astype(out[name].dtype)
    return out
```

```python
from contextlib import ExitStack

import numpy as np
import concourse.bass as bass
from concourse import mybir

P = 128
D = 1024
KT = D // P
S = 512
NT = S // P
MEM = 256
STRIP = 2048
FF = 3072
FFT = FF // P
EPS = 1e-6
MASKED = -1e30
FAR = 1e6
LAM_INIT = 0.2

PHASES = [("xa", 2), ("ga", 2), ("memk", 2), ("memv", 2), ("xq", 2), ("mq", 2), ("mk", 2), ("mv", 2)]
for _n in range(3):
    PHASES += [(f"gate{_n}", 4), (f"branch{_n}", 2)]
PHASES += [("wo", 4)]
for _f in range(2):
    PHASES += [(f"ffn{_f}", 12), (f"down{_f}", 6)]
for _g in range(2):
    PHASES += [(f"rqk{_g}", 2), (f"rv{_g}", 2), (f"rg{_g}", 2)]
PHASES += [("rmg", 4), ("rwo", 4)]
for _g in range(2):
    PHASES += [(f"dq{_g}", 2), (f"dk{_g}", 2), (f"dv{_g}", 2), (f"dg{_g}", 2)]
PHASES += [("dmg", 4), ("dwo", 4), ("wo2", 4)]

STRIP_AT, TILE_AT, OPEN_AT = {}, {}, {}
_s = _t = _u = 0
for _name, _k in PHASES:
    STRIP_AT[_name], TILE_AT[_name], OPEN_AT[_name] = _s, _t, _u
    _s += _k
    _t += 8 if _name.startswith(("down", "branch")) else 4 if _name == "memv" else 2 * _k
    if _name.startswith("down"):
        _u += 4
    elif _name in ("mv", "memv", "wo", "wo2") or _name.startswith(("rv", "dv")):
        _u += _k // 2
STRIPS = _s

COLS = {}
_c = 0
for _name, _k in [("mix_g", 8), ("mem_g", 8), ("ffn_g", 8), ("norm2_g", 8), ("lconv_w", 16), ("lconv_b", 4),
                  ("b_a", 4), ("b_x", 4), ("lam", 4), ("fconv_w", 72), ("fconv_b", 24), ("ret_g", 8),
                  ("dq_g", 1), ("dk_g", 1), ("sub_g", 8)]:
    COLS[_name] = _c
    _c += _k
NPAR = _c


def hybrid_block_kernel(nc, x, mem, par, lru_w, lqk_in, final_g, wstream, out, xb_dram, mret_dram):
    fp32, fp32r = mybir.dt.float32, mybir.dt.float32r
    ALU, ACT, AX = mybir.AluOpType, mybir.ActivationFunctionType, mybir.AxisListType
    ds = bass.ds

    ctx = ExitStack()
    with ctx:
        def sb(name, shape, dt=fp32):
            return ctx.enter_context(nc.sbuf_tensor(name, shape, dt))

        def sem(name):
            return ctx.enter_context(nc.semaphore(name))

        w_raw = sb("w_raw", [P, 2, STRIP])
        w_hi = sb("w_hi", [P, 2, STRIP], fp32r)
        w_lo = sb("w_lo", [P, 2, STRIP], fp32r)
        h_hi = sb("h_hi", [P, KT, S], fp32r)
        h_lo = sb("h_lo", [P, KT, S], fp32r)
        y_hi = sb("y_hi", [P, 12, S], fp32r)
        y_lo = sb("y_lo", [P, 12, S], fp32r)
        spare = sb("spare", [P, NT * D])
        params = sb("params", [P, NPAR])
        lqk = sb("lqk", [P, 4, 64])
        ident = sb("ident", [P, P])
        half_ones = sb("half_ones", [P, P])
        neg_dist = sb("neg_dist", [P, S])
        fwd_dist = sb("fwd_dist", [P, S])
        stats = sb("stats", [P, 192])
        arena = sb("arena", [P, 12480])
        banks = [ctx.enter_context(nc.psum_tensor(f"bank{i}", [P, 512], fp32)) for i in range(8)]
        T_BANKS, O_BANKS = (banks[6], banks[2]), (banks[7], banks[3])

        def view(where, at, *shape):
            v = where[:, at:at + int(np.prod(shape))]
            return v.rearrange("p (a b) -> p a b", b=shape[1]) if len(shape) == 2 else v

        def par_col(name, i=0):
            return params[:, COLS[name] + i:COLS[name] + i + 1]

        x_tok = view(spare, 0, NT, D)
        m_ret = view(spare, 0, KT, S)
        xn = view(arena, 0, NT, D)
        squares = view(arena, 4096, NT, D)
        gain_row = view(arena, 8192, D)
        mem_tok = view(arena, 9216, 2, D)
        mem_hi, mem_lo = (v[:, 8:12, :].rearrange("p a (b s) -> p (a b) s", b=2) for v in (y_hi, y_lo))
        xa_pad = view(arena, 0, 4, S + 3)
        lru_t = view(arena, 0, 4, S)
        xc = view(arena, 2080, 4, S)
        lru_r = view(arena, 4128, 4, S)
        lru_i = view(arena, 6176, 4, S)
        ga_gelu = view(arena, 8224, 4, S)
        lru_tmp = view(arena, 10272, 2, S)
        wa_bd = view(arena, 11296, 4, P)
        wx_bd = view(arena, 11808, 4, P)
        mkT = view(spare, 0, 4, MEM)
        mv_tok = view(spare, 1024, 2, S)
        xqT = view(spare, 2048, 4, S)
        qT = view(arena, 0, 4, S)
        kT = view(arena, 2048, 4, S)
        v_tok = view(arena, 4096, 4, S)
        gate = view(arena, 6144, 4, S)
        o_tok = view(arena, 8192, 4, S)
        bias = view(arena, 10240, 2, S)
        pT = view(arena, 11264, 2, S)
        o_squares = view(arena, 10240, 4, S)
        z = view(arena, 6144, 2, S)
        prob = view(arena, 7168, 2, S)
        dz = view(spare, 0, 2, S)
        dprob = view(spare, 1024, 4, S)
        dmix = view(spare, 3072, 2, S)
        dsq = view(spare, 0, 8, S)
        st = view(spare, 0, 2, 1280)
        ST_AT = [0, 512, 896, 1152]
        gT = view(arena, 0, KT, S)
        merged = view(arena, 4096, KT, S)
        mtmp = view(arena, 8192, 4, S)
        gpad = view(arena, 0, 2, S + 2)
        cv = view(arena, 1088, 2, S)
        gl = view(arena, 2112, 2, S)
        pr = view(arena, 3136, 2, S)
        xb = view(arena, 0, NT, D)
        res = view(arena, 4096, NT, D)

        ssq = stats[:, 0:4]
        rstd = stats[:, 4:8]
        sp8 = stats[:, 8:12]
        nsp8 = stats[:, 12:16]
        spt = stats[:, 16:36]
        lam_col = stats[:, 36:37]
        lam_t = stats[:, 37:41]
        nmax = stats[:, 44:48]
        psum_p = stats[:, 48:56]
        rsum = stats[:, 56:64]
        rsl = stats[:, 64:68]
        ossq = stats[:, 72:88]
        orstd = stats[:, 88:104]

        raw_in = [sem("raw_in0"), sem("raw_in1")]
        w_hi_ready = sem("w_hi_ready")
        w_lo_ready = sem("w_lo_ready")
        open_used = sem("open_used")
        acc_done = sem("acc_done")
        acc_out = [sem(f"acc_out{i}") for i in range(4)]
        small_in = sem("small_in")
        lruw_in = sem("lruw_in")
        x_in = [sem("x_in0"), sem("x_in1"), sem("mem_in"), sem("row_in"), sem("xb_in"), sem("mret_in")]
        x_ready = sem("x_ready")
        const_ready = sem("const_ready")
        lruw_ready = sem("lruw_ready")
        ssq_ready, var_ready, sd_ready = sem("ssq_ready"), sem("var_ready"), sem("sd_ready")
        xn_ready, hT_done, hhi_ready, hlo_ready = sem("xn_ready"), sem("hT_done"), sem("hhi_ready"), sem("hlo_ready")
        sp_e, sp_ready = sem("sp_e"), sem("sp_ready")
        lam_s, lam_e, lam_ready = sem("lam_s"), sem("lam_e"), sem("lam_ready")
        xc_ready, lru_mm, lru_ri, lru_ta, lru_m2, lru_mult, ya_ready = (
            sem(n) for n in ("xc_ready", "lru_mm", "lru_ri", "lru_ta", "lru_m2", "lru_mult", "ya_ready"))
        sc_done, z_ready, p_ready, pT_done, pT_out, o_done, o_out = (
            sem(n) for n in ("sc_done", "z_ready", "p_ready", "pT_done", "pT_out", "o_done", "o_out"))
        bias_ready, a_ready = sem("bias_ready"), sem("a_ready")
        osq_ready, ovar_ready, osd_ready, on_ready, oT_done, y_ready, yhi_ready, ylo_ready = (
            sem(n) for n in ("osq_ready", "ovar_ready", "osd_ready", "on_ready", "oT_done", "y_ready",
                             "yhi_ready", "ylo_ready"))
        gate_ready, m_ready, mhi_ready, mlo_ready = (
            sem(n) for n in ("gate_ready", "m_ready", "mhi_ready", "mlo_ready"))
        conv_ready, gelu_ready, ahi_ready, alo_ready = (
            sem(n) for n in ("conv_ready", "gelu_ready", "ahi_ready", "alo_ready"))
        x1_ready, xb_ready, xb_out, mret_ready, mret_out = (
            sem(n) for n in ("x1_ready", "xb_ready", "xb_out", "mret_ready", "mret_out"))
        dsq_ready, dss_done, dsd_ready, dn_ready = (
            sem(n) for n in ("dsq_ready", "dss_done", "dsd_ready", "dn_ready"))
        st_ready, so_done, so_out, dec_ready = (sem(n) for n in ("st_ready", "so_done", "so_out", "dec_ready"))
        res_ready, res_out = sem("res_ready"), sem("res_out")

        NORMS = ["mem", "mix", "ffn", "final", "norm2"]
        SSQ_AT = dict(zip(NORMS, [0, 2, 6, 10, 14]))
        HT_AT = dict(zip(NORMS, [0, 8, 16, None, 24]))
        U_X, U_M, U_D = 0, 16, 48
        SC_AT = {"x": 0, "m": 16, ("r", 0): 48, ("r", 1): 64, ("d", 0): 80, ("d", 1): 112}
        Z_AT = {"x": 0, "m": 16, ("d", 0): 48, ("d", 1): 80}
        O_NORM = {("r", 0): 0, ("r", 1): 1, ("d", 0): 2, ("d", 1): 3}
        OT_AT = {"x": 0, "m": 4, ("r", 0): 8, ("r", 1): 12, ("d", 0): 16, ("d", 1): 20}
        M_AT = {"one": 0, "two": 8}

        block = ctx.enter_context(nc.Block())

        @block.sync
        def _(sp):
            xv = x.rearrange("(j p) d -> p j d", p=P)
            sp.dma_start(mem_tok, mem.rearrange("(j p) d -> p j d", p=P)).then_inc(x_in[2], 16)
            sp.dma_start(params[:], par).then_inc(small_in, 16)
            sp.dma_start(lqk[:], lqk_in).then_inc(small_in, 16)
            sp.dma_start(x_tok, xv).then_inc(x_in[0], 16)
            for slot in range(2):
                sp.dma_start(w_raw[:, slot, :], wstream[slot * P:(slot + 1) * P, :]).then_inc(raw_in[slot], 16)

            def strips(lo, hi):
                with sp.Fori(lo, hi) as i:
                    for slot in range(2):
                        sp.wait_ge(w_lo_ready, i * 2 + (slot - 1))
                        sp.dma_start(w_raw[:, slot, :], wstream[ds(i * (2 * P) + slot * P, P), :]).then_inc(raw_in[slot], 16)

            def first(name):
                return STRIP_AT[name] // 2 + 1

            strips(1, first("gate0"))
            sp.wait_ge(o_out, U_D)
            sp.dma_start(x_tok, xv).then_inc(x_in[1], 16)
            strips(first("gate0"), first("down1"))
            sp.dma_start(gain_row, final_g).then_inc(x_in[3], 16)
            strips(first("down1"), first("rqk0"))
            sp.wait_ge(xb_ready, NT)
            sp.dma_start(xb_dram.rearrange("(j p) d -> p j d", p=P), x_tok).then_inc(xb_out, 16)
            strips(first("rqk0"), first("dq0"))
            sp.wait_ge(mret_ready, KT)
            sp.dma_start(mret_dram.rearrange("p (c s) -> p c s", s=S), m_ret).then_inc(mret_out, 16)
            sp.wait_ge(mret_out, 16)
            strips(first("dq0"), first("dmg"))
            sp.wait_ge(ylo_ready, OT_AT["d", 1] + 4)
            sp.dma_start(m_ret, mret_dram.rearrange("p (c s) -> p c s", s=S)).then_inc(x_in[5], 16)
            strips(first("dmg"), first("wo2"))
            sp.wait_ge(xb_out, 16)
            sp.wait_ge(mlo_ready, M_AT["two"] + KT)
            sp.dma_start(xb, xb_dram.rearrange("(j p) d -> p j d", p=P)).then_inc(x_in[4], 16)
            strips(first("wo2"), STRIPS // 2)
            for half in range(2):
                sp.wait_ge(res_ready, NT * (half + 1))
                sp.dma_start(out.rearrange("(j p) d -> p j d", p=P)[:, :, half * S:half * S + S],
                             res[:, :, half * S:half * S + S]).then_inc(res_out, 16)
            sp.wait_ge(res_out, 32)

        @block.gpsimd
        def _(pool):
            nc.gpsimd.memset(ident[:], 0.0)
            nc.gpsimd.memset(half_ones[:], 1.0)
            nc.gpsimd.memset(wa_bd, 0.0)
            nc.gpsimd.memset(wx_bd, 0.0)
            nc.gpsimd.iota(neg_dist[:], pattern=[[1, S]], base=-3 * P, channel_multiplier=-1,
                           allow_small_or_imprecise_dtypes=True)
            nc.gpsimd.iota(fwd_dist[:], pattern=[[1, S]], base=0, channel_multiplier=-1,
                           allow_small_or_imprecise_dtypes=True)
            pool.drain()
            nc.gpsimd.affine_select(out=ident[:], in_=ident[:], compare_op=ALU.not_equal, fill=1.0, base=0,
                                    pattern=[[-1, P]], channel_multiplier=1)
            nc.gpsimd.affine_select(out=half_ones[:, 0:64], in_=half_ones[:, 0:64], compare_op=ALU.is_ge, fill=0.0,
                                    base=63, pattern=[[0, 64]], channel_multiplier=-1)
            nc.gpsimd.affine_select(out=half_ones[:, 64:P], in_=half_ones[:, 64:P], compare_op=ALU.is_ge, fill=0.0,
                                    base=-64, pattern=[[0, 64]], channel_multiplier=1)
            nc.gpsimd.affine_select(out=neg_dist[:], in_=neg_dist[:], compare_op=ALU.is_ge, fill=MASKED,
                                    base=3 * P, pattern=[[-1, S]], channel_multiplier=1)
            nc.gpsimd.affine_select(out=fwd_dist[:], in_=fwd_dist[:], compare_op=ALU.is_ge, fill=FAR,
                                    base=0, pattern=[[1, S]], channel_multiplier=-1).then_inc(const_ready, 1)
            pool.wait_ge(const_ready, 1)
            for k, bd in enumerate((wa_bd, wx_bd)):
                for s in range(2):
                    pool.dma_start(bd[64 * s:64 * s + 64, :, 64 * s:64 * s + 64],
                                   lru_w[64 * s:64 * s + 64, k, :, :]).then_inc(lruw_in, 16)
            pool.wait_ge(ya_ready, 4)
            nc.gpsimd.memset(bias, 0.0).then_inc(bias_ready, 1)
            for h in range(8):
                pool.wait_ge(z_ready, U_M + max(0, 4 * (h - 1)))
                nc.gpsimd.tensor_scalar(bias[:, h % 2, :], neg_dist[:], 2.0 ** -(h + 1), None,
                                        ALU.mult).then_inc(bias_ready, 1)
            for h in range(8):
                if h % 4 < 2:
                    pool.wait_ge(ovar_ready, 2 + h // 4)
                if h % 4 >= 2:
                    pool.wait_ge(z_ready, U_D + 8 * (h - 1))
                nc.gpsimd.tensor_scalar(bias[:, h % 2, :], neg_dist[:], 2.0 ** -(h + 1), None,
                                        ALU.mult).then_inc(bias_ready, 1)

        @block.tensor
        def _(pe):
            def free_bank(b, uses):
                if not isinstance(uses, int) or uses > 0:
                    pe.wait_ge(acc_out[b], uses)

            def three(dst, w, a, weights_still, first, last):
                for k, (i, j) in enumerate(((0, 0), (0, 1), (1, 0))):
                    l, r = (w[i], a[j]) if weights_still else (a[j], w[i])
                    done = nc.tensor.matmul(dst, l, r, start=first and k == 0, stop=last and k == 2)
                return done

            def pair_a(name, i=0, src=(h_hi, h_lo), n=S, tail=None):
                s0, t0 = STRIP_AT[name], TILE_AT[name]
                for slot in range(2):
                    pe.wait_ge(w_lo_ready, i * 2 + (s0 + slot + 1))
                    for c in range(2):
                        b = 2 * slot + c
                        free_bank(b, i + t0 // 4)
                        for kt in range(KT):
                            cols = slice(kt * 256 + c * P, kt * 256 + c * P + P)
                            done = three(banks[b][:, 0:n], (w_hi[:, slot, cols], w_lo[:, slot, cols]),
                                         (src[0][:, kt, :], src[1][:, kt, :]), True, kt == 0, kt == KT - 1)
                        done.then_inc(acc_done, 1)
                    if slot == 0 and tail:
                        tail()

            def group_b(name, i=0, src=(h_hi, h_lo), strips=2, s_off=0, t_off=0, b_off=0):
                s0, t0 = STRIP_AT[name] + s_off, TILE_AT[name] + t_off
                for k in range(strips):
                    slot = (s0 + k) % 2
                    pe.wait_ge(w_lo_ready, i * strips + (s0 + k + 1))
                    for j in range(NT):
                        if k == 0 and b_off == 0:
                            free_bank(j, i + t0 // 4)
                        for q in range(4):
                            kt, cols, tok = 4 * k + q, slice(q * 512, q * 512 + 512), slice(j * P, j * P + P)
                            done = three(banks[b_off + j][:], (w_hi[:, slot, cols], w_lo[:, slot, cols]),
                                         (src[0][:, kt, tok], src[1][:, kt, tok]), False, kt == 0, kt == 4 * strips - 1)
                        if k == strips - 1:
                            done.then_inc(acc_done, 1)
                    if k < strips - 1:
                        done.then_inc(open_used, 1)

            def pair_c(name, y_at):
                s0, t0 = STRIP_AT[name], TILE_AT[name]
                for slot in range(2):
                    pe.wait_ge(w_lo_ready, s0 + slot + 1)
                    for c in range(4):
                        free_bank(c, t0 // 4 + slot)
                        for q in range(4):
                            cols = slice(q * 512 + c * P, q * 512 + c * P + P)
                            done = three(banks[c][:], (w_hi[:, slot, cols], w_lo[:, slot, cols]),
                                         (y_hi[:, y_at + q, :], y_lo[:, y_at + q, :]), True, q == 0, q == 3)
                        done.then_inc(acc_done, 1)

            def loop_a(name, pairs, **kw):
                with pe.Fori(0, pairs) as i:
                    pair_a(name, i, **kw)

            def norm_t(name, tiles):
                pe.wait_ge(xn_ready, SSQ_AT[name] + tiles - (4 if name == "norm2" else 0))
                for kt in range(KT):
                    if HT_AT[name] + kt >= 4:
                        pe.wait_ge(hlo_ready, HT_AT[name] + kt - 3)
                    for j in range(tiles):
                        done = nc.tensor.transpose(banks[4 + kt % 4][:, j * P:j * P + P],
                                                   xn[:, j, kt * P:kt * P + P], ident[:])
                    done.then_inc(hT_done, 1)
                pe.wait_ge(hlo_ready, HT_AT[name] + KT)

            def attend(units, o_cols, base_u, sub, z_at):
                def scores(k):
                    for m, (lhsT, rhs) in enumerate(units[k][0]):
                        v = k * sub + m
                        if v >= 2:
                            pe.wait_ge(*z_at(v - 1))
                        nc.tensor.matmul(banks[4 + v % 2][:, 0:units[k][2]], lhsT, rhs,
                                         start=True, stop=True).then_inc(sc_done, 1)

                def transposes(k):
                    u = base_u + k
                    pe.wait_ge(a_ready if sub == 2 else p_ready, u + 1 - (U_D if sub == 2 else 0))
                    if k >= 2:
                        pe.wait_ge(pT_out, u - 1)
                    src = dmix if sub == 2 else prob
                    for c in range(units[k][2] // P):
                        done = nc.tensor.transpose(T_BANKS[k % 2][:, c * P:c * P + P],
                                                   src[:, k % 2, c * P:c * P + P], ident[:])
                    done.then_inc(pT_done, 1)

                def outputs(k):
                    u = base_u + k
                    pe.wait_ge(pT_out, u + 1)
                    if k >= 2:
                        pe.wait_ge(o_out, u - 1)
                    vals = units[k][1]
                    for c, val in enumerate(vals):
                        done = nc.tensor.matmul(O_BANKS[k % 2][:, 0:o_cols],
                                                pT[:, k % 2, c * P:c * P + P], val,
                                                start=c == 0, stop=c == len(vals) - 1)
                    done.then_inc(o_done, 1)

                scores(0)
                for k in range(len(units)):
                    if k + 1 < len(units):
                        scores(k + 1)
                    transposes(k)
                    if k >= 1:
                        outputs(k - 1)
                outputs(len(units) - 1)

            def out_t(key, ready, count):
                pe.wait_ge(ready, count)
                for c in range(4):
                    for j in range(NT):
                        done = nc.tensor.transpose(banks[4 + c][:, j * P:j * P + P], o_tok[:, j, c * P:c * P + P], ident[:])
                    done.then_inc(oT_done, 1)
                pe.wait_ge(ylo_ready, OT_AT[key] + 4)

            pe.wait_ge(const_ready, 1)
            norm_t("mem", 2)
            norm_t("mix", 4)
            pair_a("xa")
            pair_a("ga")
            pe.wait_ge(lruw_in, 64)
            for c in range(4):
                pe.wait_ge(xc_ready, c + 1)
                for m, bd in enumerate((wa_bd, wx_bd)):
                    if c >= 2:
                        pe.wait_ge(lru_ri, 2 * (c - 2) + m + 1)
                    nc.tensor.matmul(banks[4 + 2 * (c % 2) + m][:], bd[:, c, :], xc[:, c, :],
                                     start=True, stop=True).then_inc(lru_mm, 1)
            pair_a("memk", src=(mem_hi, mem_lo), n=MEM)
            s0, t0 = STRIP_AT["memv"], TILE_AT["memv"]
            for k in range(2):
                pe.wait_ge(w_lo_ready, s0 + k + 1)
                for j in range(2):
                    for half in range(2):
                        b = 2 * j + half
                        if k == 0:
                            free_bank(b, t0 // 4)
                        for q in range(4):
                            cols = slice(q * 512 + half * 256, q * 512 + half * 256 + 256)
                            done = three(banks[b][:, 0:256], (w_hi[:, k, cols], w_lo[:, k, cols]),
                                         (mem_hi[:, 4 * k + q, j * P:j * P + P], mem_lo[:, 4 * k + q, j * P:j * P + P]),
                                         False, k == 0 and q == 0, k == 1 and q == 3)
                        if k == 1:
                            done.then_inc(acc_done, 1)
                if k == 0:
                    done.then_inc(open_used, 1)
            pair_a("xq")
            for b in range(4):
                pe.wait_ge(acc_out[b], TILE_AT["mq"] // 4)
            attend([([(xqT[:, h, t * P:t * P + P], mkT[:, h, :])], [mv_tok[:, c, h * P:h * P + P] for c in range(2)], MEM)
                    for h in range(4) for t in range(NT)], P, U_X, 1, lambda v: (z_ready, U_X + v))
            out_t("x", o_out, U_M)
            pair_a("mq")
            pair_a("mk")
            group_b("mv")
            for b in range(4):
                pe.wait_ge(acc_out[b], TILE_AT["gate0"] // 4)
            units = []
            for h in range(8):
                rows, tile = slice(64 * (h % 2), 64 * (h % 2) + 64), h // 2
                for t in range(NT):
                    units.append(([(qT[rows, tile, t * P:t * P + P], kT[rows, tile, 0:(t + 1) * P])],
                                  [v_tok[:, c, h * 64:h * 64 + 64] for c in range(t + 1)], (t + 1) * P))
            attend(units, 64, U_M, 1, lambda v: (z_ready, U_M + v))
            out_t("m", o_out, U_D)
            for n, y_at in enumerate((0, 4, 8)):
                loop_a(f"gate{n}", 2)
                pair_c(f"branch{n}", y_at)
            pe.wait_ge(mlo_ready, M_AT["one"] + KT)
            with pe.Fori(0, 2) as i:
                group_b("wo", i)
            norm_t("ffn", 4)
            for f in range(2):
                loop_a(f"ffn{f}", 6)
                pe.wait_ge(alo_ready, 12 * (f + 1))
                for half in range(2):
                    group_b(f"down{f}", src=(y_hi, y_lo), strips=3, s_off=3 * half, t_off=4 * half)
            norm_t("norm2", 4)
            for g in range(2):
                pair_a(f"rqk{g}")
                group_b(f"rv{g}")
                pair_a(f"rg{g}")
                for b in range(4):
                    pe.wait_ge(acc_out[b], TILE_AT[f"rg{g}"] // 4)

                def ret_scores(hh):
                    rows, tile = slice(64 * (hh % 2), 64 * (hh % 2) + 64), hh // 2
                    for c in range(NT):
                        r = (4 * g + hh) * 4 + c
                        if r % 16 >= 2:
                            pe.wait_ge(st_ready, r - 1)
                        nc.tensor.matmul(banks[4 + r % 2][:, 0:S - c * P], kT[rows, tile, c * P:c * P + P],
                                         qT[rows, tile, c * P:S], start=True, stop=True).then_inc(sc_done, 1)

                def ret_outputs(hh):
                    head = 4 * g + hh
                    pe.wait_ge(st_ready, 4 * head + 4)
                    if hh >= 2:
                        pe.wait_ge(so_out, head - 1)
                    for j in range(NT):
                        for c in range(j + 1):
                            at = ST_AT[c] + (j - c) * P
                            done = nc.tensor.matmul(banks[6 + head % 2][:, j * P:j * P + P], st[:, hh % 2, at:at + P],
                                                    v_tok[:, c, hh * P:hh * P + P], start=c == 0, stop=c == j)
                    done.then_inc(so_done, 1)

                ret_scores(0)
                for hh in range(1, 4):
                    ret_scores(hh)
                    ret_outputs(hh - 1)
                ret_outputs(3)
                out_t(("r", g), on_ready, O_NORM["r", g] + 1)
            loop_a("rmg", 2)
            with pe.Fori(0, 2) as i:
                pair_a("rwo", i, src=(y_hi, y_lo))
            for g in range(2):
                def head_sums(which, g=g):
                    name = f"d{'qk'[which]}{g}"
                    for c in range(4):
                        pe.wait_ge(acc_out[c], TILE_AT[name] // 4 + 1)
                        if which:
                            pe.wait_ge(dsd_ready, 8 * g + c + 1)
                        nc.tensor.matmul(banks[4 + c][:], half_ones[:], dsq[:, 4 * which + c, :],
                                         start=True, stop=True).then_inc(dss_done, 1)

                pair_a(f"dq{g}")
                pair_a(f"dk{g}", tail=lambda: head_sums(0))
                s1 = STRIP_AT[f"dv{g}"]
                group_b(f"dv{g}")
                head_sums(1)
                pair_a(f"dg{g}")
                pe.wait_ge(dn_ready, 8 * g + 8)
                for b in range(4):
                    pe.wait_ge(acc_out[b], TILE_AT[f"dg{g}"] // 4)
                units = []
                for hh in range(4):
                    for t in range(NT):
                        maps = [(qT[64 * m:64 * m + 64, hh, t * P:t * P + P], kT[64 * m:64 * m + 64, hh, 0:(t + 1) * P])
                                for m in range(2)]
                        units.append((maps, [v_tok[:, c, hh * P:hh * P + P] for c in range(t + 1)], (t + 1) * P))
                attend(units, P, U_D + 16 * g, 2, lambda v, g=g: (z_ready, U_D + 32 * g + v))
                out_t(("d", g), on_ready, O_NORM["d", g] + 1)
            loop_a("dmg", 2)
            with pe.Fori(0, 2) as i:
                pair_a("dwo", i, src=(y_hi, y_lo))
            pe.wait_ge(mlo_ready, M_AT["two"] + KT)
            for half in range(2):
                group_b("wo2", half, b_off=4 * half)

        @block.scalar
        def _(act):
            def split_hi(name, slot, i=0, ahead=2):
                n = STRIP_AT[name] + slot + ahead
                if isinstance(i, int) and n + 2 * i >= STRIPS:
                    return
                act.wait_ge(raw_in[n % 2], i * 16 + 16 * (n // 2 + 1))
                nc.scalar.activation(w_hi[:, n % 2, :], w_raw[:, n % 2, :], ACT.Copy).then_inc(w_hi_ready, 1)

            def tile_done(name, k, i=0):
                act.wait_ge(acc_done, i * 4 + (TILE_AT[name] + k + 1))

            def pair_a(name, post, i=0):
                for slot in range(2):
                    for c in range(2):
                        tile_done(name, 2 * slot + c, i)
                        post(2 * slot + c, banks[2 * slot + c]).then_inc(acc_out[2 * slot + c], 1)
                    split_hi(name, slot, i)

            def group_b(name, post=None, i=0):
                act.wait_ge(open_used, i + (OPEN_AT[name] + 1))
                split_hi(name, 0, i)
                for j in range(NT):
                    tile_done(name, j, i)
                    if post:
                        post(j, banks[j]).then_inc(acc_out[j], 1)
                split_hi(name, 1, i)

            def norm_stats(name, src, tiles):
                for j in range(tiles):
                    nc.scalar.activation(squares[:, j, :], src[:, j, :], ACT.Square,
                                         accum_out=ssq[:, j:j + 1]).then_inc(ssq_ready, 1)
                act.wait_ge(var_ready, NORMS.index(name) + 1)
                nc.scalar.activation(rstd[:, 0:tiles], ssq[:, 0:tiles], ACT.Sqrt).then_inc(sd_ready, 1)

            def norm_hi(name, gain, hi, n):
                for kt in range(KT):
                    act.wait_ge(hT_done, HT_AT[name] + kt + 1)
                    nc.scalar.activation(hi[:, kt, :], banks[4 + kt % 4][:, 0:n], ACT.Identity,
                                         scale=par_col(gain, kt)).then_inc(hhi_ready, 1)

            def copy_to(dst, scale=1.0):
                return lambda k, bank: nc.scalar.activation(dst(k), bank[:, 0:dst(k).shape[-1]], ACT.Copy, scale=scale)

            def attend(widths, base_u):
                def transposed(k):
                    u = base_u + k
                    act.wait_ge(pT_done, u + 1)
                    if k >= 2:
                        act.wait_ge(o_done, u - 1)
                    nc.scalar.activation(pT[:, k % 2, 0:widths[k]], T_BANKS[k % 2][:, 0:widths[k]], ACT.Copy).then_inc(pT_out, 1)

                for k, w in enumerate(widths):
                    u = base_u + k
                    act.wait_ge(z_ready, u + 1)
                    if k >= 2:
                        act.wait_ge(pT_done, u - 1)
                    nc.scalar.activation(prob[:, k % 2, 0:w], z[:, k % 2, 0:w], ACT.Exp, scale=-1.0,
                                         bias=nmax[:, k % 4:k % 4 + 1],
                                         accum_out=psum_p[:, k % 4:k % 4 + 1]).then_inc(p_ready, 1)
                    if k >= 1:
                        transposed(k - 1)
                transposed(len(widths) - 1)

            def diff_attend(g):
                base_u, z0 = U_D + 16 * g, Z_AT["d", g]

                def transposed(k):
                    u, w = base_u + k, (k % NT + 1) * P
                    act.wait_ge(pT_done, u + 1)
                    if k >= 2:
                        act.wait_ge(o_done, u - 1)
                    nc.scalar.activation(pT[:, k % 2, 0:w], T_BANKS[k % 2][:, 0:w], ACT.Copy).then_inc(pT_out, 1)

                def output(k):
                    act.wait_ge(o_done, base_u + k + 1)
                    nc.scalar.activation(o_tok[:, k % NT, k // NT * P:k // NT * P + P],
                                         O_BANKS[k % 2][:, 0:P], ACT.Copy).then_inc(o_out, 1)

                for k in range(18):
                    if k < 16:
                        w = (k % NT + 1) * P
                        if k >= 2:
                            act.wait_ge(a_ready, 16 * g + k - 1)
                        for m in range(2):
                            v = 2 * k + m
                            act.wait_ge(z_ready, z0 + v + 1)
                            nc.scalar.activation(dprob[:, v % 4, 0:w], dz[:, m, 0:w], ACT.Exp, scale=-1.0,
                                                 bias=nmax[:, v % 4:v % 4 + 1],
                                                 accum_out=psum_p[:, v % 4:v % 4 + 1]).then_inc(p_ready, 1)
                    if 1 <= k <= 16:
                        transposed(k - 1)
                    if k >= 2:
                        output(k - 2)

            def out_hi(key, y_at):
                for c in range(4):
                    act.wait_ge(oT_done, OT_AT[key] + c + 1)
                    nc.scalar.activation(y_hi[:, y_at + c, :], banks[4 + c][:], ACT.Copy).then_inc(yhi_ready, 1)

            def group_norm(key, y_at):
                n = O_NORM[key]
                nc.scalar.activation(o_squares, o_tok, ACT.Square).then_inc(osq_ready, 1)
                act.wait_ge(ovar_ready, n + 1)
                nc.scalar.activation(ossq, ossq, ACT.Sqrt).then_inc(osd_ready, 1)
                for c in range(4):
                    act.wait_ge(y_ready, 4 * n + c + 1)
                    nc.scalar.activation(y_hi[:, y_at + c, :], gate[:, c, :], ACT.Copy).then_inc(yhi_ready, 1)

            act.wait_ge(x_in[2], 16)
            norm_stats("mem", mem_tok, 2)
            act.wait_ge(small_in, 32)
            norm_hi("mem", "mem_g", mem_hi, MEM)
            act.wait_ge(x_in[0], 16)
            norm_stats("mix", x_tok, 4)
            split_hi("xa", 0, ahead=0)
            split_hi("xa", 1, ahead=0)
            norm_hi("mix", "mix_g", h_hi, S)
            act.wait_ge(sp_e, 1)
            nc.scalar.activation(spt[:, 4:8], spt[:, 0:4], ACT.Exp, scale=-1.0).then_inc(sp_e, 1)
            act.wait_ge(lam_s, 1)
            nc.scalar.activation(lam_t[:, 2:4], lam_t[:, 0:2], ACT.Exp).then_inc(lam_e, 1)
            pair_a("xa", copy_to(lambda k: xa_pad[:, k, 3:3 + S]))
            pair_a("ga", lambda k, bank: nc.scalar.activation(ga_gelu[:, k, :], bank[:], ACT.Gelu_apprx_tanh))

            def lru_gates():
                for c in range(4):
                    for m, (dst, b) in enumerate(((lru_r, "b_a"), (lru_i, "b_x"))):
                        act.wait_ge(lru_mm, 2 * c + m + 1)
                        nc.scalar.activation(dst[:, c, :], banks[4 + 2 * (c % 2) + m][:], ACT.Sigmoid,
                                             bias=par_col(b, c)).then_inc(lru_ri, 1)

            def lru_decays():
                act.wait_ge(sp_ready, 1)
                act.wait_ge(xc_ready, 4)
                act.wait_ge(lru_ri, 8)
                for c in range(4):
                    nc.scalar.activation(lru_t[:, c, :], lru_r[:, c, :], ACT.Tanh, scale=sp8[:, c:c + 1]).then_inc(lru_ta, 1)
                act.wait_ge(lru_ta, 4)
                for c in range(4):
                    nc.scalar.activation(lru_r[:, c, :], lru_r[:, c, :], ACT.Exp, scale=nsp8[:, c:c + 1]).then_inc(lru_ta, 1)

            lru_gates()
            for slot, work in enumerate((lru_decays, None)):
                for c in range(2):
                    tile_done("memk", 2 * slot + c)
                    copy_to(lambda k: mkT[:, k, :])(2 * slot + c, banks[2 * slot + c]).then_inc(acc_out[2 * slot + c], 1)
                split_hi("memk", slot)
                if work:
                    work()
            group_b("memv", lambda k, bank: nc.scalar.activation(
                mv_tok[:, k // 2, k % 2 * 256:k % 2 * 256 + 256], bank[:, 0:256], ACT.Copy))
            for c in range(4):
                act.wait_ge(lru_m2, c + 1)
                nc.scalar.activation(lru_t[:, c, :], lru_t[:, c, :], ACT.Sqrt).then_inc(lru_mult, 1)
            pair_a("xq", copy_to(lambda k: xqT[:, k, :], P ** -0.5))
            act.wait_ge(ya_ready, 4)
            attend([MEM] * 16, U_X)
            out_hi("x", 8)
            pair_a("mq", copy_to(lambda k: qT[:, k, :], 64 ** -0.5))
            pair_a("mk", copy_to(lambda k: kT[:, k, :]))
            group_b("mv", copy_to(lambda k: v_tok[:, k, :]))
            attend([(t + 1) * P for h in range(8) for t in range(NT)], U_M)
            out_hi("m", 4)
            for n in range(3):
                if n == 0:
                    act.wait_ge(o_out, U_D)
                    act.wait_ge(oT_done, OT_AT["m"] + 4)
                else:
                    act.wait_ge(m_ready, 8 * n)
                with act.Fori(0, 2) as i:
                    pair_a(f"gate{n}", lambda k, bank: nc.scalar.activation(
                        gT[:, ds(i * 4 + k, 1), :].rearrange("p a s -> p (a s)"), bank[:], ACT.Sigmoid), i)
                for slot in range(2):
                    tile_done(f"branch{n}", 4 * slot + 3)
                    split_hi(f"branch{n}", slot)
            for c in range(KT):
                act.wait_ge(m_ready, 16 + c + 1)
                nc.scalar.activation(h_hi[:, c, :], merged[:, c, :], ACT.Copy).then_inc(mhi_ready, 1)
            with act.Fori(0, 2) as i:
                group_b("wo", None, i)
            act.wait_ge(x1_ready, 8)
            norm_stats("ffn", x_tok, 4)
            norm_hi("ffn", "ffn_g", h_hi, S)
            for f in range(2):
                with act.Fori(0, 6) as i:
                    s0 = STRIP_AT[f"ffn{f}"]
                    for c in range(2):
                        tile_done(f"ffn{f}", c, i)
                        act.wait_ge(conv_ready, i * 2 + (12 * f + 1))
                        nc.scalar.activation(gpad[:, c, 2:2 + S], banks[c][:], ACT.Copy).then_inc(acc_out[c], 1)
                    split_hi(f"ffn{f}", 0, i)
                    for c in range(2):
                        act.wait_ge(conv_ready, i * 2 + (12 * f + c + 2))
                        nc.scalar.activation(gl[:, c, :], cv[:, c, :], ACT.Gelu_apprx_tanh).then_inc(gelu_ready, 1)
                    for c in range(2):
                        act.wait_ge(acc_out[2 + c], i + (TILE_AT[f"ffn{f}"] // 4 + 1))
                        nc.scalar.activation(y_hi[:, ds(i * 2 + c, 1), :].rearrange("p a s -> p (a s)"), pr[:, c, :],
                                             ACT.Copy).then_inc(ahi_ready, 1)
                    split_hi(f"ffn{f}", 1, i)
                name = f"down{f}"
                for half in range(2):
                    for k in range(3):
                        if k < 2:
                            act.wait_ge(open_used, OPEN_AT[name] + 2 * half + k + 1)
                        else:
                            tile_done(name, 4 * half + 3)
                        split_hi(name, 3 * half + k)
            act.wait_ge(x1_ready, 8 + 16)
            norm_stats("final", x_tok, 4)
            act.wait_ge(xb_ready, NT)
            norm_stats("norm2", x_tok, 4)
            norm_hi("norm2", "norm2_g", h_hi, S)
            for g in range(2):
                pair_a(f"rqk{g}", lambda k, bank: nc.scalar.activation(
                    (qT if k < 2 else kT)[:, k % 2, :], bank[:], ACT.Copy, scale=1.0 if k < 2 else 64 ** -0.5))
                group_b(f"rv{g}", copy_to(lambda k: v_tok[:, k, :]))
                pair_a(f"rg{g}", lambda k, bank: nc.scalar.activation(gate[:, k, :], bank[:], ACT.Silu))

                def decays(hh):
                    head = 4 * g + hh
                    if head >= 2:
                        act.wait_ge(st_ready, 4 * (head - 1))
                    nc.scalar.activation(bias[:, hh % 2, :], fwd_dist[:], ACT.Exp,
                                         scale=float(np.log1p(-2.0 ** (-5.0 - head)))).then_inc(dec_ready, 1)

                decays(0)
                decays(1)
                for hh in range(4):
                    head = 4 * g + hh
                    if hh >= 1 and hh + 1 < 4:
                        decays(hh + 1)
                    act.wait_ge(so_done, head + 1)
                    nc.scalar.activation(o_tok[:, :, hh * P:hh * P + P],
                                         banks[6 + head % 2].rearrange("p (j e) -> p j e", e=P), ACT.Copy).then_inc(so_out, 1)
                act.wait_ge(so_out, 4 * g + 4)
                group_norm(("r", g), 4 * g)
            with act.Fori(0, 2) as i:
                pair_a("rmg", lambda k, bank: nc.scalar.activation(
                    gT[:, ds(i * 4 + k, 1), :].rearrange("p a s -> p (a s)"), bank[:], ACT.Sigmoid), i)
            for i in range(2):
                for slot in range(2):
                    tile_done("rwo", 4 * i + 2 * slot + 1)
                    split_hi("rwo", slot, i)
            act.wait_ge(mret_out, 16)
            act.wait_ge(mret_ready, KT)
            for g in range(2):
                def norms(which):
                    for c in range(4):
                        act.wait_ge(dss_done, 8 * g + 4 * which + c + 1)
                        nc.scalar.activation(dsq[:, 4 * which + c, :], banks[4 + c][:], ACT.Sqrt,
                                             scale=1 / 64 if which else 1.0,
                                             bias=stats[:, 41 + which:42 + which]).then_inc(dsd_ready, 1)

                def square_too(k, bank, which):
                    nc.scalar.activation((qT, kT)[which][:, k, :], bank[:], ACT.Copy)
                    return nc.scalar.activation(dsq[:, 4 * which + k, :], bank[:], ACT.Square)

                pair_a(f"dq{g}", lambda k, bank: square_too(k, bank, 0))
                for slot in range(2):
                    for c in range(2):
                        k = 2 * slot + c
                        tile_done(f"dk{g}", k)
                        square_too(k, banks[k], 1).then_inc(acc_out[k], 1)
                    split_hi(f"dk{g}", slot)
                    if slot == 0:
                        norms(0)
                group_b(f"dv{g}", copy_to(lambda k: v_tok[:, k, :]))
                norms(1)
                pair_a(f"dg{g}", lambda k, bank: nc.scalar.activation(gate[:, k, :], bank[:], ACT.Silu))
                act.wait_ge(dn_ready, 8 * g + 8)
                diff_attend(g)
                act.wait_ge(o_out, U_D + 16 * g + 16)
                group_norm(("d", g), 4 * g)
            with act.Fori(0, 2) as i:
                pair_a("dmg", lambda k, bank: nc.scalar.activation(
                    gT[:, ds(i * 4 + k, 1), :].rearrange("p a s -> p (a s)"), bank[:], ACT.Sigmoid), i)
            for i in range(2):
                for slot in range(2):
                    for c in range(2):
                        k = 4 * i + 2 * slot + c
                        act.wait_ge(m_ready, 24 + k + 1)
                        nc.scalar.activation(h_hi[:, k, :], gT[:, k, :], ACT.Copy).then_inc(mhi_ready, 1)
                    split_hi("dwo", slot, i)
            for i in range(2):
                group_b("wo2", None, i)

        @block.vector
        def _(dve):
            then = dve.drain

            def split_lo(name, slot, i=0, ahead=2):
                n = STRIP_AT[name] + slot + ahead
                if isinstance(i, int) and n + 2 * i >= STRIPS:
                    return
                dve.wait_ge(w_hi_ready, i * 2 + (n + 1))
                nc.vector.tensor_tensor(w_lo[:, n % 2, :], w_raw[:, n % 2, :], w_hi[:, n % 2, :].bitcast(fp32),
                                        ALU.subtract).then_inc(w_lo_ready, 1)

            def both_lo(name, i=0):
                split_lo(name, 0, i)
                split_lo(name, 1, i)

            def norm_scale(name, tiles, apply):
                k = NORMS.index(name)
                dve.wait_ge(ssq_ready, SSQ_AT[name] + tiles)
                nc.vector.tensor_scalar(ssq[:, 0:tiles], ssq[:, 0:tiles], 1.0 / D, EPS, ALU.mult, ALU.add).then_inc(var_ready, 1)
                dve.wait_ge(sd_ready, k + 1)
                nc.vector.reciprocal(rstd[:, 0:tiles], rstd[:, 0:tiles])
                then()
                for j in range(tiles):
                    apply(j)

            def normed(src):
                return lambda j: nc.vector.tensor_scalar(xn[:, j, :], src[:, j, :], rstd[:, j:j + 1], None,
                                                         ALU.mult).then_inc(xn_ready, 1)

            def norm_lo(name, gain, hi, lo, n):
                for kt in range(KT):
                    dve.wait_ge(hhi_ready, HT_AT[name] + kt + 1)
                    nc.vector.scalar_tensor_tensor(lo[:, kt, :], banks[4 + kt % 4][:, 0:n], par_col(gain, kt),
                                                   hi[:, kt, :].bitcast(fp32), ALU.mult, ALU.subtract).then_inc(hlo_ready, 1)

            def with_bias(bank, bias_cols, dst, col):
                return nc.vector.tensor_tensor_reduce(out=dst, in0=bank, in1=bias_cols, scale=-1.0, scalar=3e38,
                                                      op0=ALU.add, op1=ALU.min, accum_out=nmax[:, col:col + 1])

            def attend(units, key, base_u):
                def output(k):
                    u, dst = base_u + k, units[k][3]
                    dve.wait_ge(o_done, u + 1)
                    nc.vector.reciprocal(rsum[:, k % 4:k % 4 + 1], psum_p[:, k % 4:k % 4 + 1])
                    then()
                    nc.vector.tensor_scalar(dst, O_BANKS[k % 2][:, 0:dst.shape[-1]],
                                            rsum[:, k % 4:k % 4 + 1], None, ALU.mult).then_inc(o_out, 1)

                for k, (w, cols, number, _) in enumerate(units):
                    dve.wait_ge(sc_done, SC_AT[key] + k + 1)
                    dve.wait_ge(bias_ready, number)
                    if k >= 2:
                        dve.wait_ge(p_ready, base_u + k - 1)
                    with_bias(banks[4 + k % 2][:, 0:w], cols, z[:, k % 2, 0:w], k % 4).then_inc(z_ready, 1)
                    if k >= 2:
                        output(k - 2)
                output(len(units) - 2)
                output(len(units) - 1)

            def diff_attend(g):
                def mix(k):
                    w = (k % NT + 1) * P
                    a, s = 2 * k % 4, 2 * (k % 2)
                    dve.wait_ge(p_ready, Z_AT["d", g] + 2 * k + 2)
                    if k >= 2:
                        dve.wait_ge(pT_done, U_D + 16 * g + k - 1)
                    nc.vector.reciprocal(rsum[:, a:a + 2], psum_p[:, a:a + 2])
                    then()
                    nc.vector.tensor_tensor(rsl[:, k % 2:k % 2 + 1], rsum[:, a + 1:a + 2], lam_col, ALU.mult)
                    then()
                    nc.vector.tensor_scalar(dprob[:, s + 1, 0:w], dprob[:, s + 1, 0:w], rsl[:, k % 2:k % 2 + 1], None, ALU.mult)
                    then()
                    nc.vector.scalar_tensor_tensor(dmix[:, k % 2, 0:w], dprob[:, s, 0:w], rsum[:, a:a + 1],
                                                   dprob[:, s + 1, 0:w], ALU.mult, ALU.add).then_inc(a_ready, 1)

                for k in range(16):
                    hh, t = k // NT, k % NT
                    dve.wait_ge(bias_ready, 9 + 4 * g + hh + 1)
                    for m in range(2):
                        v = 2 * k + m
                        dve.wait_ge(sc_done, SC_AT["d", g] + v + 1)
                        if v >= 2:
                            dve.wait_ge(p_ready, Z_AT["d", g] + v - 1)
                        with_bias(banks[4 + m][:, 0:(t + 1) * P], bias[:, hh % 2, (3 - t) * P:S],
                                  dz[:, m, 0:(t + 1) * P], v % 4).then_inc(z_ready, 1)
                    if k >= 1:
                        mix(k - 1)
                mix(15)

            def out_lo(key, y_at):
                for c in range(4):
                    dve.wait_ge(yhi_ready, OT_AT[key] + c + 1)
                    nc.vector.tensor_tensor(y_lo[:, y_at + c, :], banks[4 + c][:], y_hi[:, y_at + c, :].bitcast(fp32),
                                            ALU.subtract).then_inc(ylo_ready, 1)

            def group_norm(key, y_at, gains, gain_at, const):
                n = O_NORM[key]
                dve.wait_ge(osq_ready, n + 1)
                nc.vector.tensor_reduce(ossq, o_squares.rearrange("p j (h e) -> p (j h) e", e=P), AX.X, ALU.add)
                then()
                nc.vector.tensor_scalar(ossq, ossq, 1.0 / P, EPS, ALU.mult, ALU.add).then_inc(ovar_ready, 1)
                dve.wait_ge(osd_ready, n + 1)
                nc.vector.reciprocal(orstd, ossq)
                then()
                if const != 1.0:
                    nc.vector.tensor_scalar(orstd, orstd, const, None, ALU.mult)
                    then()
                o3 = o_tok.rearrange("p j (h e) -> p (j h) e", e=P)
                nc.vector.tensor_tensor(o3, o3, orstd.rearrange("p (a b) -> p a b", b=1).to_broadcast([P, 16, P]),
                                        ALU.mult).then_inc(on_ready, 1)
                for c in range(4):
                    dve.wait_ge(oT_done, OT_AT[key] + c + 1)
                    nc.vector.scalar_tensor_tensor(gate[:, c, :], banks[4 + c][:], par_col(gains, gain_at + c), gate[:, c, :],
                                                   ALU.mult, ALU.mult).then_inc(y_ready, 1)
                for c in range(4):
                    dve.wait_ge(yhi_ready, OT_AT[key] + c + 1)
                    nc.vector.tensor_tensor(y_lo[:, y_at + c, :], gate[:, c, :], y_hi[:, y_at + c, :].bitcast(fp32),
                                            ALU.subtract).then_inc(ylo_ready, 1)

            dve.wait_ge(x_in[2], 16)
            norm_scale("mem", 2, normed(mem_tok))
            dve.wait_ge(small_in, 32)
            norm_lo("mem", "mem_g", mem_hi, mem_lo, MEM)
            dve.wait_ge(x_in[0], 16)
            norm_scale("mix", 4, normed(x_tok))
            split_lo("xa", 0, ahead=0)
            split_lo("xa", 1, ahead=0)
            norm_lo("mix", "mix_g", h_hi, h_lo, S)
            lam4 = params[:, COLS["lam"]:COLS["lam"] + 4]
            neg, e, zz, z2, acc = (spt[:, 0:4], spt[:, 4:8], spt[:, 8:12], spt[:, 12:16], spt[:, 16:20])
            nc.vector.tensor_scalar(neg, lam4, -1.0, None, ALU.mult)
            then()
            nc.vector.tensor_tensor(neg, neg, lam4, ALU.max).then_inc(sp_e, 1)
            lprod = lqk[:, 0:2, :]
            nc.vector.tensor_tensor(lprod, lprod, lqk[:, 2:4, :], ALU.mult)
            then()
            nc.vector.tensor_reduce(lam_t[:, 0:2], lprod, AX.X, ALU.add).then_inc(lam_s, 1)
            nc.vector.memset(stats[:, 41:42], 64 * EPS)
            nc.vector.memset(stats[:, 42:43], EPS)
            nc.vector.memset(xa_pad[:, :, 0:3], 0.0)
            dve.wait_ge(sp_e, 2)
            nc.vector.tensor_scalar(acc, e, 2.0, None, ALU.add)
            then()
            nc.vector.reciprocal(acc, acc)
            then()
            nc.vector.tensor_tensor(zz, e, acc, ALU.mult)
            then()
            nc.vector.tensor_tensor(z2, zz, zz, ALU.mult)
            then()
            nc.vector.tensor_scalar(acc, z2, 1.0 / 15, None, ALU.mult)
            for k in (13, 11, 9, 7, 5, 3):
                then()
                nc.vector.scalar_tensor_tensor(acc, acc, 1.0 / k, z2, ALU.add, ALU.mult)
            then()
            nc.vector.scalar_tensor_tensor(acc, acc, 1.0, zz, ALU.add, ALU.mult)
            nc.vector.tensor_scalar(neg, lam4, -1.0, 0.0, ALU.mult, ALU.max)
            then()
            nc.vector.scalar_tensor_tensor(acc, acc, 2.0, neg, ALU.mult, ALU.add)
            then()
            nc.vector.tensor_scalar(sp8, acc, 8.0, None, ALU.mult)
            nc.vector.tensor_scalar(nsp8, acc, -8.0, None, ALU.mult).then_inc(sp_ready, 1)
            dve.wait_ge(lam_e, 1)
            nc.vector.tensor_tensor(lam_col, lam_t[:, 3:4], lam_t[:, 2:3], ALU.subtract)
            then()
            nc.vector.tensor_scalar(lam_col, lam_col, -LAM_INIT, None, ALU.add)
            then()
            for slot in range(2):
                for c in (2 * slot, 2 * slot + 1):
                    dve.wait_ge(acc_out[c], 1)
                    w = lambda k: par_col("lconv_w", 4 * c + k)
                    nc.vector.tensor_scalar(xc[:, c, :], xa_pad[:, c, 3:3 + S], w(3), par_col("lconv_b", c), ALU.mult, ALU.add)
                    for k in (2, 1, 0):
                        then()
                        done = nc.vector.scalar_tensor_tensor(xc[:, c, :], xa_pad[:, c, k:k + S], w(k), xc[:, c, :],
                                                              ALU.mult, ALU.add)
                    done.then_inc(xc_ready, 1)
                split_lo("xa", slot)
            both_lo("ga")
            split_lo("memk", 0)
            split_lo("memk", 1)
            for c in range(4):
                dve.wait_ge(lru_ta, 4)
                s = c % 2
                nc.vector.tensor_scalar(lru_tmp[:, s, :], lru_t[:, c, :], 1.0, None, ALU.add)
                then()
                nc.vector.reciprocal(lru_tmp[:, s, :], lru_tmp[:, s, :])
                then()
                nc.vector.scalar_tensor_tensor(lru_t[:, c, :], lru_t[:, c, :], 2.0, lru_tmp[:, s, :],
                                               ALU.mult, ALU.mult).then_inc(lru_m2, 1)
            both_lo("memv")
            both_lo("xq")
            dve.wait_ge(lru_ta, 8)
            for c in range(4):
                dve.wait_ge(lru_mult, c + 1)
                nc.vector.tensor_tensor(lru_i[:, c, :], lru_i[:, c, :], lru_t[:, c, :], ALU.mult)
                then()
                nc.vector.tensor_tensor(lru_i[:, c, :], lru_i[:, c, :], xc[:, c, :], ALU.mult)
                then()
                nc.vector.tensor_tensor_scan(xc[:, c, :], lru_r[:, c, :], lru_i[:, c, :], 0.0, ALU.mult, ALU.add)
                then()
                dve.wait_ge(acc_out[c], 2)
                nc.vector.tensor_tensor(xc[:, c, :], xc[:, c, :], ga_gelu[:, c, :], ALU.mult)
                then()
                nc.vector.tensor_copy(y_hi[:, c, :], xc[:, c, :])
                then()
                nc.vector.tensor_tensor(y_lo[:, c, :], xc[:, c, :], y_hi[:, c, :].bitcast(fp32),
                                        ALU.subtract).then_inc(ya_ready, 1)
            attend([(MEM, bias[:, k // NT % 2, 0:MEM], 1, o_tok[:, k % NT, k // NT * P:k // NT * P + P])
                    for k in range(16)], "x", U_X)
            out_lo("x", 8)
            both_lo("mq")
            both_lo("mk")
            both_lo("mv")
            attend([((t + 1) * P, bias[:, h % 2, (3 - t) * P:S], h + 2, o_tok[:, t, h * 64:h * 64 + 64])
                    for h in range(8) for t in range(NT)], "m", U_M)
            out_lo("m", 4)
            for n in range(3):
                with dve.Fori(0, 2) as i:
                    both_lo(f"gate{n}", i)
                t0 = TILE_AT[f"branch{n}"]
                for slot in range(2):
                    for c in range(4):
                        k = 4 * slot + c
                        dve.wait_ge(acc_done, t0 + k + 1)
                        dve.wait_ge(acc_out[k % 4], TILE_AT[f"gate{n}"] // 4 + k // 4 + 1)
                        if n == 0:
                            nc.vector.tensor_tensor(merged[:, k, :], banks[c][:], gT[:, k, :], ALU.mult).then_inc(acc_out[c], 1)
                            dve.wait_ge(acc_out[c], t0 // 4 + slot + 1)
                            nc.vector.engine_nop().then_inc(m_ready, 1)
                        else:
                            nc.vector.tensor_tensor(mtmp[:, c, :], banks[c][:], gT[:, k, :], ALU.mult).then_inc(acc_out[c], 1)
                            dve.wait_ge(acc_out[c], t0 // 4 + slot + 1)
                            nc.vector.tensor_tensor(merged[:, k, :], merged[:, k, :], mtmp[:, c, :], ALU.add).then_inc(m_ready, 1)
                            then()
                    split_lo(f"branch{n}", slot)
            for c in range(KT):
                dve.wait_ge(mhi_ready, c + 1)
                nc.vector.tensor_tensor(h_lo[:, c, :], merged[:, c, :], h_hi[:, c, :].bitcast(fp32),
                                        ALU.subtract).then_inc(mlo_ready, 1)
            dve.wait_ge(x_in[1], 16)
            def add_residual(name, t_off, half):
                for j in range(NT):
                    dve.wait_ge(acc_done, TILE_AT[name] + t_off + j + 1)
                    xs = x_tok[:, j, half * S:half * S + S]
                    nc.vector.tensor_tensor(xs, xs, banks[j][:], ALU.add).then_inc(acc_out[j], 1)

            for half in range(2):
                split_lo("wo", 0, half)
                add_residual("wo", 4 * half, half)
                split_lo("wo", 1, half)
            then()
            nc.vector.engine_nop().then_inc(x1_ready, 8)
            norm_scale("ffn", 4, normed(x_tok))
            norm_lo("ffn", "ffn_g", h_hi, h_lo, S)
            nc.vector.memset(gpad[:, :, 0:2], 0.0).then_inc(conv_ready, 1)
            for f in range(2):
                t0 = TILE_AT[f"ffn{f}"]
                with dve.Fori(0, 6) as i:
                    for c in range(2):
                        dve.wait_ge(acc_out[c], i + (t0 // 4 + 1))
                        col = lambda name, k: params[:, ds(i * 2 * k[1] + (COLS[name] + (12 * f + c) * k[1] + k[0]), 1)]
                        nc.vector.tensor_scalar(cv[:, c, :], gpad[:, c, 2:2 + S], col("fconv_w", (2, 3)), col("fconv_b", (0, 1)),
                                                ALU.mult, ALU.add)
                        then()
                        nc.vector.scalar_tensor_tensor(cv[:, c, :], gpad[:, c, 1:1 + S], col("fconv_w", (1, 3)), cv[:, c, :],
                                                       ALU.mult, ALU.add)
                        then()
                        nc.vector.scalar_tensor_tensor(cv[:, c, :], gpad[:, c, 0:S], col("fconv_w", (0, 3)), cv[:, c, :],
                                                       ALU.mult, ALU.add).then_inc(conv_ready, 1)
                    split_lo(f"ffn{f}", 0, i)
                    for c in range(2):
                        dve.wait_ge(gelu_ready, i * 2 + (12 * f + c + 1))
                        dve.wait_ge(acc_done, i * 4 + (t0 + 2 + c + 1))
                        nc.vector.tensor_tensor(pr[:, c, :], gl[:, c, :], banks[2 + c][:], ALU.mult).then_inc(acc_out[2 + c], 1)
                    for c in range(2):
                        dve.wait_ge(ahi_ready, i * 2 + (12 * f + c + 1))
                        nc.vector.tensor_tensor(y_lo[:, ds(i * 2 + c, 1), :].rearrange("p a s -> p (a s)"), pr[:, c, :],
                                                y_hi[:, ds(i * 2 + c, 1), :].rearrange("p a s -> p (a s)").bitcast(fp32),
                                                ALU.subtract).then_inc(alo_ready, 1)
                    split_lo(f"ffn{f}", 1, i)
                name = f"down{f}"
                for half in range(2):
                    for k in range(2):
                        split_lo(name, 3 * half + k)
                    add_residual(name, 4 * half, half)
                    split_lo(name, 3 * half + 2)
                then()
                nc.vector.engine_nop().then_inc(x1_ready, 8)
            dve.wait_ge(x_in[3], 16)
            norm_scale("final", 4, lambda j: nc.vector.scalar_tensor_tensor(
                x_tok[:, j, :], x_tok[:, j, :], rstd[:, j:j + 1], gain_row, ALU.mult, ALU.mult).then_inc(xb_ready, 1))
            then()
            norm_scale("norm2", 4, normed(x_tok))
            norm_lo("norm2", "norm2_g", h_hi, h_lo, S)
            dve.wait_ge(xb_out, 16)
            for g in range(2):
                both_lo(f"rqk{g}")
                both_lo(f"rv{g}")
                both_lo(f"rg{g}")
                for hh in range(4):
                    head = 4 * g + hh
                    dve.wait_ge(dec_ready, head + 1)
                    if head >= 2:
                        dve.wait_ge(so_done, head - 1)
                    for c in range(NT):
                        r = 4 * head + c
                        dve.wait_ge(sc_done, SC_AT["r", 0] + r + 1)
                        n = S - c * P
                        nc.vector.tensor_tensor(st[:, hh % 2, ST_AT[c]:ST_AT[c] + n], banks[4 + r % 2][:, 0:n],
                                                bias[:, hh % 2, 0:n], ALU.mult).then_inc(st_ready, 1)
                group_norm(("r", g), 4 * g, "ret_g", 4 * g, 1.0)

            def gate_tile(name, k):
                return TILE_AT[name] // 4 + k // 4 + 1
            with dve.Fori(0, 2) as i:
                both_lo("rmg", i)
            for i in range(2):
                for slot in range(2):
                    for c in range(2):
                        b = 2 * slot + c
                        k = 4 * i + b
                        dve.wait_ge(acc_done, TILE_AT["rwo"] + k + 1)
                        dve.wait_ge(acc_out[b], gate_tile("rmg", k))
                        nc.vector.tensor_tensor(m_ret[:, k, :], banks[b][:], gT[:, k, :], ALU.mult).then_inc(acc_out[b], 1)
                    split_lo("rwo", slot, i)
            then()
            nc.vector.engine_nop().then_inc(mret_ready, 8)
            dve.wait_ge(mret_out, 16)
            for g in range(2):
                def unit_norms(which):
                    for c in range(4):
                        dve.wait_ge(dsd_ready, 8 * g + 4 * which + c + 1)
                        sd, v = dsq[:, 4 * which + c, :], (qT, kT)[which][:, c, :]
                        nc.vector.reciprocal(sd, sd)
                        then()
                        nc.vector.scalar_tensor_tensor(v, v, par_col(("dq_g", "dk_g")[which]), sd,
                                                       ALU.mult, ALU.mult).then_inc(dn_ready, 1)

                both_lo(f"dq{g}")
                split_lo(f"dk{g}", 0)
                unit_norms(0)
                split_lo(f"dk{g}", 1)
                both_lo(f"dv{g}")
                unit_norms(1)
                both_lo(f"dg{g}")
                diff_attend(g)
                group_norm(("d", g), 4 * g, "sub_g", 4 * g, 1.0 - LAM_INIT)
            with dve.Fori(0, 2) as i:
                both_lo("dmg", i)
            dve.wait_ge(x_in[5], 16)
            for i in range(2):
                for slot in range(2):
                    for c in range(2):
                        b = 2 * slot + c
                        k = 4 * i + b
                        dve.wait_ge(acc_done, TILE_AT["dwo"] + k + 1)
                        dve.wait_ge(acc_out[b], gate_tile("dmg", k))
                        nc.vector.tensor_tensor(gT[:, k, :], banks[b][:], gT[:, k, :], ALU.mult).then_inc(acc_out[b], 1)
                        dve.wait_ge(acc_out[b], gate_tile("dwo", k))
                        nc.vector.tensor_tensor(gT[:, k, :], gT[:, k, :], m_ret[:, k, :], ALU.add).then_inc(m_ready, 1)
                        dve.wait_ge(mhi_ready, M_AT["two"] + k + 1)
                        nc.vector.tensor_tensor(h_lo[:, k, :], gT[:, k, :], h_hi[:, k, :].bitcast(fp32),
                                                ALU.subtract).then_inc(mlo_ready, 1)
                    split_lo("dwo", slot, i)
            dve.wait_ge(x_in[4], 16)
            for half in range(2):
                split_lo("wo2", 0, half)
                for j in range(NT):
                    dve.wait_ge(acc_done, TILE_AT["wo2"] + 4 * half + j + 1)
                    cols = slice(half * S, half * S + S)
                    nc.vector.tensor_tensor(res[:, j, cols], xb[:, j, cols], banks[4 * half + j][:], ALU.add).then_inc(res_ready, 1)
                split_lo("wo2", 1, half)


_INPUTS = ("x", "mem", "par", "lru_w", "lqk", "final_g", "wstream")


def _laid_out(v):
    a = {k: np.asarray(t) for k, t in v.items()}

    def cols(t, n):
        return t.reshape(n, P).T

    def strip_a(w, c0):
        return w[:, c0:c0 + 256].reshape(KT, P, 256).transpose(1, 0, 2).reshape(P, STRIP)

    def strip_b(w, r0, c0):
        return w[r0:r0 + 512, c0:c0 + 512].reshape(4, P, 512).transpose(1, 0, 2).reshape(P, STRIP)

    w1, w2, kv = a["w_in"][0], a["w_in_2"][0], a["w_mem_kv"][0]
    strips = []

    def take_a(w, c0, n):
        strips.extend(strip_a(w, c0 + 256 * i) for i in range(n))

    def take_b(w, c0, halves, r0=0, k=2):
        strips.extend(strip_b(w, r0 + 512 * i, c0 + 512 * h) for h in range(halves) for i in range(k))

    for c0 in (0, 512):
        take_a(w1, c0, 2)
    take_a(kv, 0, 2)
    take_b(kv, 512, 1)
    take_a(w1, 2560, 2)
    take_a(w1, 1024, 2)
    take_a(w1, 1536, 2)
    take_b(w1, 2048, 1)
    for n in range(3):
        take_a(w1, 3072 + D * n, 4)
        take_b(a["w_branch"][0, n], 0, 2, k=1)
    take_b(a["w_out"][0], 0, 2)
    wg, wu, wd = a["w_ffn_gate"][0], a["w_ffn_up"][0], a["w_ffn_down"][0]
    for f in range(2):
        for i in range(6):
            take_a(wg, (6 * f + i) * 256, 1)
            take_a(wu, (6 * f + i) * 256, 1)
        take_b(wd, 0, 2, r0=f * FF // 2, k=3)
    for g in range(2):
        take_a(w2, 256 * g, 1)
        take_a(w2, 512 + 256 * g, 1)
        take_b(w2, 1024 + 512 * g, 1)
        take_a(w2, 2048 + 512 * g, 2)
    take_a(w2, 7168, 4)
    take_a(a["ret_w_o_2"][0], 0, 4)
    for g in range(2):
        take_a(w2, 3072 + 512 * g, 2)
        take_a(w2, 4096 + 512 * g, 2)
        take_b(w2, 5120 + 512 * g, 1)
        take_a(w2, 6144 + 512 * g, 2)
    take_a(w2, 8192, 4)
    take_a(a["diff_w_o_2"][0], 0, 4)
    take_b(a["w_out_2"][0], 0, 2)
    assert len(strips) == STRIPS

    twice = lambda t: np.concatenate([t, t]).reshape(P, 1)
    small = np.concatenate([
        cols(a["mix_norm_gain"][0], 8), cols(a["mem_norm_gain"][0], 8), cols(a["ffn_norm_gain"][0], 8),
        cols(a["norm_g_2"][0], 8),
        a["lru_conv_w"][0].reshape(4, 4, P).transpose(2, 1, 0).reshape(P, 16), cols(a["lru_conv_b"][0], 4),
        cols(a["lru_b_a"][0].reshape(-1), 4), cols(a["lru_b_x"][0].reshape(-1), 4), cols(a["lru_lambda"][0], 4),
        a["ffn_conv_w"][0].reshape(3, FFT, P).transpose(2, 1, 0).reshape(P, 3 * FFT), cols(a["ffn_conv_b"][0], FFT),
        cols(a["ret_norm_g_2"][0], 8), twice(a["diff_q_norm_g_2"][0]), twice(a["diff_k_norm_g_2"][0]),
        cols(a["diff_sub_norm_g_2"][0], 8)], axis=1)
    lru = np.stack([a[k][0].reshape(4, P, 64).transpose(1, 0, 2) for k in ("lru_w_a", "lru_w_x")], axis=1)
    lq = np.stack([a[f"diff_{k}_2"][0] for k in ("lq1", "lq2", "lk1", "lk2")])
    return {
        "x": a["x"][0], "mem": a["mem"][0], "par": small, "lru_w": lru,
        "lqk": np.broadcast_to(lq, (P, 4, 64)), "final_g": np.broadcast_to(a["final_norm_gain"], (P, D)),
        "wstream": np.concatenate(strips, axis=0),
    }


def kernel(**inputs):
    import concourse.bacc as _bacc
    from concourse.bass_utils import run_bass_kernel_spmd as _run

    nc = _bacc.Bacc("TRN2", target_bir_lowering=False, num_devices=1)
    laid = _laid_out(inputs)
    arrays, args = {}, []
    for name in _INPUTS:
        arr = np.ascontiguousarray(laid[name])
        arrays[f"in_{name}"] = arr
        args.append(nc.dram_tensor(f"in_{name}", arr.shape, mybir.dt.from_np(arr.dtype), kind="ExternalInput").ap())
    out = nc.dram_tensor("out_dram", (S, D), mybir.dt.float32, kind="ExternalOutput").ap()
    xb = nc.dram_tensor("xb_dram", (S, D), mybir.dt.float32, kind="Internal").ap()
    mret = nc.dram_tensor("mret_dram", (P, KT * S), mybir.dt.float32, kind="Internal").ap()
    hybrid_block_kernel(nc, *args, out, xb, mret)
    r = _run(nc, [arrays], core_ids=[0])
    return r.results[0]["out_dram"].reshape(1, S, D)
```

```python
from contextlib import ExitStack

import numpy as np
import concourse.bass as bass
from concourse import mybir

P = 128
D = 1024
KT = D // P
S = 512
NT = S // P
MEM = 256
STRIP = 2048
FF = 3072
FFT = FF // P
EPS = 1e-6
MASKED = -1e30
FAR = 1e6
LAM_INIT = 0.2

PHASES = [("xa", 2), ("ga", 2), ("memk", 2), ("memv", 2), ("xq", 2), ("mq", 2), ("mk", 2), ("mv", 2)]
for _n in range(3):
    PHASES += [(f"gate{_n}", 4), (f"branch{_n}", 2)]
PHASES += [("wo", 4)]
for _f in range(2):
    PHASES += [(f"ffn{_f}", 12), (f"down{_f}", 6)]
PHASES += [("rqk0", 2), ("rv0", 2), ("rqk1", 2), ("rv1", 2), ("rg0", 2), ("rmg", 4), ("rg1", 2), ("rwo", 4)]
PHASES += [("dqk0", 2), ("dv0", 2), ("dqk1", 2), ("dg0", 2), ("dqk2", 2), ("dv1", 2), ("dqk3", 2), ("dg1", 2)]
PHASES += [("dmg", 4), ("dwo", 4), ("wo2", 4)]

STRIP_AT, TILE_AT, OPEN_AT = {}, {}, {}
_s = _t = _u = 0
for _name, _k in PHASES:
    STRIP_AT[_name], TILE_AT[_name], OPEN_AT[_name] = _s, _t, _u
    _s += _k
    _t += 8 if _name.startswith(("down", "branch")) else 4 if _name == "memv" else 2 * _k
    if _name.startswith("down"):
        _u += 4
    elif _name in ("mv", "memv", "wo", "wo2", "rv0", "rv1", "dv0", "dv1"):
        _u += _k // 2
STRIPS = _s

COLS = {}
_c = 0
for _name, _k in [("mix_g", 8), ("mem_g", 8), ("ffn_g", 8), ("norm2_g", 8), ("lconv_w", 16), ("lconv_b", 4),
                  ("b_a", 4), ("b_x", 4), ("lam", 4), ("fconv_w", 72), ("fconv_b", 24), ("ret_g", 8),
                  ("dq_g", 1), ("dk_g", 1), ("sub_g", 8)]:
    COLS[_name] = _c
    _c += _k
NPAR = _c


def pacer(steps, num, den):
    at = [0]

    def slot():
        at[0] += 1
        for _ in range(at[0] * num // den - (at[0] - 1) * num // den):
            next(steps, None)
    return slot


def finish(steps):
    for _ in steps:
        pass


def hybrid_block_kernel(nc, x, mem, par, lru_w, lqk_in, final_g, wstream, out, xb_dram, mret_dram):
    fp32, fp32r = mybir.dt.float32, mybir.dt.float32r
    ALU, ACT, AX = mybir.AluOpType, mybir.ActivationFunctionType, mybir.AxisListType
    ds = bass.ds

    ctx = ExitStack()
    with ctx:
        def sb(name, shape, dt=fp32):
            return ctx.enter_context(nc.sbuf_tensor(name, shape, dt))

        def sem(name):
            return ctx.enter_context(nc.semaphore(name))

        w_raw = sb("w_raw", [P, 2, STRIP])
        w_hi = sb("w_hi", [P, 2, STRIP], fp32r)
        w_lo = sb("w_lo", [P, 2, STRIP], fp32r)
        h_hi = sb("h_hi", [P, KT, S], fp32r)
        h_lo = sb("h_lo", [P, KT, S], fp32r)
        y_hi = sb("y_hi", [P, 12, S], fp32r)
        y_lo = sb("y_lo", [P, 12, S], fp32r)
        params = sb("params", [P, NPAR])
        lqk = sb("lqk", [P, 4, 64])
        ident = sb("ident", [P, P])
        half_ones = sb("half_ones", [P, P])
        neg_dist = sb("neg_dist", [P, S])
        fwd_dist = sb("fwd_dist", [P, S])
        stats = sb("stats", [P, 192])
        arena = sb("arena", [P, 18496])
        banks = [ctx.enter_context(nc.psum_tensor(f"bank{i}", [P, 512], fp32)) for i in range(8)]
        T_BANK, O_BANK = banks[6], banks[7]

        def view(where, at, *shape):
            v = where[:, at:at + int(np.prod(shape))]
            return v.rearrange("p (a b) -> p a b", b=shape[1]) if len(shape) == 2 else v

        def par_col(name, i=0):
            return params[:, COLS[name] + i:COLS[name] + i + 1]

        x_in_tok = view(arena, 0, NT, D)
        xn0 = view(arena, 12320, NT, D)
        squares0 = view(arena, 4096, NT, D)
        mem_tok = view(arena, 8192, 2, D)
        mem_hi, mem_lo = (v[:, 8:12, :].rearrange("p a (b s) -> p (a b) s", b=2) for v in (y_hi, y_lo))
        xa_pad = view(arena, 0, 4, S + 3)
        lru_t = view(arena, 0, 4, S)
        xc = view(arena, 2080, 4, S)
        lru_r = view(arena, 4128, 4, S)
        lru_i = view(arena, 6176, 4, S)
        ga_gelu = view(arena, 8224, 4, S)
        lru_tmp = view(arena, 10272, 2, S)
        wa_bd = view(arena, 11296, 4, P)
        wx_bd = view(arena, 11808, 4, P)
        mkT = view(arena, 12320, 4, MEM)
        mv_tok = view(arena, 13344, 2, S)
        xqT = view(arena, 14368, 4, S)
        qT = view(arena, 0, 4, S)
        kT = view(arena, 2048, 4, S)
        v_tok = view(arena, 4096, 4, S)
        z = view(arena, 6144, 2, S)
        prob = view(arena, 7168, 2, S)
        bias1 = view(arena, 8192, 2, S)
        pT1 = view(arena, 9216, 2, S)
        o_tok1 = view(arena, 10240, 4, S)
        merged = view(arena, 12320, KT, S)
        gT = view(arena, 0, KT, S)
        mtmp = view(arena, 4096, 4, S)
        x_tok = view(arena, 6144, NT, D)
        xn = view(arena, 0, NT, D)
        squares = view(arena, 12320, NT, D)
        gain_row = view(arena, 4608, D)
        gpad = view(arena, 12320, 2, S + 2)
        cv = view(arena, 13408, 2, S)
        gl = view(arena, 14432, 2, S)
        pr = view(arena, 15456, 2, S)
        rqT = [view(arena, 4096 * g, 2, S) for g in range(2)]
        rkT = [view(arena, 4096 * g + 1024, 2, S) for g in range(2)]
        rv = [view(arena, 4096 * g + 2048, 4, S) for g in range(2)]
        gate = view(arena, 8192, 4, S)
        o_tok = view(arena, 10240, 4, S)
        st = view(arena, 12288, 2, 1280)
        ST_AT = [0, 512, 896, 1152]
        decay = view(arena, 14848, 2, S)
        o_squares = view(arena, 15872, 4, S)
        m_ret = view(arena, 0, KT, S)
        m_back = view(arena, 4096, KT, S)
        dqT = [view(arena, 4096 * p, 2, S) for p in range(2)]
        dkT = [view(arena, 4096 * p + 1024, 2, S) for p in range(2)]
        dv = [view(arena, 4096 * p + 2048, 4, S) for p in range(2)]
        do_tok = [view(arena, 10240 + 1024 * p, 4, 2 * P) for p in range(2)]
        bias2 = view(arena, 12288, 2, S)
        pT2 = view(arena, 13312, 2, S)
        dprob = view(arena, 14336, 4, S)
        dsq = view(arena, 16384, 4, S)
        xb = view(arena, 8192, NT, D)
        res = view(arena, 0, NT, D)

        ssq = stats[:, 0:4]
        rstd = stats[:, 4:8]
        sp8 = stats[:, 8:12]
        nsp8 = stats[:, 12:16]
        spt = stats[:, 16:36]
        lam_col = stats[:, 36:37]
        lam_t = stats[:, 37:41]
        nmax = stats[:, 44:48]
        psum_p = stats[:, 48:56]
        rsum = stats[:, 56:64]
        rsl = stats[:, 64:68]
        ossq = stats[:, 72:88]
        orstd = stats[:, 88:104]

        raw_in = [sem("raw_in0"), sem("raw_in1")]
        w_hi_ready = sem("w_hi_ready")
        w_lo_ready = sem("w_lo_ready")
        open_used = sem("open_used")
        acc_done = sem("acc_done")
        acc_out = [sem(f"acc_out{i}") for i in range(4)]
        small_in = sem("small_in")
        lruw_in = sem("lruw_in")
        x_in = [sem("x_in0"), sem("x_in1"), sem("mem_in"), sem("row_in"), sem("xb_in"), sem("mret_in")]
        x_ready = sem("x_ready")
        const_ready = sem("const_ready")
        lruw_ready = sem("lruw_ready")
        ssq_ready, var_ready, sd_ready = sem("ssq_ready"), sem("var_ready"), sem("sd_ready")
        xn_ready, hT_done, hhi_ready, hlo_ready = sem("xn_ready"), sem("hT_done"), sem("hhi_ready"), sem("hlo_ready")
        sp_e, sp_ready = sem("sp_e"), sem("sp_ready")
        lam_s, lam_e, lam_ready = sem("lam_s"), sem("lam_e"), sem("lam_ready")
        xc_ready, lru_mm, lru_ri, lru_ta, lru_m2, lru_mult, ya_ready = (
            sem(n) for n in ("xc_ready", "lru_mm", "lru_ri", "lru_ta", "lru_m2", "lru_mult", "ya_ready"))
        sc_done, z_ready, p_ready, pT_done, pT_out, o_done, o_out = (
            sem(n) for n in ("sc_done", "z_ready", "p_ready", "pT_done", "pT_out", "o_done", "o_out"))
        bias_ready, a_ready = sem("bias_ready"), sem("a_ready")
        osq_ready, ovar_ready, osd_ready, on_ready, oT_done, y_ready, yhi_ready, ylo_ready = (
            sem(n) for n in ("osq_ready", "ovar_ready", "osd_ready", "on_ready", "oT_done", "y_ready",
                             "yhi_ready", "ylo_ready"))
        gate_ready, m_ready, mhi_ready, mlo_ready = (
            sem(n) for n in ("gate_ready", "m_ready", "mhi_ready", "mlo_ready"))
        conv_ready, gelu_ready, ahi_ready, alo_ready = (
            sem(n) for n in ("conv_ready", "gelu_ready", "ahi_ready", "alo_ready"))
        x1_ready, xb_ready, xb_out, mret_ready, mret_out = (
            sem(n) for n in ("x1_ready", "xb_ready", "xb_out", "mret_ready", "mret_out"))
        dsq_ready, dss_done, dsd_ready, dn_ready = (
            sem(n) for n in ("dsq_ready", "dss_done", "dsd_ready", "dn_ready"))
        st_ready, so_done, so_out, dec_ready = (sem(n) for n in ("st_ready", "so_done", "so_out", "dec_ready"))
        res_ready, res_out = sem("res_ready"), sem("res_out")

        NORMS = ["mix", "mem", "ffn", "final", "norm2"]
        SSQ_AT = dict(zip(NORMS, [0, 4, 6, 10, 14]))
        XN_AT = dict(zip(NORMS, [0, 4, 6, None, 10]))
        HT_AT = dict(zip(NORMS, [0, 8, 16, None, 24]))
        U_X, U_M, U_D = 0, 16, 48
        SC_AT = {"x": 0, "m": 16, "r": 48, "d": 80}
        Z_AT = {"x": 0, "m": 16, "d": 48}
        O_NORM = {"r0": 0, "r1": 1, "d0": 2, "d1": 3, "d2": 4, "d3": 5}
        OT_AT = {"x": 0, "m": 4, "r0": 8, "r1": 12, "d0": 16, "d1": 18, "d2": 20, "d3": 22}
        M_AT = {"one": 0, "two": 8}
        MOBA_UNITS = [(h, t) for h in range(8) for t in range(NT)]
        PACE = {"x": (1, 1), "m": (4, 3), "r": (1, 1), "d": (1, 1), "d3": (5, 4)}

        block = ctx.enter_context(nc.Block())

        @block.sync
        def _(sp):
            xv = x.rearrange("(j p) d -> p j d", p=P)
            sp.dma_start(x_in_tok, xv).then_inc(x_in[0], 16)
            sp.dma_start(params[:], par).then_inc(small_in, 16)
            for slot in range(2):
                sp.dma_start(w_raw[:, slot, :], wstream[slot * P:(slot + 1) * P, :]).then_inc(raw_in[slot], 16)
            sp.dma_start(mem_tok, mem.rearrange("(j p) d -> p j d", p=P)).then_inc(x_in[2], 16)
            sp.dma_start(lqk[:], lqk_in).then_inc(small_in, 16)

            def strips(lo, hi):
                with sp.Fori(lo, hi) as i:
                    for slot in range(2):
                        sp.wait_ge(w_lo_ready, i * 2 + (slot - 1))
                        sp.dma_start(w_raw[:, slot, :], wstream[ds(i * (2 * P) + slot * P, P), :]).then_inc(raw_in[slot], 16)

            def first(name):
                return STRIP_AT[name] // 2 + 1

            strips(1, first("gate1"))
            sp.wait_ge(oT_done, OT_AT["m"] + 4)
            sp.dma_start(x_tok, xv).then_inc(x_in[1], 16)
            strips(first("gate1"), first("down1"))
            sp.dma_start(gain_row, final_g).then_inc(x_in[3], 16)
            strips(first("down1"), first("rqk0"))
            sp.wait_ge(xb_ready, NT)
            sp.dma_start(xb_dram.rearrange("(j p) d -> p j d", p=P), x_tok).then_inc(xb_out, 16)
            strips(first("rqk0"), first("dqk0"))
            sp.wait_ge(mret_ready, KT)
            sp.dma_start(mret_dram.rearrange("p (c s) -> p c s", s=S), m_ret).then_inc(mret_out, 16)
            strips(first("dqk0"), first("dwo"))
            sp.wait_ge(mret_out, 16)
            sp.wait_ge(o_out, U_D + 32)
            sp.dma_start(m_back, mret_dram.rearrange("p (c s) -> p c s", s=S)).then_inc(x_in[5], 16)
            sp.wait_ge(xb_out, 16)
            sp.wait_ge(ylo_ready, OT_AT["d3"] + 2)
            sp.dma_start(xb, xb_dram.rearrange("(j p) d -> p j d", p=P)).then_inc(x_in[4], 16)
            strips(first("dwo"), first("wo2"))
            strips(first("wo2"), STRIPS // 2)
            for half in range(2):
                sp.wait_ge(res_ready, NT * (half + 1))
                sp.dma_start(out.rearrange("(j p) d -> p j d", p=P)[:, :, half * S:half * S + S],
                             res[:, :, half * S:half * S + S]).then_inc(res_out, 16)
            sp.wait_ge(res_out, 32)

        @block.gpsimd
        def _(pool):
            nc.gpsimd.memset(ident[:], 0.0)
            nc.gpsimd.memset(half_ones[:], 1.0)
            nc.gpsimd.memset(wa_bd, 0.0)
            nc.gpsimd.memset(wx_bd, 0.0)
            nc.gpsimd.iota(neg_dist[:], pattern=[[1, S]], base=-3 * P, channel_multiplier=-1,
                           allow_small_or_imprecise_dtypes=True)
            nc.gpsimd.iota(fwd_dist[:], pattern=[[1, S]], base=0, channel_multiplier=-1,
                           allow_small_or_imprecise_dtypes=True)
            pool.drain()
            nc.gpsimd.affine_select(out=ident[:], in_=ident[:], compare_op=ALU.not_equal, fill=1.0, base=0,
                                    pattern=[[-1, P]], channel_multiplier=1)
            nc.gpsimd.affine_select(out=half_ones[:, 0:64], in_=half_ones[:, 0:64], compare_op=ALU.is_ge, fill=0.0,
                                    base=63, pattern=[[0, 64]], channel_multiplier=-1)
            nc.gpsimd.affine_select(out=half_ones[:, 64:P], in_=half_ones[:, 64:P], compare_op=ALU.is_ge, fill=0.0,
                                    base=-64, pattern=[[0, 64]], channel_multiplier=1)
            nc.gpsimd.affine_select(out=neg_dist[:], in_=neg_dist[:], compare_op=ALU.is_ge, fill=MASKED,
                                    base=3 * P, pattern=[[-1, S]], channel_multiplier=1)
            nc.gpsimd.affine_select(out=fwd_dist[:], in_=fwd_dist[:], compare_op=ALU.is_ge, fill=FAR,
                                    base=0, pattern=[[1, S]], channel_multiplier=-1).then_inc(const_ready, 1)
            pool.wait_ge(const_ready, 1)
            for k, bd in enumerate((wa_bd, wx_bd)):
                for s in range(2):
                    pool.dma_start(bd[64 * s:64 * s + 64, :, 64 * s:64 * s + 64],
                                   lru_w[64 * s:64 * s + 64, k, :, :]).then_inc(lruw_in, 16)
            pool.wait_ge(ya_ready, 4)
            nc.gpsimd.memset(bias1, 0.0).then_inc(bias_ready, 1)
            for h in range(8):
                pool.wait_ge(z_ready, U_M + max(0, 4 * (h - 1)))
                nc.gpsimd.tensor_scalar(bias1[:, h % 2, :], neg_dist[:], 2.0 ** -(h + 1), None,
                                        ALU.mult).then_inc(bias_ready, 1)
            for h in range(8):
                if h < 2:
                    pool.wait_ge(so_out, 8)
                else:
                    pool.wait_ge(z_ready, Z_AT["d"] + 8 * (h - 1))
                nc.gpsimd.tensor_scalar(bias2[:, h % 2, :], neg_dist[:], 2.0 ** -(h + 1), None,
                                        ALU.mult).then_inc(bias_ready, 1)

        @block.tensor
        def _(pe):
            def free_bank(b, uses):
                if not isinstance(uses, int) or uses > 0:
                    pe.wait_ge(acc_out[b], uses)

            def three(dst, w, a, weights_still, first, last):
                for k, (i, j) in enumerate(((0, 0), (0, 1), (1, 0))):
                    l, r = (w[i], a[j]) if weights_still else (a[j], w[i])
                    done = nc.tensor.matmul(dst, l, r, start=first and k == 0, stop=last and k == 2)
                return done

            def pair_a(name, i=0, src=(h_hi, h_lo), n=S, side=None, hooks={}):
                s0, t0 = STRIP_AT[name], TILE_AT[name]
                for slot in range(2):
                    pe.wait_ge(w_lo_ready, i * 2 + (s0 + slot + 1))
                    for c in range(2):
                        b = 2 * slot + c
                        free_bank(b, i + t0 // 4)
                        for kt in range(KT):
                            cols = slice(kt * 256 + c * P, kt * 256 + c * P + P)
                            done = three(banks[b][:, 0:n], (w_hi[:, slot, cols], w_lo[:, slot, cols]),
                                         (src[0][:, kt, :], src[1][:, kt, :]), True, kt == 0, kt == KT - 1)
                            if kt == KT - 1:
                                done.then_inc(acc_done, 1)
                            if kt % 4 == 3:
                                if side:
                                    side()
                                if 4 * slot + 2 * c + kt // 4 in hooks:
                                    hooks[4 * slot + 2 * c + kt // 4]()

            def group_b(name, i=0, src=(h_hi, h_lo), strips=2, s_off=0, t_off=0, b_off=0, side=None,
                        hooks={}):
                s0, t0 = STRIP_AT[name] + s_off, TILE_AT[name] + t_off
                for k in range(strips):
                    slot = (s0 + k) % 2
                    pe.wait_ge(w_lo_ready, i * strips + (s0 + k + 1))
                    for j in range(NT):
                        if k == 0 and b_off == 0:
                            free_bank(j, i + t0 // 4)
                        for q in range(4):
                            kt, cols, tok = 4 * k + q, slice(q * 512, q * 512 + 512), slice(j * P, j * P + P)
                            done = three(banks[b_off + j][:], (w_hi[:, slot, cols], w_lo[:, slot, cols]),
                                         (src[0][:, kt, tok], src[1][:, kt, tok]), False, kt == 0, kt == 4 * strips - 1)
                        if k == strips - 1:
                            done.then_inc(acc_done, 1)
                        elif j == NT - 1:
                            done.then_inc(open_used, 1)
                        if side:
                            side()
                        if 4 * k + j in hooks:
                            hooks[4 * k + j]()

            def pair_c(name, y_at, side=None):
                s0, t0 = STRIP_AT[name], TILE_AT[name]
                for slot in range(2):
                    pe.wait_ge(w_lo_ready, s0 + slot + 1)
                    for c in range(4):
                        free_bank(c, t0 // 4 + slot)
                        for q in range(4):
                            cols = slice(q * 512 + c * P, q * 512 + c * P + P)
                            done = three(banks[c][:], (w_hi[:, slot, cols], w_lo[:, slot, cols]),
                                         (y_hi[:, y_at + q, :], y_lo[:, y_at + q, :]), True, q == 0, q == 3)
                        done.then_inc(acc_done, 1)
                        if side:
                            side()

            def loop_a(name, pairs, **kw):
                with pe.Fori(0, pairs) as i:
                    pair_a(name, i, **kw)

            def norm_t(name, tiles, xn=xn):
                pe.wait_ge(xn_ready, XN_AT[name] + tiles)
                for kt in range(KT):
                    if HT_AT[name] + kt >= 4:
                        pe.wait_ge(hlo_ready, HT_AT[name] + kt - 3)
                    for j in range(tiles):
                        done = nc.tensor.transpose(banks[4 + kt % 4][:, j * P:j * P + P],
                                                   xn[:, j, kt * P:kt * P + P], ident[:])
                    done.then_inc(hT_done, 1)
                pe.wait_ge(hlo_ready, HT_AT[name] + KT)

            def attend(units, o_cols, base_u, o_tok):
                def scores(k):
                    if k >= 2:
                        pe.wait_ge(z_ready, base_u + k - 1)
                    nc.tensor.matmul(banks[4 + k % 2][:, 0:units[k][2]], *units[k][0],
                                     start=True, stop=True).then_inc(sc_done, 1)

                def transposes(k):
                    pe.wait_ge(p_ready, base_u + k + 1)
                    if k >= 1:
                        pe.wait_ge(pT_out, base_u + k)
                    for c in range(units[k][2] // P):
                        done = nc.tensor.transpose(T_BANK[:, c * P:c * P + P], prob[:, k % 2, c * P:c * P + P], ident[:])
                    done.then_inc(pT_done, 1)

                def outputs(k):
                    pe.wait_ge(pT_out, base_u + k + 1)
                    if k >= 1:
                        pe.wait_ge(o_out, base_u + k)
                    vals = units[k][1]
                    for c, val in enumerate(vals):
                        done = nc.tensor.matmul(O_BANK[:, 0:o_cols], pT1[:, k % 2, c * P:c * P + P], val,
                                                start=c == 0, stop=c == len(vals) - 1)
                    done.then_inc(o_done, 1)

                scores(0)
                yield
                for k in range(len(units)):
                    if k + 1 < len(units):
                        scores(k + 1)
                    if k >= 1:
                        outputs(k - 1)
                    transposes(k)
                    yield
                outputs(len(units) - 1)
                yield
                pe.wait_ge(o_out, base_u + len(units))
                for c in range(4):
                    for j in range(NT):
                        done = nc.tensor.transpose(banks[4 + c][:, j * P:j * P + P], o_tok[:, j, c * P:c * P + P], ident[:])
                    done.then_inc(oT_done, 1)
                yield

            def ret_attend(g):
                def outputs(hh):
                    head = 4 * g + hh
                    pe.wait_ge(st_ready, 4 * head + 4)
                    if head >= 2:
                        pe.wait_ge(so_out, head - 1)
                    for j in range(NT):
                        for c in range(j + 1):
                            at = ST_AT[c] + (j - c) * P
                            done = nc.tensor.matmul(banks[6 + head % 2][:, j * P:j * P + P], st[:, hh % 2, at:at + P],
                                                    rv[g][:, c, hh * P:hh * P + P], start=c == 0, stop=c == j)
                    done.then_inc(so_done, 1)

                for hh in range(4):
                    rows, tile = slice(64 * (hh % 2), 64 * (hh % 2) + 64), hh // 2
                    for c in range(NT):
                        r = (4 * g + hh) * 4 + c
                        if r >= 2:
                            pe.wait_ge(st_ready, r - 1)
                        if g == 1 and r == 16:
                            pe.wait_ge(y_ready, 4)
                        nc.tensor.matmul(banks[4 + r % 2][:, 0:S - c * P], rkT[g][rows, tile, c * P:c * P + P],
                                         rqT[g][rows, tile, c * P:S], start=True, stop=True).then_inc(sc_done, 1)
                        if c == 1 and hh >= 1:
                            outputs(hh - 1)
                        yield
                yield
                outputs(3)
                yield

            def group_t(key, tokens, tiles, b0):
                pe.wait_ge(on_ready, O_NORM[key] + 1)
                for c in range(tiles):
                    for j in range(NT):
                        done = nc.tensor.transpose(banks[b0 + c][:, j * P:j * P + P], tokens[:, j, c * P:c * P + P], ident[:])
                    done.then_inc(oT_done, 1)

            def group_side(key, tokens, tiles, b0, at):
                for _ in range(at):
                    yield
                group_t(key, tokens, tiles, b0)
                yield

            def diff_attend(g):
                q, k_, v = dqT[g % 2], dkT[g % 2], dv[g // 2]
                base_u, z0 = U_D + 8 * g, Z_AT["d"] + 16 * g

                def scores(k):
                    hh, t = k // NT, k % NT
                    for m in range(2):
                        if g or k:
                            pe.wait_ge(z_ready, z0 + 2 * k + m - 1)
                        rows = slice(64 * m, 64 * m + 64)
                        nc.tensor.matmul(banks[4 + m][:, 0:(t + 1) * P], q[rows, hh, t * P:t * P + P],
                                         k_[rows, hh, 0:(t + 1) * P], start=True, stop=True).then_inc(sc_done, 1)

                def transposes(k):
                    pe.wait_ge(a_ready, 8 * g + k + 1)
                    if k >= 1:
                        pe.wait_ge(pT_out, base_u + k)
                    elif g:
                        pe.wait_ge(y_ready, 8 + 2 * g)
                    for c in range(k % NT + 1):
                        done = nc.tensor.transpose(T_BANK[:, c * P:c * P + P], dprob[:, 2 * (k % 2), c * P:c * P + P], ident[:])
                    done.then_inc(pT_done, 1)

                def outputs(k):
                    pe.wait_ge(pT_out, base_u + k + 1)
                    if k >= 1:
                        pe.wait_ge(o_out, base_u + k)
                    hh, t, at = k // NT, k % NT, (2 * (g % 2) + k // NT) * P
                    for c in range(t + 1):
                        done = nc.tensor.matmul(O_BANK[:, 0:P], pT2[:, k % 2, c * P:c * P + P], v[:, c, at:at + P],
                                                start=c == 0, stop=c == t)
                    done.then_inc(o_done, 1)

                pe.wait_ge(dn_ready, 4 * g + 4)
                for b in range(4):
                    pe.wait_ge(acc_out[b], TILE_AT["dqk1"] // 4 if g < 2 else TILE_AT["dqk3"] // 4)
                scores(0)
                yield
                for k in range(8):
                    if k < 7:
                        scores(k + 1)
                    if k >= 1:
                        outputs(k - 1)
                    transposes(k)
                    yield
                outputs(7)
                yield

            def head_sums(g, tiles):
                for c in tiles:
                    pe.wait_ge(dsq_ready, 4 * g + c + 1)
                    nc.tensor.matmul(banks[c][:], half_ones[:], dsq[:, c, :], start=True, stop=True).then_inc(dss_done, 1)

            def both(*parts):
                for part in parts:
                    yield from part

            pe.wait_ge(const_ready, 1)
            norm_t("mix", 4, xn0)
            pair_a("xa")
            norm_t("mem", 2, xn0)
            pair_a("ga")
            pe.wait_ge(lruw_in, 64)
            for c in range(4):
                pe.wait_ge(xc_ready, c + 1)
                for m, bd in enumerate((wa_bd, wx_bd)):
                    if c >= 2:
                        pe.wait_ge(lru_ri, 2 * (c - 2) + m + 1)
                    nc.tensor.matmul(banks[4 + 2 * (c % 2) + m][:], bd[:, c, :], xc[:, c, :],
                                     start=True, stop=True).then_inc(lru_mm, 1)
            pair_a("memk", src=(mem_hi, mem_lo), n=MEM)
            s0, t0 = STRIP_AT["memv"], TILE_AT["memv"]
            for k in range(2):
                pe.wait_ge(w_lo_ready, s0 + k + 1)
                for j in range(2):
                    for half in range(2):
                        b = 2 * j + half
                        if k == 0:
                            free_bank(b, t0 // 4)
                        for q in range(4):
                            cols = slice(q * 512 + half * 256, q * 512 + half * 256 + 256)
                            done = three(banks[b][:, 0:256], (w_hi[:, k, cols], w_lo[:, k, cols]),
                                         (mem_hi[:, 4 * k + q, j * P:j * P + P], mem_lo[:, 4 * k + q, j * P:j * P + P]),
                                         False, k == 0 and q == 0, k == 1 and q == 3)
                        if k == 1:
                            done.then_inc(acc_done, 1)
                if k == 0:
                    done.then_inc(open_used, 1)
            pair_a("xq")

            def cross():
                for b in range(4):
                    pe.wait_ge(acc_out[b], TILE_AT["mq"] // 4)
                yield from attend([((xqT[:, h, t * P:t * P + P], mkT[:, h, :]),
                                    [mv_tok[:, c, h * P:h * P + P] for c in range(2)], MEM)
                                   for h in range(4) for t in range(NT)], P, U_X, o_tok1)

            steps = cross()
            side = pacer(steps, *PACE["x"])
            pair_a("mq", side=side)
            pair_a("mk", side=side)
            group_b("mv", side=side)
            finish(steps)

            def moba():
                for b in range(4):
                    pe.wait_ge(acc_out[b], TILE_AT["gate0"] // 4)
                pe.wait_ge(ylo_ready, OT_AT["x"] + 4)
                units = []
                for h, t in MOBA_UNITS:
                    rows = slice(64 * (h % 2), 64 * (h % 2) + 64)
                    units.append(((qT[rows, h // 2, t * P:t * P + P], kT[rows, h // 2, 0:(t + 1) * P]),
                                  [v_tok[:, c, h * 64:h * 64 + 64] for c in range(t + 1)], (t + 1) * P))
                yield from attend(units, 64, U_M, o_tok1)

            steps = moba()
            side = pacer(steps, *PACE["m"])
            for i in range(2):
                pair_a("gate0", i, side=side)
            pe.wait_ge(ya_ready, 4)
            pair_c("branch0", 0, side=side)
            finish(steps)
            loop_a("gate1", 2)
            pe.wait_ge(ylo_ready, OT_AT["m"] + 4)
            pair_c("branch1", 4)
            loop_a("gate2", 2)
            pair_c("branch2", 8)
            pe.wait_ge(mlo_ready, M_AT["one"] + KT)
            with pe.Fori(0, 2) as i:
                group_b("wo", i)
            norm_t("ffn", 4)
            for f in range(2):
                loop_a(f"ffn{f}", 6)
                pe.wait_ge(alo_ready, 12 * (f + 1))
                for half in range(2):
                    group_b(f"down{f}", src=(y_hi, y_lo), strips=3, s_off=3 * half, t_off=4 * half)
            norm_t("norm2", 4)
            pair_a("rqk0")
            group_b("rv0")
            for b in range(4):
                pe.wait_ge(acc_out[b], TILE_AT["rqk1"] // 4)
            steps = ret_attend(0)
            side = pacer(steps, *PACE["r"])
            pair_a("rqk1", side=side)
            group_b("rv1", side=side)
            finish(steps)
            pair_a("rg0", hooks={3: lambda: group_t("r0", o_tok, 4, 4)})
            for b in range(4):
                pe.wait_ge(acc_out[b], TILE_AT["rg0"] // 4)
            steps = ret_attend(1)
            side = pacer(steps, *PACE["r"])
            for i in range(2):
                pair_a("rmg", i, side=side)
            finish(steps)
            pair_a("rg1", hooks={3: lambda: group_t("r1", o_tok, 4, 4)})
            pe.wait_ge(ylo_ready, OT_AT["r1"] + 4)
            with pe.Fori(0, 2) as i:
                pair_a("rwo", i, src=(y_hi, y_lo))
            early = lambda g: {5: lambda: head_sums(g, (0, 1))}
            late = lambda g: {1: lambda: head_sums(g, (2, 3))}
            pair_a("dqk0", hooks=early(0))
            group_b("dv0", hooks=late(0))
            side = steps = None
            for g, beside in enumerate((("dqk1", "dg0"), ("dqk2", "dv1"), ("dqk3", "dg1"))):
                last = [group_side(f"d{g - 1}", do_tok[(g - 1) % 2], 2, 6, 1)] if g else []
                steps = both(*last, diff_attend(g))
                side = pacer(steps, *PACE["d"])
                pair_a(beside[0], side=side, hooks=early(g + 1))
                (group_b if beside[1] == "dv1" else pair_a)(beside[1], side=side, hooks=late(g + 1))
                finish(steps)
            steps = both(group_side("d2", do_tok[0], 2, 6, 1), diff_attend(3))
            side = pacer(steps, *PACE["d3"])
            for i in range(2):
                pair_a("dmg", i, side=side)
            finish(steps)
            group_t("d3", do_tok[1], 2, 6)
            pe.wait_ge(ylo_ready, OT_AT["d3"] + 2)
            with pe.Fori(0, 2) as i:
                pair_a("dwo", i, src=(y_hi, y_lo))
            pe.wait_ge(mlo_ready, M_AT["two"] + KT)
            for half in range(2):
                group_b("wo2", half, b_off=4 * half)

        @block.scalar
        def _(act):
            def split_hi(name, slot, i=0, ahead=2):
                n = STRIP_AT[name] + slot + ahead
                if isinstance(i, int) and n + 2 * i >= STRIPS:
                    return
                act.wait_ge(raw_in[n % 2], i * 16 + 16 * (n // 2 + 1))
                nc.scalar.activation(w_hi[:, n % 2, :], w_raw[:, n % 2, :], ACT.Copy).then_inc(w_hi_ready, 1)

            def tile_done(name, k, i=0):
                act.wait_ge(acc_done, i * 4 + (TILE_AT[name] + k + 1))

            def pair_a(name, post, i=0, side=None, hooks={}):
                for slot in range(2):
                    for c in range(2):
                        if side:
                            side()
                            side()
                        tile_done(name, 2 * slot + c, i)
                        done = post(2 * slot + c, banks[2 * slot + c])
                        if done:
                            done.then_inc(acc_out[2 * slot + c], 1)
                        if 2 * slot + c in hooks:
                            hooks[2 * slot + c]()
                    split_hi(name, slot, i)

            def group_b(name, post=None, i=0, side=None, hooks={}):
                for j in range(NT):
                    if side:
                        side()
                    if j in hooks:
                        hooks[j]()
                act.wait_ge(open_used, i + (OPEN_AT[name] + 1))
                split_hi(name, 0, i)
                for j in range(NT):
                    if side:
                        side()
                    tile_done(name, j, i)
                    if post:
                        post(j, banks[j]).then_inc(acc_out[j], 1)
                split_hi(name, 1, i)

            def norm_stats(name, src, tiles, squares=squares):
                for j in range(tiles):
                    nc.scalar.activation(squares[:, j, :], src[:, j, :], ACT.Square,
                                         accum_out=ssq[:, j:j + 1]).then_inc(ssq_ready, 1)
                act.wait_ge(var_ready, NORMS.index(name) + 1)
                nc.scalar.activation(rstd[:, 0:tiles], ssq[:, 0:tiles], ACT.Sqrt).then_inc(sd_ready, 1)

            def norm_hi(name, gain, hi, n):
                for kt in range(KT):
                    act.wait_ge(hT_done, HT_AT[name] + kt + 1)
                    nc.scalar.activation(hi[:, kt, :], banks[4 + kt % 4][:, 0:n], ACT.Identity,
                                         scale=par_col(gain, kt)).then_inc(hhi_ready, 1)

            def copy_to(dst, scale=1.0):
                return lambda k, bank: nc.scalar.activation(dst(k), bank[:, 0:dst(k).shape[-1]], ACT.Copy, scale=scale)

            def attend(widths, base_u, y_at):
                def transposed(k):
                    act.wait_ge(pT_done, base_u + k + 1)
                    if k >= 2:
                        act.wait_ge(o_done, base_u + k - 1)
                    nc.scalar.activation(pT1[:, k % 2, 0:widths[k]], T_BANK[:, 0:widths[k]], ACT.Copy).then_inc(pT_out, 1)

                yield
                for k, w in enumerate(widths):
                    if k >= 1:
                        transposed(k - 1)
                    act.wait_ge(z_ready, base_u + k + 1)
                    if k >= 2:
                        act.wait_ge(pT_done, base_u + k - 1)
                    nc.scalar.activation(prob[:, k % 2, 0:w], z[:, k % 2, 0:w], ACT.Exp, scale=-1.0,
                                         bias=nmax[:, k % 4:k % 4 + 1],
                                         accum_out=psum_p[:, k % 4:k % 4 + 1]).then_inc(p_ready, 1)
                    yield
                transposed(len(widths) - 1)
                yield
                yield
                for c in range(4):
                    act.wait_ge(oT_done, OT_AT["x" if y_at == 8 else "m"] + c + 1)
                    nc.scalar.activation(y_hi[:, y_at + c, :], banks[4 + c][:], ACT.Copy).then_inc(yhi_ready, 1)

            def ret_attend(g):
                def decays(hh):
                    head = 4 * g + hh
                    if head >= 2:
                        act.wait_ge(st_ready, 4 * (head - 1))
                    nc.scalar.activation(decay[:, hh % 2, :], fwd_dist[:], ACT.Exp,
                                         scale=float(np.log1p(-2.0 ** (-5.0 - head)))).then_inc(dec_ready, 1)

                def output(hh):
                    head = 4 * g + hh
                    act.wait_ge(so_done, head + 1)
                    nc.scalar.activation(o_tok[:, :, hh * P:hh * P + P],
                                         banks[6 + head % 2].rearrange("p (j e) -> p j e", e=P), ACT.Copy).then_inc(so_out, 1)

                decays(0)
                for hh in range(4):
                    for c in range(NT):
                        if c == 2 and hh >= 1:
                            output(hh - 1)
                        if c == 3 and hh < 3:
                            decays(hh + 1)
                        yield
                yield
                yield
                output(3)

            def group_square(key):
                act.wait_ge(so_out, 4 * O_NORM[key] + 4)
                nc.scalar.activation(o_squares, o_tok, ACT.Square).then_inc(osq_ready, 1)

            def group_root(key, n):
                act.wait_ge(ovar_ready, O_NORM[key] + 1)
                nc.scalar.activation(ossq[:, 0:n], ossq[:, 0:n], ACT.Sqrt).then_inc(osd_ready, 1)

            def group_hi(y_from, tiles, g_at, y_at):
                for c in range(tiles):
                    act.wait_ge(y_ready, y_from + c + 1)
                    nc.scalar.activation(y_hi[:, y_at + c, :], gate[:, g_at + c, :], ACT.Copy).then_inc(yhi_ready, 1)

            def diff_attend(g):
                base_u, z0 = U_D + 8 * g, Z_AT["d"] + 16 * g

                def transposed(k):
                    w = (k % NT + 1) * P
                    act.wait_ge(pT_done, base_u + k + 1)
                    if k >= 2:
                        act.wait_ge(o_done, base_u + k - 1)
                    nc.scalar.activation(pT2[:, k % 2, 0:w], T_BANK[:, 0:w], ACT.Copy).then_inc(pT_out, 1)

                def output(k):
                    hh, t = k // NT, k % NT
                    act.wait_ge(o_done, base_u + k + 1)
                    nc.scalar.activation(do_tok[g % 2][:, t, hh * P:hh * P + P], O_BANK[:, 0:P], ACT.Copy)
                    nc.scalar.activation(O_BANK[:, P:2 * P], O_BANK[:, 0:P], ACT.Square,
                                         accum_out=ossq[:, 2 * t + hh:2 * t + hh + 1]).then_inc(o_out, 1)

                yield
                for k in range(10):
                    if 1 <= k <= 8:
                        transposed(k - 1)
                    if k < 8:
                        w = (k % NT + 1) * P
                        for m in range(2):
                            v = 2 * k + m
                            act.wait_ge(z_ready, z0 + v + 1)
                            nc.scalar.activation(dprob[:, v % 4, 0:w], dprob[:, v % 4, 0:w], ACT.Exp, scale=-1.0,
                                                 bias=nmax[:, v % 4:v % 4 + 1],
                                                 accum_out=psum_p[:, v % 4:v % 4 + 1]).then_inc(p_ready, 1)
                    if k >= 2:
                        output(k - 2)
                    yield

            def diff_finish(g):
                group_root(f"d{g}", 8)
                yield
                group_hi(8 + 2 * g, 2, 2 * (g % 2), 2 * g)
                yield

            def both(*parts):
                for part in parts:
                    yield from part

            act.wait_ge(x_in[0], 16)
            norm_stats("mix", x_in_tok, 4, squares0)
            split_hi("xa", 0, ahead=0)
            split_hi("xa", 1, ahead=0)
            act.wait_ge(small_in, 32)
            norm_hi("mix", "mix_g", h_hi, S)
            act.wait_ge(x_in[2], 16)
            norm_stats("mem", mem_tok, 2, squares0)
            act.wait_ge(sp_e, 1)
            nc.scalar.activation(spt[:, 4:8], spt[:, 0:4], ACT.Exp, scale=-1.0).then_inc(sp_e, 1)
            act.wait_ge(lam_s, 1)
            nc.scalar.activation(lam_t[:, 2:4], lam_t[:, 0:2], ACT.Exp).then_inc(lam_e, 1)
            pair_a("xa", copy_to(lambda k: xa_pad[:, k, 3:3 + S]))
            norm_hi("mem", "mem_g", mem_hi, MEM)
            pair_a("ga", lambda k, bank: nc.scalar.activation(ga_gelu[:, k, :], bank[:], ACT.Gelu_apprx_tanh))

            def lru_gates():
                for c in range(4):
                    for m, (dst, b) in enumerate(((lru_r, "b_a"), (lru_i, "b_x"))):
                        act.wait_ge(lru_mm, 2 * c + m + 1)
                        nc.scalar.activation(dst[:, c, :], banks[4 + 2 * (c % 2) + m][:], ACT.Sigmoid,
                                             bias=par_col(b, c)).then_inc(lru_ri, 1)

            def lru_decays():
                act.wait_ge(sp_ready, 1)
                act.wait_ge(xc_ready, 4)
                act.wait_ge(lru_ri, 8)
                for c in range(4):
                    nc.scalar.activation(lru_t[:, c, :], lru_r[:, c, :], ACT.Tanh, scale=sp8[:, c:c + 1]).then_inc(lru_ta, 1)
                act.wait_ge(lru_ta, 4)
                for c in range(4):
                    nc.scalar.activation(lru_r[:, c, :], lru_r[:, c, :], ACT.Exp, scale=nsp8[:, c:c + 1]).then_inc(lru_ta, 1)

            lru_gates()
            for slot, work in enumerate((lru_decays, None)):
                for c in range(2):
                    tile_done("memk", 2 * slot + c)
                    copy_to(lambda k: mkT[:, k, :])(2 * slot + c, banks[2 * slot + c]).then_inc(acc_out[2 * slot + c], 1)
                split_hi("memk", slot)
                if work:
                    work()
            group_b("memv", lambda k, bank: nc.scalar.activation(
                mv_tok[:, k // 2, k % 2 * 256:k % 2 * 256 + 256], bank[:, 0:256], ACT.Copy))
            for c in range(4):
                act.wait_ge(lru_m2, c + 1)
                nc.scalar.activation(lru_t[:, c, :], lru_t[:, c, :], ACT.Sqrt).then_inc(lru_mult, 1)
            pair_a("xq", copy_to(lambda k: xqT[:, k, :], P ** -0.5))
            act.wait_ge(ya_ready, 4)
            steps = attend([MEM] * 16, U_X, 8)
            side = pacer(steps, *PACE["x"])
            pair_a("mq", copy_to(lambda k: qT[:, k, :], 64 ** -0.5), side=side)
            pair_a("mk", copy_to(lambda k: kT[:, k, :]), side=side)
            group_b("mv", copy_to(lambda k: v_tok[:, k, :]), side=side)
            finish(steps)
            steps = attend([(t + 1) * P for h, t in MOBA_UNITS], U_M, 4)
            side = pacer(steps, *PACE["m"])
            act.wait_ge(oT_done, OT_AT["x"] + 4)
            for i in range(2):
                pair_a("gate0", lambda k, bank: nc.scalar.activation(merged[:, 4 * i + k, :], bank[:], ACT.Sigmoid),
                       i, side=side)
            for slot in range(2):
                for c in range(4):
                    side()
                tile_done("branch0", 4 * slot + 3)
                split_hi("branch0", slot)
            finish(steps)
            for n in (1, 2):
                act.wait_ge(m_ready, 8 * n)
                if n == 1:
                    act.wait_ge(o_out, U_D)
                with act.Fori(0, 2) as i:
                    pair_a(f"gate{n}", lambda k, bank: nc.scalar.activation(
                        gT[:, ds(i * 4 + k, 1), :].rearrange("p a s -> p (a s)"), bank[:], ACT.Sigmoid), i)
                for slot in range(2):
                    tile_done(f"branch{n}", 4 * slot + 3)
                    split_hi(f"branch{n}", slot)
            for c in range(KT):
                act.wait_ge(m_ready, 16 + c + 1)
                nc.scalar.activation(h_hi[:, c, :], merged[:, c, :], ACT.Copy).then_inc(mhi_ready, 1)
            with act.Fori(0, 2) as i:
                group_b("wo", None, i)
            act.wait_ge(x1_ready, 8)
            norm_stats("ffn", x_tok, 4)
            norm_hi("ffn", "ffn_g", h_hi, S)
            for f in range(2):
                with act.Fori(0, 6) as i:
                    s0 = STRIP_AT[f"ffn{f}"]
                    for c in range(2):
                        tile_done(f"ffn{f}", c, i)
                        act.wait_ge(conv_ready, i * 2 + (12 * f + 1))
                        nc.scalar.activation(gpad[:, c, 2:2 + S], banks[c][:], ACT.Copy).then_inc(acc_out[c], 1)
                    split_hi(f"ffn{f}", 0, i)
                    for c in range(2):
                        act.wait_ge(conv_ready, i * 2 + (12 * f + c + 2))
                        nc.scalar.activation(gl[:, c, :], cv[:, c, :], ACT.Gelu_apprx_tanh).then_inc(gelu_ready, 1)
                    for c in range(2):
                        act.wait_ge(acc_out[2 + c], i + (TILE_AT[f"ffn{f}"] // 4 + 1))
                        nc.scalar.activation(y_hi[:, ds(i * 2 + c, 1), :].rearrange("p a s -> p (a s)"), pr[:, c, :],
                                             ACT.Copy).then_inc(ahi_ready, 1)
                    split_hi(f"ffn{f}", 1, i)
                name = f"down{f}"
                for half in range(2):
                    for k in range(3):
                        if k < 2:
                            act.wait_ge(open_used, OPEN_AT[name] + 2 * half + k + 1)
                        else:
                            tile_done(name, 4 * half + 3)
                        split_hi(name, 3 * half + k)
            act.wait_ge(x1_ready, 8 + 16)
            norm_stats("final", x_tok, 4)
            act.wait_ge(xb_ready, NT)
            norm_stats("norm2", x_tok, 4)
            norm_hi("norm2", "norm2_g", h_hi, S)
            act.wait_ge(xb_out, 16)

            def ret_qk(g):
                return lambda k, bank: nc.scalar.activation((rqT if k < 2 else rkT)[g][:, k % 2, :], bank[:], ACT.Copy,
                                                            scale=1.0 if k < 2 else 64 ** -0.5)

            def silu(k, bank):
                return nc.scalar.activation(gate[:, k, :], bank[:], ACT.Silu)

            pair_a("rqk0", ret_qk(0))
            group_b("rv0", copy_to(lambda k: rv[0][:, k, :]))
            steps = ret_attend(0)
            side = pacer(steps, *PACE["r"])
            pair_a("rqk1", ret_qk(1), side=side)
            group_b("rv1", copy_to(lambda k: rv[1][:, k, :]), side=side)
            finish(steps)
            group_square("r0")
            group_root("r0", 16)
            pair_a("rg0", silu)
            group_hi(0, 4, 0, 0)
            steps = ret_attend(1)
            side = pacer(steps, *PACE["r"])
            for i in range(2):
                pair_a("rmg", lambda k, bank: nc.scalar.activation(gT[:, 4 * i + k, :], bank[:], ACT.Sigmoid), i, side=side)
            finish(steps)
            group_square("r1")
            group_root("r1", 16)
            act.wait_ge(ylo_ready, OT_AT["r0"] + 4)
            pair_a("rg1", silu)
            group_hi(4, 4, 0, 4)
            for i in range(2):
                for slot in range(2):
                    tile_done("rwo", 4 * i + 2 * slot + 1)
                    split_hi("rwo", slot, i)
            act.wait_ge(mret_out, 16)

            def raw_qk(g):
                def post(k, bank):
                    nc.scalar.activation((dqT if k < 2 else dkT)[g % 2][:, k % 2, :], bank[:], ACT.Copy)
                    if g:
                        act.wait_ge(dn_ready, 4 * (g - 1) + k + 1)
                    nc.scalar.activation(dsq[:, k, :], bank[:], ACT.Square).then_inc(dsq_ready, 1)
                return post

            def roots(g, tiles):
                for c in tiles:
                    act.wait_ge(dss_done, 4 * g + c + 1)
                    nc.scalar.activation(dsq[:, c, :], banks[c][:], ACT.Sqrt, scale=1 / 64 if c >= 2 else 1.0,
                                         bias=stats[:, 41 + c // 2:42 + c // 2]).then_inc(acc_out[c], 1)

            early = lambda g: {2: lambda: roots(g, (0, 1))}
            late = lambda g: {0: lambda: roots(g, (2, 3))}
            late_b = lambda g: {2: lambda: roots(g, (2, 3))}
            pair_a("dqk0", raw_qk(0), hooks=early(0))
            group_b("dv0", copy_to(lambda k: dv[0][:, k, :]), hooks=late_b(0))
            for g, beside in enumerate((("dqk1", "dg0"), ("dqk2", "dv1"), ("dqk3", "dg1"))):
                steps = both(*([diff_finish(g - 1)] if g else []), diff_attend(g))
                side = pacer(steps, *PACE["d"])
                pair_a(beside[0], raw_qk(g + 1), side=side, hooks=early(g + 1))
                if beside[1] == "dv1":
                    group_b("dv1", copy_to(lambda k: dv[1][:, k, :]), side=side, hooks=late_b(g + 1))
                else:
                    if g == 2:
                        act.wait_ge(ylo_ready, OT_AT["d1"] + 2)
                    pair_a(beside[1], silu, side=side, hooks=late(g + 1))
                finish(steps)
            steps = both(diff_finish(2), diff_attend(3))
            side = pacer(steps, *PACE["d3"])
            for i in range(2):
                pair_a("dmg", lambda k, bank: nc.scalar.activation(gT[:, 4 * i + k, :], bank[:], ACT.Sigmoid), i, side=side)
            finish(steps)
            finish(diff_finish(3))
            for i in range(2):
                for slot in range(2):
                    for c in range(2):
                        k = 4 * i + 2 * slot + c
                        act.wait_ge(m_ready, 24 + k + 1)
                        nc.scalar.activation(h_hi[:, k, :], gT[:, k, :], ACT.Copy).then_inc(mhi_ready, 1)
                    split_hi("dwo", slot, i)
            for i in range(2):
                group_b("wo2", None, i)

        @block.vector
        def _(dve):
            then = dve.drain

            def split_lo(name, slot, i=0, ahead=2):
                n = STRIP_AT[name] + slot + ahead
                if isinstance(i, int) and n + 2 * i >= STRIPS:
                    return
                dve.wait_ge(w_hi_ready, i * 2 + (n + 1))
                nc.vector.tensor_tensor(w_lo[:, n % 2, :], w_raw[:, n % 2, :], w_hi[:, n % 2, :].bitcast(fp32),
                                        ALU.subtract).then_inc(w_lo_ready, 1)

            def both_lo(name, i=0, side=None, hooks={}):
                for slot in range(2):
                    for k in range(4):
                        if side:
                            side()
                        if 4 * slot + k in hooks:
                            hooks[4 * slot + k]()
                    split_lo(name, slot, i)

            def norm_scale(name, tiles, apply):
                k = NORMS.index(name)
                dve.wait_ge(ssq_ready, SSQ_AT[name] + tiles)
                nc.vector.tensor_scalar(ssq[:, 0:tiles], ssq[:, 0:tiles], 1.0 / D, EPS, ALU.mult, ALU.add).then_inc(var_ready, 1)
                dve.wait_ge(sd_ready, k + 1)
                nc.vector.reciprocal(rstd[:, 0:tiles], rstd[:, 0:tiles])
                then()
                for j in range(tiles):
                    apply(j)

            def normed(src, xn=xn):
                return lambda j: nc.vector.tensor_scalar(xn[:, j, :], src[:, j, :], rstd[:, j:j + 1], None,
                                                         ALU.mult).then_inc(xn_ready, 1)

            def norm_lo(name, gain, hi, lo, n):
                for kt in range(KT):
                    dve.wait_ge(hhi_ready, HT_AT[name] + kt + 1)
                    nc.vector.scalar_tensor_tensor(lo[:, kt, :], banks[4 + kt % 4][:, 0:n], par_col(gain, kt),
                                                   hi[:, kt, :].bitcast(fp32), ALU.mult, ALU.subtract).then_inc(hlo_ready, 1)

            def with_bias(bank, bias_cols, dst, col):
                return nc.vector.tensor_tensor_reduce(out=dst, in0=bank, in1=bias_cols, scale=-1.0, scalar=3e38,
                                                      op0=ALU.add, op1=ALU.min, accum_out=nmax[:, col:col + 1])

            def attend(units, key, base_u, y_at):
                def output(k):
                    dst = units[k][3]
                    dve.wait_ge(o_done, base_u + k + 1)
                    nc.vector.reciprocal(rsum[:, k % 4:k % 4 + 1], psum_p[:, k % 4:k % 4 + 1])
                    then()
                    nc.vector.tensor_scalar(dst, O_BANK[:, 0:dst.shape[-1]], rsum[:, k % 4:k % 4 + 1], None,
                                            ALU.mult).then_inc(o_out, 1)

                yield
                for k, (w, cols, number, _) in enumerate(units):
                    dve.wait_ge(sc_done, SC_AT[key] + k + 1)
                    dve.wait_ge(bias_ready, number)
                    if k >= 2:
                        dve.wait_ge(p_ready, base_u + k - 1)
                    with_bias(banks[4 + k % 2][:, 0:w], cols, z[:, k % 2, 0:w], k % 4).then_inc(z_ready, 1)
                    if k >= 2:
                        output(k - 2)
                    yield
                output(len(units) - 2)
                yield
                output(len(units) - 1)
                yield
                for c in range(4):
                    dve.wait_ge(yhi_ready, OT_AT[key] + c + 1)
                    nc.vector.tensor_tensor(y_lo[:, y_at + c, :], banks[4 + c][:], y_hi[:, y_at + c, :].bitcast(fp32),
                                            ALU.subtract).then_inc(ylo_ready, 1)

            def ret_attend(g):
                yield
                for hh in range(4):
                    head = 4 * g + hh
                    dve.wait_ge(dec_ready, head + 1)
                    if head >= 2:
                        dve.wait_ge(so_done, head - 1)
                    for c in range(NT):
                        r = 4 * head + c
                        dve.wait_ge(sc_done, SC_AT["r"] + r + 1)
                        n = S - c * P
                        nc.vector.tensor_tensor(st[:, hh % 2, ST_AT[c]:ST_AT[c] + n], banks[4 + r % 2][:, 0:n],
                                                decay[:, hh % 2, 0:n], ALU.mult).then_inc(st_ready, 1)
                        yield

            def group_scale(key, tokens, groups, const):
                n, sums, roots = O_NORM[key], ossq[:, 0:groups], orstd[:, 0:groups]
                nc.vector.tensor_scalar(sums, sums, 1.0 / P, EPS, ALU.mult, ALU.add).then_inc(ovar_ready, 1)
                dve.wait_ge(osd_ready, n + 1)
                nc.vector.reciprocal(roots, sums)
                then()
                if const != 1.0:
                    nc.vector.tensor_scalar(roots, roots, const, None, ALU.mult)
                    then()
                o3 = tokens.rearrange("p j (h e) -> p (j h) e", e=P)
                nc.vector.tensor_tensor(o3, o3, roots.rearrange("p (a b) -> p a b", b=1).to_broadcast([P, groups, P]),
                                        ALU.mult).then_inc(on_ready, 1)

            def group_sum(key):
                dve.wait_ge(osq_ready, O_NORM[key] + 1)
                nc.vector.tensor_reduce(ossq, o_squares.rearrange("p j (h e) -> p (j h) e", e=P), AX.X, ALU.add)
                then()

            def group_gate(key, gains, gain_at, tiles, b0, g_at, y_at):
                for c in range(tiles):
                    dve.wait_ge(oT_done, OT_AT[key] + c + 1)
                    nc.vector.scalar_tensor_tensor(gate[:, g_at + c, :], banks[b0 + c][:], par_col(gains, gain_at + c),
                                                   gate[:, g_at + c, :], ALU.mult, ALU.mult).then_inc(y_ready, 1)
                for c in range(tiles):
                    dve.wait_ge(yhi_ready, OT_AT[key] + c + 1)
                    nc.vector.tensor_tensor(y_lo[:, y_at + c, :], gate[:, g_at + c, :], y_hi[:, y_at + c, :].bitcast(fp32),
                                            ALU.subtract).then_inc(ylo_ready, 1)

            def diff_attend(g):
                def mix(k):
                    w = (k % NT + 1) * P
                    a = 2 * (k % 2)
                    dve.wait_ge(p_ready, Z_AT["d"] + 16 * g + 2 * k + 2)
                    nc.vector.reciprocal(rsum[:, a:a + 2], psum_p[:, a:a + 2])
                    then()
                    nc.vector.tensor_tensor(rsl[:, k % 2:k % 2 + 1], rsum[:, a + 1:a + 2], lam_col, ALU.mult)
                    then()
                    nc.vector.tensor_scalar(dprob[:, a + 1, 0:w], dprob[:, a + 1, 0:w], rsl[:, k % 2:k % 2 + 1], None, ALU.mult)
                    then()
                    nc.vector.scalar_tensor_tensor(dprob[:, a, 0:w], dprob[:, a, 0:w], rsum[:, a:a + 1],
                                                   dprob[:, a + 1, 0:w], ALU.mult, ALU.add).then_inc(a_ready, 1)

                yield
                for k in range(8):
                    hh, t = k // NT, k % NT
                    dve.wait_ge(bias_ready, 9 + 2 * g + hh + 1)
                    for m in range(2):
                        v = 2 * k + m
                        dve.wait_ge(sc_done, SC_AT["d"] + 16 * g + v + 1)
                        if k >= 2:
                            dve.wait_ge(pT_done, U_D + 8 * g + k - 1)
                        with_bias(banks[4 + m][:, 0:(t + 1) * P], bias2[:, hh % 2, (3 - t) * P:S],
                                  dprob[:, v % 4, 0:(t + 1) * P], v % 4).then_inc(z_ready, 1)
                    mix(k)
                    yield
                yield
                yield

            def diff_finish(g):
                dve.wait_ge(o_out, U_D + 8 * g + 8)
                group_scale(f"d{g}", do_tok[g % 2], 8, 1.0 - LAM_INIT)
                yield
                group_gate(f"d{g}", "sub_g", 2 * g, 2, 6, 2 * (g % 2), 2 * g)
                yield

            def both(*parts):
                for part in parts:
                    yield from part

            dve.wait_ge(x_in[0], 16)
            norm_scale("mix", 4, normed(x_in_tok, xn0))
            split_lo("xa", 0, ahead=0)
            split_lo("xa", 1, ahead=0)
            dve.wait_ge(small_in, 32)
            norm_lo("mix", "mix_g", h_hi, h_lo, S)
            dve.wait_ge(x_in[2], 16)
            norm_scale("mem", 2, normed(mem_tok, xn0))
            lam4 = params[:, COLS["lam"]:COLS["lam"] + 4]
            neg, e, zz, z2, acc = (spt[:, 0:4], spt[:, 4:8], spt[:, 8:12], spt[:, 12:16], spt[:, 16:20])
            nc.vector.tensor_scalar(neg, lam4, -1.0, None, ALU.mult)
            then()
            nc.vector.tensor_tensor(neg, neg, lam4, ALU.max).then_inc(sp_e, 1)
            lprod = lqk[:, 0:2, :]
            nc.vector.tensor_tensor(lprod, lprod, lqk[:, 2:4, :], ALU.mult)
            then()
            nc.vector.tensor_reduce(lam_t[:, 0:2], lprod, AX.X, ALU.add).then_inc(lam_s, 1)
            nc.vector.memset(stats[:, 41:42], 64 * EPS)
            nc.vector.memset(stats[:, 42:43], EPS)
            nc.vector.memset(xa_pad[:, :, 0:3], 0.0)
            dve.wait_ge(sp_e, 2)
            nc.vector.tensor_scalar(acc, e, 2.0, None, ALU.add)
            then()
            nc.vector.reciprocal(acc, acc)
            then()
            nc.vector.tensor_tensor(zz, e, acc, ALU.mult)
            then()
            nc.vector.tensor_tensor(z2, zz, zz, ALU.mult)
            then()
            nc.vector.tensor_scalar(acc, z2, 1.0 / 15, None, ALU.mult)
            for k in (13, 11, 9, 7, 5, 3):
                then()
                nc.vector.scalar_tensor_tensor(acc, acc, 1.0 / k, z2, ALU.add, ALU.mult)
            then()
            nc.vector.scalar_tensor_tensor(acc, acc, 1.0, zz, ALU.add, ALU.mult)
            nc.vector.tensor_scalar(neg, lam4, -1.0, 0.0, ALU.mult, ALU.max)
            then()
            nc.vector.scalar_tensor_tensor(acc, acc, 2.0, neg, ALU.mult, ALU.add)
            then()
            nc.vector.tensor_scalar(sp8, acc, 8.0, None, ALU.mult)
            nc.vector.tensor_scalar(nsp8, acc, -8.0, None, ALU.mult).then_inc(sp_ready, 1)
            dve.wait_ge(lam_e, 1)
            nc.vector.tensor_tensor(lam_col, lam_t[:, 3:4], lam_t[:, 2:3], ALU.subtract)
            then()
            nc.vector.tensor_scalar(lam_col, lam_col, -LAM_INIT, None, ALU.add)
            then()
            for slot in range(2):
                for c in (2 * slot, 2 * slot + 1):
                    dve.wait_ge(acc_out[c], 1)
                    w = lambda k: par_col("lconv_w", 4 * c + k)
                    nc.vector.tensor_scalar(xc[:, c, :], xa_pad[:, c, 3:3 + S], w(3), par_col("lconv_b", c), ALU.mult, ALU.add)
                    for k in (2, 1, 0):
                        then()
                        done = nc.vector.scalar_tensor_tensor(xc[:, c, :], xa_pad[:, c, k:k + S], w(k), xc[:, c, :],
                                                              ALU.mult, ALU.add)
                    done.then_inc(xc_ready, 1)
                split_lo("xa", slot)
            norm_lo("mem", "mem_g", mem_hi, mem_lo, MEM)
            both_lo("ga")
            split_lo("memk", 0)
            split_lo("memk", 1)
            for c in range(4):
                dve.wait_ge(lru_ta, 4)
                s = c % 2
                nc.vector.tensor_scalar(lru_tmp[:, s, :], lru_t[:, c, :], 1.0, None, ALU.add)
                then()
                nc.vector.reciprocal(lru_tmp[:, s, :], lru_tmp[:, s, :])
                then()
                nc.vector.scalar_tensor_tensor(lru_t[:, c, :], lru_t[:, c, :], 2.0, lru_tmp[:, s, :],
                                               ALU.mult, ALU.mult).then_inc(lru_m2, 1)
            both_lo("memv")
            both_lo("xq")
            dve.wait_ge(lru_ta, 8)
            for c in range(4):
                dve.wait_ge(lru_mult, c + 1)
                nc.vector.tensor_tensor(lru_i[:, c, :], lru_i[:, c, :], lru_t[:, c, :], ALU.mult)
                then()
                nc.vector.tensor_tensor(lru_i[:, c, :], lru_i[:, c, :], xc[:, c, :], ALU.mult)
                then()
                nc.vector.tensor_tensor_scan(xc[:, c, :], lru_r[:, c, :], lru_i[:, c, :], 0.0, ALU.mult, ALU.add)
                then()
                dve.wait_ge(acc_out[c], 2)
                nc.vector.tensor_tensor(xc[:, c, :], xc[:, c, :], ga_gelu[:, c, :], ALU.mult)
                then()
                nc.vector.tensor_copy(y_hi[:, c, :], xc[:, c, :])
                then()
                nc.vector.tensor_tensor(y_lo[:, c, :], xc[:, c, :], y_hi[:, c, :].bitcast(fp32),
                                        ALU.subtract).then_inc(ya_ready, 1)
            steps = attend([(MEM, bias1[:, k // NT % 2, 0:MEM], 1, o_tok1[:, k % NT, k // NT * P:k // NT * P + P])
                            for k in range(16)], "x", U_X, 8)
            side = pacer(steps, *PACE["x"])
            both_lo("mq", side=side)
            both_lo("mk", side=side)
            both_lo("mv", side=side)
            finish(steps)
            steps = attend([((t + 1) * P, bias1[:, h % 2, (3 - t) * P:S], h + 2, o_tok1[:, t, h * 64:h * 64 + 64])
                            for h, t in MOBA_UNITS], "m", U_M, 4)
            side = pacer(steps, *PACE["m"])
            for i in range(2):
                both_lo("gate0", i, side=side)
            for slot in range(2):
                for c in range(4):
                    k = 4 * slot + c
                    side()
                    dve.wait_ge(acc_done, TILE_AT["branch0"] + k + 1)
                    dve.wait_ge(acc_out[c], TILE_AT["gate0"] // 4 + slot + 1)
                    nc.vector.tensor_tensor(merged[:, k, :], banks[c][:], merged[:, k, :], ALU.mult).then_inc(acc_out[c], 1)
                split_lo("branch0", slot)
            then()
            nc.vector.engine_nop().then_inc(m_ready, 8)
            finish(steps)
            for n in (1, 2):
                with dve.Fori(0, 2) as i:
                    both_lo(f"gate{n}", i)
                t0 = TILE_AT[f"branch{n}"]
                for slot in range(2):
                    for c in range(4):
                        k = 4 * slot + c
                        dve.wait_ge(acc_done, t0 + k + 1)
                        dve.wait_ge(acc_out[k % 4], TILE_AT[f"gate{n}"] // 4 + k // 4 + 1)
                        nc.vector.tensor_tensor(mtmp[:, c, :], banks[c][:], gT[:, k, :], ALU.mult).then_inc(acc_out[c], 1)
                        dve.wait_ge(acc_out[c], t0 // 4 + slot + 1)
                        nc.vector.tensor_tensor(merged[:, k, :], merged[:, k, :], mtmp[:, c, :], ALU.add).then_inc(m_ready, 1)
                    split_lo(f"branch{n}", slot)
            for c in range(KT):
                dve.wait_ge(mhi_ready, c + 1)
                nc.vector.tensor_tensor(h_lo[:, c, :], merged[:, c, :], h_hi[:, c, :].bitcast(fp32),
                                        ALU.subtract).then_inc(mlo_ready, 1)
            dve.wait_ge(x_in[1], 16)
            def add_residual(name, t_off, half):
                for j in range(NT):
                    dve.wait_ge(acc_done, TILE_AT[name] + t_off + j + 1)
                    xs = x_tok[:, j, half * S:half * S + S]
                    nc.vector.tensor_tensor(xs, xs, banks[j][:], ALU.add).then_inc(acc_out[j], 1)

            for half in range(2):
                split_lo("wo", 0, half)
                add_residual("wo", 4 * half, half)
                split_lo("wo", 1, half)
            then()
            nc.vector.engine_nop().then_inc(x1_ready, 8)
            norm_scale("ffn", 4, normed(x_tok))
            norm_lo("ffn", "ffn_g", h_hi, h_lo, S)
            nc.vector.memset(gpad[:, :, 0:2], 0.0).then_inc(conv_ready, 1)
            for f in range(2):
                t0 = TILE_AT[f"ffn{f}"]
                with dve.Fori(0, 6) as i:
                    for c in range(2):
                        dve.wait_ge(acc_out[c], i + (t0 // 4 + 1))
                        col = lambda name, k: params[:, ds(i * 2 * k[1] + (COLS[name] + (12 * f + c) * k[1] + k[0]), 1)]
                        nc.vector.tensor_scalar(cv[:, c, :], gpad[:, c, 2:2 + S], col("fconv_w", (2, 3)), col("fconv_b", (0, 1)),
                                                ALU.mult, ALU.add)
                        then()
                        nc.vector.scalar_tensor_tensor(cv[:, c, :], gpad[:, c, 1:1 + S], col("fconv_w", (1, 3)), cv[:, c, :],
                                                       ALU.mult, ALU.add)
                        then()
                        nc.vector.scalar_tensor_tensor(cv[:, c, :], gpad[:, c, 0:S], col("fconv_w", (0, 3)), cv[:, c, :],
                                                       ALU.mult, ALU.add).then_inc(conv_ready, 1)
                    split_lo(f"ffn{f}", 0, i)
                    for c in range(2):
                        dve.wait_ge(gelu_ready, i * 2 + (12 * f + c + 1))
                        dve.wait_ge(acc_done, i * 4 + (t0 + 2 + c + 1))
                        nc.vector.tensor_tensor(pr[:, c, :], gl[:, c, :], banks[2 + c][:], ALU.mult).then_inc(acc_out[2 + c], 1)
                    for c in range(2):
                        dve.wait_ge(ahi_ready, i * 2 + (12 * f + c + 1))
                        nc.vector.tensor_tensor(y_lo[:, ds(i * 2 + c, 1), :].rearrange("p a s -> p (a s)"), pr[:, c, :],
                                                y_hi[:, ds(i * 2 + c, 1), :].rearrange("p a s -> p (a s)").bitcast(fp32),
                                                ALU.subtract).then_inc(alo_ready, 1)
                    split_lo(f"ffn{f}", 1, i)
                name = f"down{f}"
                for half in range(2):
                    for k in range(2):
                        split_lo(name, 3 * half + k)
                    add_residual(name, 4 * half, half)
                    split_lo(name, 3 * half + 2)
                then()
                nc.vector.engine_nop().then_inc(x1_ready, 8)
            dve.wait_ge(x_in[3], 16)
            norm_scale("final", 4, lambda j: nc.vector.scalar_tensor_tensor(
                x_tok[:, j, :], x_tok[:, j, :], rstd[:, j:j + 1], gain_row, ALU.mult, ALU.mult).then_inc(xb_ready, 1))
            then()
            norm_scale("norm2", 4, normed(x_tok))
            norm_lo("norm2", "norm2_g", h_hi, h_lo, S)
            both_lo("rqk0")
            both_lo("rv0")
            steps = ret_attend(0)
            side = pacer(steps, *PACE["r"])
            both_lo("rqk1", side=side)
            both_lo("rv1", side=side)
            finish(steps)
            group_sum("r0")
            group_scale("r0", o_tok, 16, 1.0)
            both_lo("rg0")
            for c in range(4):
                dve.wait_ge(acc_out[c], TILE_AT["rg0"] // 4 + 1)
            group_gate("r0", "ret_g", 0, 4, 4, 0, 0)
            steps = ret_attend(1)
            side = pacer(steps, *PACE["r"])
            for i in range(2):
                both_lo("rmg", i, side=side)
            finish(steps)
            group_sum("r1")
            group_scale("r1", o_tok, 16, 1.0)
            both_lo("rg1")
            for c in range(4):
                dve.wait_ge(acc_out[c], TILE_AT["rg1"] // 4 + 1)
            group_gate("r1", "ret_g", 4, 4, 4, 0, 4)

            def gate_tile(name, k):
                return TILE_AT[name] // 4 + k // 4 + 1
            for i in range(2):
                for slot in range(2):
                    for c in range(2):
                        b = 2 * slot + c
                        k = 4 * i + b
                        dve.wait_ge(acc_done, TILE_AT["rwo"] + k + 1)
                        dve.wait_ge(acc_out[b], gate_tile("rmg", k))
                        nc.vector.tensor_tensor(gT[:, k, :], banks[b][:], gT[:, k, :], ALU.mult).then_inc(acc_out[b], 1)
                    split_lo("rwo", slot, i)
            then()
            nc.vector.engine_nop().then_inc(mret_ready, 8)
            def unit_norms(g, tiles):
                for c in tiles:
                    t0 = TILE_AT[f"dqk{g}"] // 4
                    dve.wait_ge(acc_out[c], t0 + 1)
                    v = (dqT if c < 2 else dkT)[g % 2][:, c % 2, :]
                    nc.vector.reciprocal(dsq[:, c, :], dsq[:, c, :])
                    then()
                    nc.vector.scalar_tensor_tensor(v, v, par_col("dq_g" if c < 2 else "dk_g"), dsq[:, c, :],
                                                   ALU.mult, ALU.mult).then_inc(dn_ready, 1)

            early = lambda g: {7: lambda: unit_norms(g, (0, 1))}
            late = lambda g: {3: lambda: unit_norms(g, (2, 3))}
            both_lo("dqk0", hooks=early(0))
            both_lo("dv0", hooks=late(0))
            for g, beside in enumerate((("dqk1", "dg0"), ("dqk2", "dv1"), ("dqk3", "dg1"))):
                steps = both(*([diff_finish(g - 1)] if g else []), diff_attend(g))
                side = pacer(steps, *PACE["d"])
                both_lo(beside[0], side=side, hooks=early(g + 1))
                both_lo(beside[1], side=side, hooks=late(g + 1))
                finish(steps)
            steps = both(diff_finish(2), diff_attend(3))
            side = pacer(steps, *PACE["d3"])
            for i in range(2):
                both_lo("dmg", i, side=side)
            finish(steps)
            finish(diff_finish(3))
            dve.wait_ge(x_in[5], 16)
            for i in range(2):
                for slot in range(2):
                    for c in range(2):
                        b = 2 * slot + c
                        k = 4 * i + b
                        dve.wait_ge(acc_done, TILE_AT["dwo"] + k + 1)
                        dve.wait_ge(acc_out[b], gate_tile("dmg", k))
                        nc.vector.tensor_tensor(gT[:, k, :], banks[b][:], gT[:, k, :], ALU.mult).then_inc(acc_out[b], 1)
                        dve.wait_ge(acc_out[b], gate_tile("dwo", k))
                        nc.vector.tensor_tensor(gT[:, k, :], gT[:, k, :], m_back[:, k, :], ALU.add).then_inc(m_ready, 1)
                        dve.wait_ge(mhi_ready, M_AT["two"] + k + 1)
                        nc.vector.tensor_tensor(h_lo[:, k, :], gT[:, k, :], h_hi[:, k, :].bitcast(fp32),
                                                ALU.subtract).then_inc(mlo_ready, 1)
                    split_lo("dwo", slot, i)
            dve.wait_ge(x_in[4], 16)
            for half in range(2):
                split_lo("wo2", 0, half)
                for j in range(NT):
                    dve.wait_ge(acc_done, TILE_AT["wo2"] + 4 * half + j + 1)
                    cols = slice(half * S, half * S + S)
                    nc.vector.tensor_tensor(res[:, j, cols], xb[:, j, cols], banks[4 * half + j][:], ALU.add).then_inc(res_ready, 1)
                split_lo("wo2", 1, half)


_INPUTS = ("x", "mem", "par", "lru_w", "lqk", "final_g", "wstream")


def _laid_out(v):
    a = {k: np.asarray(t) for k, t in v.items()}

    def cols(t, n):
        return t.reshape(n, P).T

    def strip_a(w, c0):
        return w[:, c0:c0 + 256].reshape(KT, P, 256).transpose(1, 0, 2).reshape(P, STRIP)

    def strip_b(w, r0, c0):
        return w[r0:r0 + 512, c0:c0 + 512].reshape(4, P, 512).transpose(1, 0, 2).reshape(P, STRIP)

    w1, w2, kv = a["w_in"][0], a["w_in_2"][0], a["w_mem_kv"][0]
    strips = []

    def take_a(w, c0, n):
        strips.extend(strip_a(w, c0 + 256 * i) for i in range(n))

    def take_b(w, c0, halves, r0=0, k=2):
        strips.extend(strip_b(w, r0 + 512 * i, c0 + 512 * h) for h in range(halves) for i in range(k))

    for c0 in (0, 512):
        take_a(w1, c0, 2)
    take_a(kv, 0, 2)
    take_b(kv, 512, 1)
    take_a(w1, 2560, 2)
    take_a(w1, 1024, 2)
    take_a(w1, 1536, 2)
    take_b(w1, 2048, 1)
    for n in range(3):
        take_a(w1, 3072 + D * n, 4)
        take_b(a["w_branch"][0, n], 0, 2, k=1)
    take_b(a["w_out"][0], 0, 2)
    wg, wu, wd = a["w_ffn_gate"][0], a["w_ffn_up"][0], a["w_ffn_down"][0]
    for f in range(2):
        for i in range(6):
            take_a(wg, (6 * f + i) * 256, 1)
            take_a(wu, (6 * f + i) * 256, 1)
        take_b(wd, 0, 2, r0=f * FF // 2, k=3)
    for g in range(2):
        take_a(w2, 256 * g, 1)
        take_a(w2, 512 + 256 * g, 1)
        take_b(w2, 1024 + 512 * g, 1)
    take_a(w2, 2048, 2)
    take_a(w2, 7168, 4)
    take_a(w2, 2560, 2)
    take_a(a["ret_w_o_2"][0], 0, 4)
    for g in range(4):
        take_a(w2, 3072 + 256 * g, 1)
        take_a(w2, 4096 + 256 * g, 1)
        if g % 2 == 0:
            take_b(w2, 5120 + 256 * g, 1)
        else:
            take_a(w2, 6144 + 256 * (g - 1), 2)
    take_a(w2, 8192, 4)
    take_a(a["diff_w_o_2"][0], 0, 4)
    take_b(a["w_out_2"][0], 0, 2)
    assert len(strips) == STRIPS

    twice = lambda t: np.concatenate([t, t]).reshape(P, 1)
    small = np.concatenate([
        cols(a["mix_norm_gain"][0], 8), cols(a["mem_norm_gain"][0], 8), cols(a["ffn_norm_gain"][0], 8),
        cols(a["norm_g_2"][0], 8),
        a["lru_conv_w"][0].reshape(4, 4, P).transpose(2, 1, 0).reshape(P, 16), cols(a["lru_conv_b"][0], 4),
        cols(a["lru_b_a"][0].reshape(-1), 4), cols(a["lru_b_x"][0].reshape(-1), 4), cols(a["lru_lambda"][0], 4),
        a["ffn_conv_w"][0].reshape(3, FFT, P).transpose(2, 1, 0).reshape(P, 3 * FFT), cols(a["ffn_conv_b"][0], FFT),
        cols(a["ret_norm_g_2"][0], 8), twice(a["diff_q_norm_g_2"][0]), twice(a["diff_k_norm_g_2"][0]),
        cols(a["diff_sub_norm_g_2"][0], 8)], axis=1)
    lru = np.stack([a[k][0].reshape(4, P, 64).transpose(1, 0, 2) for k in ("lru_w_a", "lru_w_x")], axis=1)
    lq = np.stack([a[f"diff_{k}_2"][0] for k in ("lq1", "lq2", "lk1", "lk2")])
    return {
        "x": a["x"][0], "mem": a["mem"][0], "par": small, "lru_w": lru,
        "lqk": np.broadcast_to(lq, (P, 4, 64)), "final_g": np.broadcast_to(a["final_norm_gain"], (P, D)),
        "wstream": np.concatenate(strips, axis=0),
    }


def kernel(**inputs):
    import concourse.bacc as _bacc
    from concourse.bass_utils import run_bass_kernel_spmd as _run

    nc = _bacc.Bacc("TRN2", target_bir_lowering=False, num_devices=1)
    laid = _laid_out(inputs)
    arrays, args = {}, []
    for name in _INPUTS:
        arr = np.ascontiguousarray(laid[name])
        arrays[f"in_{name}"] = arr
        args.append(nc.dram_tensor(f"in_{name}", arr.shape, mybir.dt.from_np(arr.dtype), kind="ExternalInput").ap())
    out = nc.dram_tensor("out_dram", (S, D), mybir.dt.float32, kind="ExternalOutput").ap()
    xb = nc.dram_tensor("xb_dram", (S, D), mybir.dt.float32, kind="Internal").ap()
    mret = nc.dram_tensor("mret_dram", (P, KT * S), mybir.dt.float32, kind="Internal").ap()
    hybrid_block_kernel(nc, *args, out, xb, mret)
    r = _run(nc, [arrays], core_ids=[0])
    return r.results[0]["out_dram"].reshape(1, S, D)
```

```python
from contextlib import ExitStack

import numpy as np
import concourse.bass as bass
from concourse import mybir

P = 128
D = 1024
KT = D // P
S = 512
NT = S // P
MEM = 256
STRIP = 2048
FF = 3072
FFT = FF // P
EPS = 1e-6
MASKED = -1e30
FAR = 1e6
LAM_INIT = 0.2

PHASES = [("xa", 2), ("ga", 2), ("memk", 2), ("memv", 2), ("xq", 2), ("mq", 2), ("mk", 2), ("mv", 2)]
for _n in range(3):
    PHASES += [(f"gate{_n}", 4), (f"branch{_n}", 2)]
PHASES += [("wo", 4)]
for _f in range(2):
    PHASES += [(f"ffn{_f}", 12), (f"down{_f}", 6)]
PHASES += [("rqk0", 2), ("rv0", 2), ("rqk1", 2), ("rv1", 2), ("rg0", 2), ("rmg", 4), ("rg1", 2), ("rwo", 4)]
PHASES += [("dqk0", 2), ("dv0", 2), ("dqk1", 2), ("dg0", 2), ("dqk2", 2), ("dv1", 2), ("dqk3", 2), ("dg1", 2)]
PHASES += [("dmg", 4), ("dwo", 4), ("wo2", 4)]

STRIP_AT, TILE_AT, OPEN_AT = {}, {}, {}
_s = _t = _u = 0
for _name, _k in PHASES:
    STRIP_AT[_name], TILE_AT[_name], OPEN_AT[_name] = _s, _t, _u
    _s += _k
    _t += 8 if _name.startswith(("down", "branch")) else 4 if _name == "memv" else 2 * _k
    if _name.startswith("down"):
        _u += 4
    elif _name in ("mv", "memv", "wo", "wo2", "rv0", "rv1", "dv0", "dv1"):
        _u += _k // 2
STRIPS = _s

COLS = {}
_c = 0
for _name, _k in [("mix_g", 8), ("mem_g", 8), ("ffn_g", 8), ("norm2_g", 8), ("lconv_w", 16), ("lconv_b", 4),
                  ("b_a", 4), ("b_x", 4), ("lam", 4), ("fconv_w", 72), ("fconv_b", 24), ("ret_g", 8),
                  ("dq_g", 1), ("dk_g", 1), ("sub_g", 8)]:
    COLS[_name] = _c
    _c += _k
NPAR = _c
POOL_MOBA = range(STRIP_AT["mk"] + 2, STRIP_AT["gate1"] + 2)
POOL_DIFF = range(STRIP_AT["dqk0"] + 2, STRIP_AT["dwo"] + 2)
POOL_STRIPS = {*POOL_MOBA, *POOL_DIFF}


def pacer(steps, num, den):
    at = [0]

    def slot():
        at[0] += 1
        for _ in range(at[0] * num // den - (at[0] - 1) * num // den):
            next(steps, None)
    return slot


def lead(slots):
    for _ in range(slots):
        yield


def finish(steps):
    for _ in steps:
        pass


def hybrid_block_kernel(nc, x, mem, par, lru_w, lqk_in, final_g, wstream, out, xb_dram, mret_dram):
    fp32, fp32r = mybir.dt.float32, mybir.dt.float32r
    ALU, ACT, AX = mybir.AluOpType, mybir.ActivationFunctionType, mybir.AxisListType
    ds = bass.ds

    ctx = ExitStack()
    with ctx:
        def sb(name, shape, dt=fp32):
            return ctx.enter_context(nc.sbuf_tensor(name, shape, dt))

        def sem(name):
            return ctx.enter_context(nc.semaphore(name))

        w_raw = sb("w_raw", [P, 2, STRIP])
        w_hi = sb("w_hi", [P, 2, STRIP], fp32r)
        w_lo = sb("w_lo", [P, 2, STRIP], fp32r)
        h_hi = sb("h_hi", [P, KT, S], fp32r)
        h_lo = sb("h_lo", [P, KT, S], fp32r)
        y_hi = sb("y_hi", [P, 12, S], fp32r)
        y_lo = sb("y_lo", [P, 12, S], fp32r)
        params = sb("params", [P, NPAR])
        lqk = sb("lqk", [P, 4, 64])
        ident = sb("ident", [P, P])
        half_ones = sb("half_ones", [P, P])
        neg_dist = sb("neg_dist", [P, S])
        fwd_dist = sb("fwd_dist", [P, S])
        stats = sb("stats", [P, 192])
        arena = sb("arena", [P, 18496])
        banks = [ctx.enter_context(nc.psum_tensor(f"bank{i}", [P, 512], fp32)) for i in range(8)]
        T_BANK, O_BANK = banks[6], banks[7]

        def view(where, at, *shape):
            v = where[:, at:at + int(np.prod(shape))]
            return v.rearrange("p (a b) -> p a b", b=shape[1]) if len(shape) == 2 else v

        def tile_cols(strips, c):
            return strips[:, 0, :].rearrange("p (k m) -> p k m", m=2 * P)[:, :, c * P:c * P + P]

        def par_col(name, i=0):
            return params[:, COLS[name] + i:COLS[name] + i + 1]

        x_in_tok = view(arena, 0, NT, D)
        xn0 = view(arena, 12320, NT, D)
        squares0 = view(arena, 4096, NT, D)
        mem_tok = view(arena, 8192, 2, D)
        mem_hi, mem_lo = (v[:, 8:12, :].rearrange("p a (b s) -> p (a b) s", b=2) for v in (y_hi, y_lo))
        xc = view(arena, 2048, 4, S)
        xa_pad = view(arena, 4096, 4, S + 3)
        lru_t = view(arena, 4096, 4, S)
        lru_i = view(arena, 6144, 4, S)
        lru_tmp = view(arena, 8192, 2, S)
        lru_r = view(arena, 10240, 4, S)
        ga_gelu = view(arena, 16416, 4, S)
        wa_bd = view(arena, 9216, 4, P)
        wx_bd = view(arena, 9728, 4, P)
        mkT = view(arena, 12320, 4, MEM)
        mv_tok = view(arena, 13344, 2, S)
        xqT = view(arena, 14368, 4, S)
        qT = view(arena, 0, 4, S)
        kT = view(arena, 2048, 4, S)
        v_tok = view(arena, 4096, 4, S)
        z = view(arena, 6144, 2, S)
        prob = view(arena, 7168, 2, S)
        bias1 = view(arena, 8192, 2, S)
        pT1 = view(arena, 9216, 2, S)
        o_tok1 = view(arena, 10240, 4, S)
        merged = view(arena, 12320, KT, S)
        gT = view(arena, 0, KT, S)
        mtmp = view(arena, 4096, 4, S)
        x_tok = view(arena, 6144, NT, D)
        xn = view(arena, 0, NT, D)
        squares = view(arena, 12320, NT, D)
        gain_row = view(arena, 4608, D)
        squares2 = [view(arena, at, D) for at in (10240, 11264, 16416, 17440)]
        gpad = view(arena, 12320, 2, S + 2)
        cv = view(arena, 13408, 2, S)
        gl = view(arena, 14432, 2, S)
        pr = view(arena, 15456, 2, S)
        rqT = [view(arena, 4096 * g, 2, S) for g in range(2)]
        rkT = [view(arena, 4096 * g + 1024, 2, S) for g in range(2)]
        rv = [view(arena, 4096 * g + 2048, 4, S) for g in range(2)]
        gate = view(arena, 8192, 4, S)
        o_tok = view(arena, 10240, 4, S)
        st = view(arena, 12288, 2, 1280)
        ST_AT = [0, 512, 896, 1152]
        decay = view(arena, 14848, 2, S)
        o_squares = view(arena, 15872, 4, S)
        m_ret = view(arena, 0, KT, S)
        m_back = view(arena, 4096, KT, S)
        dqT = [view(arena, 4096 * p, 2, S) for p in range(2)]
        dkT = [view(arena, 4096 * p + 1024, 2, S) for p in range(2)]
        dv = [view(arena, 4096 * p + 2048, 4, S) for p in range(2)]
        do_tok = [view(arena, 10240 + 1024 * p, 4, 2 * P) for p in range(2)]
        bias2 = view(arena, 12288, 2, S)
        pT2 = view(arena, 13312, 2, S)
        dprob = view(arena, 14336, 4, S)
        dsq = view(arena, 16384, 4, S)
        xb = view(arena, 8192, NT, D)
        res = view(arena, 0, NT, D)

        ssq = stats[:, 0:4]
        rstd = stats[:, 4:8]
        ssq2, rstd2 = stats[:, 104:108], stats[:, 108:112]
        sp8 = stats[:, 8:12]
        nsp8 = stats[:, 12:16]
        spt = stats[:, 16:36]
        lam_col = stats[:, 36:37]
        lam_t = stats[:, 37:41]
        nmax = stats[:, 44:48]
        psum_p = stats[:, 48:56]
        rsum = stats[:, 56:64]
        rsl = stats[:, 64:68]
        ossq = stats[:, 72:88]
        orstd = stats[:, 88:104]

        raw_in = [sem("raw_in0"), sem("raw_in1")]
        half_hi, half_lo = sem("half_hi"), sem("half_lo")
        w_hi_ready = sem("w_hi_ready")
        w_lo_ready = [sem("w_lo_ready0"), sem("w_lo_ready1")]
        open_used = sem("open_used")
        acc_done = sem("acc_done")
        acc_out = [sem(f"acc_out{i}") for i in range(4)]
        small_in, lqk_ready = sem("small_in"), sem("lqk_ready")
        lruw_in = sem("lruw_in")
        x_tile_in = [sem(f"x_tile_in{j}") for j in range(NT)]
        x_in = [None, sem("x_in1"), sem("mem_in"), sem("row_in"), sem("xb_in"), sem("mret_in")]
        const_ready = sem("const_ready")
        ssq_ready, var_ready, sd_ready = sem("ssq_ready"), sem("var_ready"), sem("sd_ready")
        xg_ready, eps_ready = sem("xg_ready"), sem("eps_ready")
        xn_ready, hT_done, hhi_ready, hlo_ready = sem("xn_ready"), sem("hT_done"), sem("hhi_ready"), sem("hlo_ready")
        sp_e, sp_ready = sem("sp_e"), sem("sp_ready")
        lam_s, lam_e = sem("lam_s"), sem("lam_e")
        ixc_ready = sem("ixc_ready")
        xc_ready, lru_mm, lru_ri, lru_ta, lru_m2, lru_mult, ya_ready = (
            sem(n) for n in ("xc_ready", "lru_mm", "lru_ri", "lru_ta", "lru_m2", "lru_mult", "ya_ready"))
        sc_done, z_ready, p_ready, pT_done, pT_out, o_done, o_out = (
            sem(n) for n in ("sc_done", "z_ready", "p_ready", "pT_done", "pT_out", "o_done", "o_out"))
        bias_ready, a_ready = sem("bias_ready"), sem("a_ready")
        ovar_ready, osd_ready, on_ready, oT_done, y_ready, yhi_ready, ylo_ready = (
            sem(n) for n in ("ovar_ready", "osd_ready", "on_ready", "oT_done", "y_ready",
                             "yhi_ready", "ylo_ready"))
        m_ready, mhi_ready, mlo_ready = sem("m_ready"), sem("mhi_ready"), sem("mlo_ready")
        conv_ready, gelu_ready, ahi_ready, alo_ready = (
            sem(n) for n in ("conv_ready", "gelu_ready", "ahi_ready", "alo_ready"))
        x1_ready, xb_ready, xb_out, mret_ready, mret_out = (
            sem(n) for n in ("x1_ready", "xb_ready", "xb_out", "mret_ready", "mret_out"))
        dsq_ready, dss_done, dn_ready, th_ready = (
            sem(n) for n in ("dsq_ready", "dss_done", "dn_ready", "th_ready"))
        st_ready, so_done, so_out, dec_ready = (sem(n) for n in ("st_ready", "so_done", "so_out", "dec_ready"))
        res_ready, res_out = sem("res_ready"), sem("res_out")

        NORMS = ["mix", "mem", "ffn", "final", "norm2"]
        SSQ_AT = dict(zip(NORMS, [0, 4, 6, 10, 11]))

        def ssq_count(name, j):
            return SSQ_AT[name] + (2 * j if name in ("final", "norm2") else j) + 1

        XN_AT = dict(zip(NORMS, [0, 4, 6, None, 10]))
        HT_AT = dict(zip(NORMS, [0, 8, 16, None, 24]))
        U_X, U_M, U_D = 0, 16, 48
        SC_AT = {"x": 0, "m": 16, "r": 48, "d": 80}
        Z_AT = {"x": 0, "m": 16, "d": 48}
        O_NORM = {"r0": 0, "r1": 1, "d0": 2, "d1": 3, "d2": 4, "d3": 5}
        OT_AT = {"x": 0, "m": 4, "r0": 8, "r1": 12, "d0": 16, "d1": 18, "d2": 20, "d3": 22}
        M_AT = {"one": 0, "two": 8}
        X1_AT = {"wo": 0, "down1": 4}
        MOBA_UNITS = [(h, t) for h in range(8) for t in range(NT)]
        PACE = {"x": (5, 4), "m": (3, 2), "r": (5, 4), "d": (1, 1)}
        LEAD = [0, 0, 0, 0]

        block = ctx.enter_context(nc.Block())

        @block.sync
        def _(sp):
            xv = x.rearrange("(j p) d -> p j d", p=P)
            for j in range(NT):
                sp.dma_start(x_in_tok[:, j, :], x[j * P:(j + 1) * P, :]).then_inc(x_tile_in[j], 16)
            sp.dma_start(params[:], par).then_inc(small_in, 16)
            for slot in range(2):
                sp.dma_start(w_raw[:, slot, :], wstream[slot * P:(slot + 1) * P, :]).then_inc(raw_in[slot], 16)
            sp.dma_start(mem_tok, mem.rearrange("(j p) d -> p j d", p=P)).then_inc(x_in[2], 16)
            sp.dma_start(lqk[:], lqk_in).then_inc(lqk_ready, 16)

            def strips(lo, hi):
                with sp.Fori(lo, hi) as i:
                    for slot in range(2):
                        sp.wait_ge(w_lo_ready[slot], i)
                        sp.dma_start(w_raw[:, slot, :], wstream[ds(i * (2 * P) + slot * P, P), :]).then_inc(raw_in[slot], 16)

            def first(name):
                return STRIP_AT[name] // 2 + 1

            strips(1, first("gate1"))
            sp.wait_ge(oT_done, OT_AT["m"] + 4)
            sp.dma_start(x_tok, xv).then_inc(x_in[1], 16)
            strips(first("gate1"), first("down1"))
            sp.dma_start(gain_row, final_g).then_inc(x_in[3], 16)
            strips(first("down1"), first("rv0"))
            sp.wait_ge(xb_ready, NT)
            sp.dma_start(xb_dram.rearrange("(j p) d -> p j d", p=P), x_tok).then_inc(xb_out, 16)
            strips(first("rv0"), first("dqk0"))
            sp.wait_ge(mret_ready, KT)
            sp.dma_start(mret_dram.rearrange("p (c s) -> p c s", s=S), m_ret).then_inc(mret_out, 16)
            strips(first("dqk0"), first("dwo"))
            sp.wait_ge(mret_out, 16)
            sp.wait_ge(o_out, U_D + 32)
            sp.dma_start(m_back, mret_dram.rearrange("p (c s) -> p c s", s=S)).then_inc(x_in[5], 16)
            sp.wait_ge(xb_out, 16)
            sp.wait_ge(ylo_ready, OT_AT["d3"] + 2)
            sp.dma_start(xb, xb_dram.rearrange("(j p) d -> p j d", p=P)).then_inc(x_in[4], 16)
            strips(first("dwo"), first("wo2"))
            strips(first("wo2"), STRIPS // 2)
            sp.wait_ge(res_ready, NT)
            sp.dma_start(out.rearrange("(j p) d -> p j d", p=P)[:, :, 0:S], res[:, :, 0:S]).then_inc(res_out, 16)
            for j in range(NT):
                sp.wait_ge(res_ready, NT + j + 1)
                sp.dma_start(out[j * P:(j + 1) * P, S:D], res[:, j, S:D]).then_inc(res_out, 16)
            sp.wait_ge(res_out, 16 * (NT + 1))

        @block.gpsimd
        def _(pool):
            nc.gpsimd.memset(ident[:], 0.0)
            nc.gpsimd.memset(half_ones[:], 1.0)
            nc.gpsimd.iota(neg_dist[:], pattern=[[1, S]], base=-3 * P, channel_multiplier=-1,
                           allow_small_or_imprecise_dtypes=True)
            nc.gpsimd.iota(fwd_dist[:], pattern=[[1, S]], base=0, channel_multiplier=-1,
                           allow_small_or_imprecise_dtypes=True)
            pool.drain()
            nc.gpsimd.affine_select(out=ident[:], in_=ident[:], compare_op=ALU.not_equal, fill=1.0, base=0,
                                    pattern=[[-1, P]], channel_multiplier=1)
            nc.gpsimd.affine_select(out=half_ones[:, 0:64], in_=half_ones[:, 0:64], compare_op=ALU.is_ge, fill=0.0,
                                    base=63, pattern=[[0, 64]], channel_multiplier=-1)
            nc.gpsimd.affine_select(out=half_ones[:, 64:P], in_=half_ones[:, 64:P], compare_op=ALU.is_ge, fill=0.0,
                                    base=-64, pattern=[[0, 64]], channel_multiplier=1)
            nc.gpsimd.affine_select(out=neg_dist[:], in_=neg_dist[:], compare_op=ALU.is_ge, fill=MASKED,
                                    base=3 * P, pattern=[[-1, S]], channel_multiplier=1)
            nc.gpsimd.affine_select(out=fwd_dist[:], in_=fwd_dist[:], compare_op=ALU.is_ge, fill=FAR,
                                    base=0, pattern=[[1, S]], channel_multiplier=-1).then_inc(const_ready, 1)
            pool.wait_ge(xn_ready, XN_AT["mem"] + 2)
            nc.gpsimd.memset(wa_bd, 0.0)
            nc.gpsimd.memset(wx_bd, 0.0).then_inc(const_ready, 1)
            pool.wait_ge(const_ready, 2)
            for k, bd in enumerate((wa_bd, wx_bd)):
                for s in range(2):
                    pool.dma_start(bd[64 * s:64 * s + 64, :, 64 * s:64 * s + 64],
                                   lru_w[64 * s:64 * s + 64, k, :, :]).then_inc(lruw_in, 16)
            for c in range(4):
                pool.wait_ge(lru_ri, 2 * c + 2)
                nc.gpsimd.tensor_tensor(lru_i[:, c, :], lru_i[:, c, :], xc[:, c, :], ALU.mult).then_inc(ixc_ready, 1)
            pool.wait_ge(lru_m2, 4)
            nc.gpsimd.memset(bias1, 0.0).then_inc(bias_ready, 1)

            def low(n):
                pool.wait_ge(w_hi_ready, n + 1)
                nc.gpsimd.tensor_tensor(w_lo[:, n % 2, :], w_raw[:, n % 2, :], w_hi[:, n % 2, :].bitcast(fp32),
                                        ALU.subtract).then_inc(w_lo_ready[n % 2], 1)

            def moba_bias(h):
                pool.wait_ge(z_ready, U_M + max(0, 4 * (h - 1)))
                nc.gpsimd.tensor_scalar(bias1[:, h % 2, :], neg_dist[:], 2.0 ** -(h + 1), None,
                                        ALU.mult).then_inc(bias_ready, 1)

            def diff_bias(h):
                if h < 2:
                    pool.wait_ge(so_out, 8)
                else:
                    pool.wait_ge(z_ready, Z_AT["d"] + 8 * (h - 1))
                nc.gpsimd.tensor_scalar(bias2[:, h % 2, :], neg_dist[:], 2.0 ** -(h + 1), None,
                                        ALU.mult).then_inc(bias_ready, 1)

            num, den = PACE["m"]
            jobs = [(4 * (m + 1) - 16 + 0.5, low, n) for m, n in enumerate(POOL_MOBA)]
            jobs += [((4 * h + 1) * den / num - 1, moba_bias, h) for h in range(8)]
            for _, job, n in sorted(jobs, key=lambda j: j[0]):
                job(n)
            jobs = [(4 * (m + 1) - 16 + 0.5, low, n) for m, n in enumerate(POOL_DIFF)]
            jobs += [(16 * (h // 2) + (2 if h > 1 else 0) + LEAD[h // 2] + 4 * (h % 2) - 1, diff_bias, h) for h in range(8)]
            for _, job, n in sorted(jobs, key=lambda j: j[0]):
                job(n)

        @block.tensor
        def _(pe):
            def half_slots(steps, kind):
                num, den = PACE[kind]
                return pacer(steps, num, 2 * den)

            def free_bank(b, uses):
                if not isinstance(uses, int) or uses > 0:
                    pe.wait_ge(acc_out[b], uses)

            def three(dst, w, a, weights_still, first, last):
                for k, (i, j) in enumerate(((0, 0), (0, 1), (1, 0))):
                    l, r = (w[i], a[j]) if weights_still else (a[j], w[i])
                    done = nc.tensor.matmul(dst, l, r, start=first and k == 0, stop=last and k == 2)
                return done

            def pair_a(name, i=0, src=(h_hi, h_lo), n=S, side=None, hooks={}, operand=None, late=None):
                s0, t0 = STRIP_AT[name], TILE_AT[name]
                for slot in range(2):
                    if name == "xa" and slot == 0:
                        pe.wait_ge(half_lo, 1)
                    else:
                        pe.wait_ge(w_lo_ready[slot], i + (s0 // 2 + 1))
                    order = [(c, kt) for c in range(2) for kt in range(KT)]
                    if late and slot == 0:
                        order.sort(key=lambda ck: ck[1] >= late)
                    seen = set()
                    for c, kt in order:
                        b = 2 * slot + c
                        if name == "xa" and (b, kt) == (1, 0):
                            pe.wait_ge(w_lo_ready[0], 1)
                        if kt == 0:
                            free_bank(b, i + t0 // 4)
                        if operand and slot == 0 and kt not in seen:
                            operand(kt)
                            seen.add(kt)
                        cols = slice(kt * 256 + c * P, kt * 256 + c * P + P)
                        done = three(banks[b][:, 0:n], (w_hi[:, slot, cols], w_lo[:, slot, cols]),
                                     (src[0][:, kt, :], src[1][:, kt, :]), True, kt == 0, kt == KT - 1)
                        if kt == KT - 1:
                            done.then_inc(acc_done, 1)
                        if side and kt % 2:
                            side()
                        if kt % 4 == 3:
                            if 4 * slot + 2 * c + kt // 4 in hooks:
                                hooks[4 * slot + 2 * c + kt // 4]()

            def group_b(name, i=0, src=(h_hi, h_lo), strips=2, s_off=0, t_off=0, b_off=0, side=None,
                        hooks={}, operand=None):
                s0, t0 = STRIP_AT[name] + s_off, TILE_AT[name] + t_off
                for k in range(strips):
                    slot = (s0 + k) % 2
                    pe.wait_ge(w_lo_ready[slot], (i * strips + s0 + k) // 2 + 1)
                    for j in range(NT):
                        if k == 0 and b_off == 0:
                            free_bank(j, i + t0 // 4)
                        for q in range(4):
                            kt, cols, tok = 4 * k + q, slice(q * 512, q * 512 + 512), slice(j * P, j * P + P)
                            if operand and j == 0:
                                operand(kt)
                            done = three(banks[b_off + j][:], (w_hi[:, slot, cols], w_lo[:, slot, cols]),
                                         (src[0][:, kt, tok], src[1][:, kt, tok]), False, kt == 0, kt == 4 * strips - 1)
                            if side and q == 1:
                                side()
                        if k == strips - 1:
                            done.then_inc(acc_done, 1)
                        elif j == NT - 1:
                            done.then_inc(open_used, 1)
                        if side:
                            side()
                        if 4 * k + j in hooks:
                            hooks[4 * k + j]()

            def pair_c(name, y_at, side=None):
                s0, t0 = STRIP_AT[name], TILE_AT[name]
                for slot in range(2):
                    pe.wait_ge(w_lo_ready[slot], s0 // 2 + 1)
                    for c in range(4):
                        free_bank(c, t0 // 4 + slot)
                        for q in range(4):
                            cols = slice(q * 512 + c * P, q * 512 + c * P + P)
                            done = three(banks[c][:], (w_hi[:, slot, cols], w_lo[:, slot, cols]),
                                         (y_hi[:, y_at + q, :], y_lo[:, y_at + q, :]), True, q == 0, q == 3)
                            if side and q == 1:
                                side()
                        done.then_inc(acc_done, 1)
                        if side:
                            side()

            def loop_a(name, pairs, **kw):
                with pe.Fori(0, pairs) as i:
                    pair_a(name, i, **kw)

            def stay_warm(columns):
                for n in columns:
                    nc.tensor.matmul(banks[7][:, 0:n], ident[:], fwd_dist[:, 0:n], start=True, stop=True)

            def norm_t(name, following, xn=xn, fill=()):
                stay_warm(fill)
                for j in range(NT):
                    pe.wait_ge(xn_ready, XN_AT[name] + j + 1)
                    for kt in (4, 5, 6, 7, 0, 1, 2, 3) if j == 0 else range(KT):
                        if j == 0 and kt < 4:
                            free_bank(kt, TILE_AT[following] // 4)
                        done = nc.tensor.transpose(banks[kt][:, j * P:j * P + P],
                                                   xn[:, j, kt * P:kt * P + P], ident[:])
                        if j == NT - 1:
                            done.then_inc(hT_done, 1)

            def mem_norm_t(kts):
                pe.wait_ge(xn_ready, XN_AT["mem"] + 2)
                for kt in kts:
                    pe.wait_ge(hlo_ready, HT_AT["mem"] + kt - 3 if kt >= 4 else HT_AT["mem"])
                    for j in range(2):
                        done = nc.tensor.transpose(banks[4 + kt % 4][:, j * P:j * P + P],
                                                   xn0[:, j, kt * P:kt * P + P], ident[:])
                    done.then_inc(hT_done, 1)

            def split_rows(name):
                return lambda kt: pe.wait_ge(hlo_ready, HT_AT[name] + kt + 1)

            def attend(units, o_cols, base_u, o_tok):
                def scores(k):
                    if k >= 2:
                        pe.wait_ge(z_ready, base_u + k - 1)
                    nc.tensor.matmul(banks[4 + k % 2][:, 0:units[k][2]], *units[k][0],
                                     start=True, stop=True).then_inc(sc_done, 1)

                def transposes(k):
                    pe.wait_ge(p_ready, base_u + k + 1)
                    if k >= 1:
                        pe.wait_ge(pT_out, base_u + k)
                    for c in range(units[k][2] // P):
                        done = nc.tensor.transpose(T_BANK[:, c * P:c * P + P], prob[:, k % 2, c * P:c * P + P], ident[:])
                    done.then_inc(pT_done, 1)

                def outputs(k):
                    pe.wait_ge(pT_out, base_u + k + 1)
                    if k >= 1:
                        pe.wait_ge(o_out, base_u + k)
                    vals = units[k][1]
                    for c, val in enumerate(vals):
                        done = nc.tensor.matmul(O_BANK[:, 0:o_cols], pT1[:, k % 2, c * P:c * P + P], val,
                                                start=c == 0, stop=c == len(vals) - 1)
                    done.then_inc(o_done, 1)

                scores(0)
                yield
                for k in range(len(units)):
                    if k + 1 < len(units):
                        scores(k + 1)
                    if k >= 1:
                        outputs(k - 1)
                    transposes(k)
                    yield
                outputs(len(units) - 1)
                yield
                pe.wait_ge(o_out, base_u + len(units))
                for c in range(4):
                    for j in range(NT):
                        done = nc.tensor.transpose(banks[4 + c][:, j * P:j * P + P], o_tok[:, j, c * P:c * P + P], ident[:])
                    done.then_inc(oT_done, 1)
                yield

            def ret_attend(g):
                def outputs(hh):
                    head = 4 * g + hh
                    pe.wait_ge(st_ready, 4 * head + 4)
                    if head >= 2:
                        pe.wait_ge(so_out, head - 1)
                    for j in range(NT):
                        for c in range(j + 1):
                            at = ST_AT[c] + (j - c) * P
                            done = nc.tensor.matmul(banks[6 + head % 2][:, j * P:j * P + P], st[:, hh % 2, at:at + P],
                                                    rv[g][:, c, hh * P:hh * P + P], start=c == 0, stop=c == j)
                    done.then_inc(so_done, 1)

                for hh in range(4):
                    rows, tile = slice(64 * (hh % 2), 64 * (hh % 2) + 64), hh // 2
                    for c in range(NT):
                        r = (4 * g + hh) * 4 + c
                        if r >= 2:
                            pe.wait_ge(st_ready, r - 1)
                        if g == 1 and r == 16:
                            pe.wait_ge(y_ready, 4)
                        nc.tensor.matmul(banks[4 + r % 2][:, 0:S - c * P], rkT[g][rows, tile, c * P:c * P + P],
                                         rqT[g][rows, tile, c * P:S], start=True, stop=True).then_inc(sc_done, 1)
                        if c == 1 and hh >= 1:
                            outputs(hh - 1)
                        yield
                yield
                outputs(3)
                yield

            def group_t(key, tokens, tiles, b0):
                pe.wait_ge(on_ready, O_NORM[key] + 1)
                for c in range(tiles):
                    for j in range(NT):
                        done = nc.tensor.transpose(banks[b0 + c][:, j * P:j * P + P], tokens[:, j, c * P:c * P + P], ident[:])
                    done.then_inc(oT_done, 1)

            def group_side(key, tokens, tiles, b0, at):
                for _ in range(at):
                    yield
                group_t(key, tokens, tiles, b0)
                yield

            def diff_attend(g):
                q, k_, v = dqT[g % 2], dkT[g % 2], dv[g // 2]
                base_u, z0 = U_D + 8 * g, Z_AT["d"] + 16 * g

                def scores(k):
                    hh, t = k // NT, k % NT
                    for m in range(2):
                        if g or k:
                            pe.wait_ge(z_ready, z0 + 2 * k + m - 1)
                        rows = slice(64 * m, 64 * m + 64)
                        nc.tensor.matmul(banks[4 + m][:, 0:(t + 1) * P], q[rows, hh, t * P:t * P + P],
                                         k_[rows, hh, 0:(t + 1) * P], start=True, stop=True).then_inc(sc_done, 1)

                def transposes(k):
                    pe.wait_ge(a_ready, 8 * g + k + 1)
                    if k >= 1:
                        pe.wait_ge(pT_out, base_u + k)
                    elif g:
                        pe.wait_ge(y_ready, 8 + 2 * g)
                    for c in range(k % NT + 1):
                        done = nc.tensor.transpose(T_BANK[:, c * P:c * P + P], dprob[:, 2 * (k % 2), c * P:c * P + P], ident[:])
                    done.then_inc(pT_done, 1)

                def outputs(k):
                    pe.wait_ge(pT_out, base_u + k + 1)
                    if k >= 1:
                        pe.wait_ge(o_out, base_u + k)
                    hh, t, at = k // NT, k % NT, (2 * (g % 2) + k // NT) * P
                    for c in range(t + 1):
                        done = nc.tensor.matmul(O_BANK[:, 0:P], pT2[:, k % 2, c * P:c * P + P], v[:, c, at:at + P],
                                                start=c == 0, stop=c == t)
                    done.then_inc(o_done, 1)

                pe.wait_ge(dn_ready, 4 * g + 4)
                for b in range(4):
                    pe.wait_ge(acc_out[b], TILE_AT["dqk1"] // 4 if g < 2 else TILE_AT["dqk3"] // 4)
                scores(0)
                yield
                for k in range(8):
                    if k < 7:
                        scores(k + 1)
                    if k >= 1:
                        outputs(k - 1)
                    transposes(k)
                    yield
                outputs(7)
                yield

            def head_sums(g, tiles):
                for c in tiles:
                    pe.wait_ge(dsq_ready, 4 * g + c + 1)
                    nc.tensor.matmul(banks[c][:], half_ones[:], dsq[:, c, :], start=True, stop=True).then_inc(dss_done, 1)

            def both(*parts):
                for part in parts:
                    yield from part

            pe.wait_ge(const_ready, 1)
            norm_t("mix", "xa", xn0, fill=(512, 256))
            pair_a("xa", operand=split_rows("mix"))
            mem_norm_t(range(4))

            def lru_gates(tiles):
                pe.wait_ge(lruw_in, 64)
                pe.wait_ge(hlo_ready, HT_AT["mem"] + KT)
                for c in tiles:
                    pe.wait_ge(xc_ready, c + 1)
                    for m, bd in enumerate((wa_bd, wx_bd)):
                        if c >= 2:
                            pe.wait_ge(lru_ri, 2 * (c - 2) + m + 1)
                        nc.tensor.matmul(banks[4 + 2 * (c % 2) + m][:], bd[:, c, :], xc[:, c, :],
                                         start=True, stop=True).then_inc(lru_mm, 1)

            pair_a("ga", hooks={0: lambda: mem_norm_t(range(4, 8)), 6: lambda: lru_gates((0, 1))})
            pair_a("memk", src=(mem_hi, mem_lo), n=MEM, hooks={3: lambda: lru_gates((2,)), 5: lambda: lru_gates((3,))})
            s0, t0 = STRIP_AT["memv"], TILE_AT["memv"]
            for k in range(2):
                pe.wait_ge(w_lo_ready[k], s0 // 2 + 1)
                for j in range(2):
                    for half in range(2):
                        b = 2 * j + half
                        if k == 0:
                            free_bank(b, t0 // 4)
                        for q in range(4):
                            cols = slice(q * 512 + half * 256, q * 512 + half * 256 + 256)
                            done = three(banks[b][:, 0:256], (w_hi[:, k, cols], w_lo[:, k, cols]),
                                         (mem_hi[:, 4 * k + q, j * P:j * P + P], mem_lo[:, 4 * k + q, j * P:j * P + P]),
                                         False, k == 0 and q == 0, k == 1 and q == 3)
                        if k == 1:
                            done.then_inc(acc_done, 1)
                if k == 0:
                    done.then_inc(open_used, 1)
            pair_a("xq")

            def cross():
                for b in range(4):
                    pe.wait_ge(acc_out[b], TILE_AT["mq"] // 4)
                yield from attend([((xqT[:, h, t * P:t * P + P], mkT[:, h, :]),
                                    [mv_tok[:, c, h * P:h * P + P] for c in range(2)], MEM)
                                   for h in range(4) for t in range(NT)], P, U_X, o_tok1)

            pair_a("mq")
            steps = cross()
            side = half_slots(steps, "x")
            pair_a("mk", side=side)
            group_b("mv", side=side)
            finish(steps)

            def moba():
                for b in range(4):
                    pe.wait_ge(acc_out[b], TILE_AT["gate0"] // 4)
                pe.wait_ge(ylo_ready, OT_AT["x"] + 4)
                units = []
                for h, t in MOBA_UNITS:
                    rows = slice(64 * (h % 2), 64 * (h % 2) + 64)
                    units.append(((qT[rows, h // 2, t * P:t * P + P], kT[rows, h // 2, 0:(t + 1) * P]),
                                  [v_tok[:, c, h * 64:h * 64 + 64] for c in range(t + 1)], (t + 1) * P))
                yield from attend(units, 64, U_M, o_tok1)

            steps = moba()
            side = half_slots(steps, "m")
            for i in range(2):
                pair_a("gate0", i, side=side)
            pe.wait_ge(ya_ready, 4)
            pair_c("branch0", 0, side=side)
            finish(steps)
            loop_a("gate1", 2)
            pe.wait_ge(ylo_ready, OT_AT["m"] + 4)
            pair_c("branch1", 4)
            loop_a("gate2", 2)
            pair_c("branch2", 8)
            group_b("wo", operand=lambda kt: pe.wait_ge(mlo_ready, M_AT["one"] + kt + 1))
            group_b("wo", 1)
            norm_t("ffn", "ffn0")
            for f in range(2):
                if f == 0:
                    pair_a("ffn0", operand=split_rows("ffn"))
                with pe.Fori(1 - f, 6) as i:
                    pair_a(f"ffn{f}", i)
                for half in range(2):
                    split_hidden = lambda kt: pe.wait_ge(alo_ready, 12 * f + kt + 1)
                    group_b(f"down{f}", src=(y_hi, y_lo), strips=3, s_off=3 * half, t_off=4 * half, operand=split_hidden)
            norm_t("norm2", "rqk0")
            pair_a("rqk0", operand=split_rows("norm2"))
            group_b("rv0")
            for b in range(4):
                pe.wait_ge(acc_out[b], TILE_AT["rqk1"] // 4)
            steps = ret_attend(0)
            side = half_slots(steps, "r")
            pair_a("rqk1", side=side)
            group_b("rv1", side=side)
            finish(steps)
            pair_a("rg0", hooks={3: lambda: group_t("r0", o_tok, 4, 4)})
            for b in range(4):
                pe.wait_ge(acc_out[b], TILE_AT["rg0"] // 4)
            steps = ret_attend(1)
            side = half_slots(steps, "r")
            for i in range(2):
                pair_a("rmg", i, side=side)
            finish(steps)
            pair_a("rg1", hooks={3: lambda: group_t("r1", o_tok, 4, 4)})
            def split_outputs(key, first_kt, tiles):
                return lambda kt: kt >= first_kt and pe.wait_ge(ylo_ready, OT_AT[key] + min(kt - first_kt + 1, tiles))

            pair_a("rwo", src=(y_hi, y_lo), operand=split_outputs("r1", 4, 4), late=4)
            pair_a("rwo", 1, src=(y_hi, y_lo))
            early = lambda g: {5: lambda: head_sums(g, (0, 1))}
            late = lambda g: {1: lambda: head_sums(g, (2, 3))}
            late_b = lambda g: {0: lambda: head_sums(g, (2, 3))}
            pair_a("dqk0", hooks=early(0))
            group_b("dv0", hooks=late_b(0))
            side = steps = None
            for g, beside in enumerate((("dqk1", "dg0"), ("dqk2", "dv1"), ("dqk3", "dg1"))):
                last = [group_side(f"d{g - 1}", do_tok[(g - 1) % 2], 2, 6, 1)] if g else []
                steps = both(*last, lead(LEAD[g]), diff_attend(g))
                side = half_slots(steps, "d")
                pair_a(beside[0], side=side, hooks=early(g + 1))
                if beside[1] == "dv1":
                    group_b("dv1", side=side, hooks=late_b(g + 1))
                else:
                    pair_a(beside[1], side=side, hooks=late(g + 1))
                finish(steps)
            steps = both(group_side("d2", do_tok[0], 2, 6, 1), lead(LEAD[3]), diff_attend(3),
                         group_side("d3", do_tok[1], 2, 6, 1))
            side = half_slots(steps, "d")
            for i in range(2):
                pair_a("dmg", i, side=side)
            finish(steps)
            pair_a("dwo", src=(y_hi, y_lo), operand=split_outputs("d3", 6, 2), late=6)
            pair_a("dwo", 1, src=(y_hi, y_lo))
            group_b("wo2", operand=lambda kt: pe.wait_ge(mlo_ready, M_AT["two"] + kt + 1))
            group_b("wo2", 1, b_off=4)

        @block.scalar
        def _(act):
            def split_hi(name, slot, i=0, ahead=2):
                n = STRIP_AT[name] + slot + ahead
                if isinstance(i, int) and n + 2 * i >= STRIPS:
                    return
                act.wait_ge(raw_in[n % 2], i * 16 + 16 * (n // 2 + 1))
                nc.scalar.activation(w_hi[:, n % 2, :], w_raw[:, n % 2, :], ACT.Copy).then_inc(w_hi_ready, 1)

            def tile_done(name, k, i=0):
                act.wait_ge(acc_done, i * 4 + (TILE_AT[name] + k + 1))

            def pair_a(name, post, i=0, side=None, hooks={}):
                for slot in range(2):
                    for c in range(2):
                        if side:
                            side()
                            side()
                        tile_done(name, 2 * slot + c, i)
                        done = post(2 * slot + c, banks[2 * slot + c])
                        if done:
                            done.then_inc(acc_out[2 * slot + c], 1)
                        if 2 * slot + c in hooks:
                            hooks[2 * slot + c]()
                    split_hi(name, slot, i)

            def group_b(name, post=None, i=0, side=None, hooks={}):
                for j in range(NT):
                    if side:
                        side()
                    if j in hooks:
                        hooks[j]()
                act.wait_ge(open_used, i + (OPEN_AT[name] + 1))
                split_hi(name, 0, i)
                for j in range(NT):
                    if side:
                        side()
                    tile_done(name, j, i)
                    if post:
                        post(j, banks[j]).then_inc(acc_out[j], 1)
                split_hi(name, 1, i)

            def norm_square(name, src, j, sums, squares):
                nc.scalar.activation(squares[j], src[:, j, :], ACT.Square,
                                     accum_out=sums[:, j:j + 1]).then_inc(ssq_ready, 1)

            def norm_sd(name, j, sums, roots):
                act.wait_ge(var_ready, ssq_count(name, j))
                nc.scalar.activation(roots[:, j:j + 1], sums[:, j:j + 1], ACT.Sqrt).then_inc(sd_ready, 1)

            def norm_stats(name, src, j, squares=squares):
                norm_square(name, src, j, ssq, [squares[:, k, :] for k in range(NT)])
                norm_sd(name, j, ssq, rstd)

            def norm_hi(name, gain, hi, n, kts=range(KT)):
                for kt in kts:
                    act.wait_ge(hT_done, HT_AT[name] + kt + 1)
                    bank = banks[4 + kt % 4 if name == "mem" else kt]
                    nc.scalar.activation(hi[:, kt, :], bank[:, 0:n], ACT.Identity,
                                         scale=par_col(gain, kt)).then_inc(hhi_ready, 1)

            def half_tanh(dst, bank):
                return nc.scalar.activation(dst, bank[:], ACT.Tanh, scale=0.5)

            def copy_to(dst, scale=1.0):
                return lambda k, bank: nc.scalar.activation(dst(k), bank[:, 0:dst(k).shape[-1]], ACT.Copy, scale=scale)

            def attend(widths, base_u, y_at):
                def transposed(k):
                    act.wait_ge(pT_done, base_u + k + 1)
                    if k >= 2:
                        act.wait_ge(o_done, base_u + k - 1)
                    nc.scalar.activation(pT1[:, k % 2, 0:widths[k]], T_BANK[:, 0:widths[k]], ACT.Copy).then_inc(pT_out, 1)

                yield
                for k, w in enumerate(widths):
                    if k >= 1:
                        transposed(k - 1)
                    act.wait_ge(z_ready, base_u + k + 1)
                    if k >= 2:
                        act.wait_ge(pT_done, base_u + k - 1)
                    nc.scalar.activation(prob[:, k % 2, 0:w], z[:, k % 2, 0:w], ACT.Exp, scale=-1.0,
                                         bias=nmax[:, k % 4:k % 4 + 1],
                                         accum_out=psum_p[:, k % 4:k % 4 + 1]).then_inc(p_ready, 1)
                    yield
                transposed(len(widths) - 1)
                yield
                yield
                for c in range(4):
                    act.wait_ge(oT_done, OT_AT["x" if y_at == 8 else "m"] + c + 1)
                    nc.scalar.activation(y_hi[:, y_at + c, :], banks[4 + c][:], ACT.Copy).then_inc(yhi_ready, 1)

            def ret_attend(g):
                def decays(hh):
                    head = 4 * g + hh
                    if head >= 2:
                        act.wait_ge(st_ready, 4 * (head - 1))
                    nc.scalar.activation(decay[:, hh % 2, :], fwd_dist[:], ACT.Exp,
                                         scale=float(np.log1p(-2.0 ** (-5.0 - head)))).then_inc(dec_ready, 1)

                def output(hh):
                    head = 4 * g + hh
                    act.wait_ge(so_done, head + 1)
                    bank = banks[6 + head % 2].rearrange("p (j e) -> p j e", e=P)
                    nc.scalar.activation(o_tok[:, :, hh * P:hh * P + P], bank, ACT.Copy)
                    nc.scalar.activation(o_squares[:, :, hh * P:hh * P + P], bank, ACT.Square).then_inc(so_out, 1)

                decays(0)
                for hh in range(4):
                    for c in range(NT):
                        if c == 2 and hh >= 1:
                            output(hh - 1)
                        if c == 3 and hh < 3:
                            decays(hh + 1)
                        yield
                yield
                yield
                output(3)

            def group_root(key, n):
                act.wait_ge(ovar_ready, O_NORM[key] + 1)
                nc.scalar.activation(ossq[:, 0:n], ossq[:, 0:n], ACT.Sqrt).then_inc(osd_ready, 1)

            def group_hi(y_from, tiles, g_at, y_at):
                for c in tiles:
                    act.wait_ge(y_ready, y_from + c + 1)
                    nc.scalar.activation(y_hi[:, y_at + c, :], gate[:, g_at + c, :], ACT.Copy).then_inc(yhi_ready, 1)

            def diff_attend(g):
                base_u, z0 = U_D + 8 * g, Z_AT["d"] + 16 * g

                def transposed(k):
                    w = (k % NT + 1) * P
                    act.wait_ge(pT_done, base_u + k + 1)
                    if k >= 2:
                        act.wait_ge(o_done, base_u + k - 1)
                    nc.scalar.activation(pT2[:, k % 2, 0:w], T_BANK[:, 0:w], ACT.Copy).then_inc(pT_out, 1)

                def output(k):
                    hh, t = k // NT, k % NT
                    act.wait_ge(o_done, base_u + k + 1)
                    r0 = rsum[:, k % 4:k % 4 + 1]
                    nc.scalar.activation(do_tok[g % 2][:, t, hh * P:hh * P + P], O_BANK[:, 0:P], ACT.Copy, scale=r0)
                    nc.scalar.activation(O_BANK[:, P:2 * P], O_BANK[:, 0:P], ACT.Square, scale=r0,
                                         accum_out=ossq[:, 2 * t + hh:2 * t + hh + 1]).then_inc(o_out, 1)

                yield
                for k in range(10):
                    if 1 <= k <= 8:
                        transposed(k - 1)
                    if k < 8:
                        w = (k % NT + 1) * P
                        for m in range(2):
                            v = 2 * k + m
                            act.wait_ge(z_ready, z0 + v + 1)
                            nc.scalar.activation(dprob[:, v % 4, 0:w], dprob[:, v % 4, 0:w], ACT.Exp, scale=-1.0,
                                                 bias=nmax[:, v % 4:v % 4 + 1],
                                                 accum_out=psum_p[:, v % 4:v % 4 + 1]).then_inc(p_ready, 1)
                    if k >= 2:
                        output(k - 2)
                    yield

            def diff_finish(g):
                group_root(f"d{g}", 8)
                yield
                group_hi(8 + 2 * g, range(2), 2 * (g % 2), 2 * g)
                yield

            def both(*parts):
                for part in parts:
                    yield from part

            def fetch_root_table():
                nc.scalar.activation(stats[:, 43:44], stats[:, 42:43], ACT.Sqrt)

            act.wait_ge(eps_ready, 1)
            fetch_root_table()
            for j in range(NT):
                act.wait_ge(x_tile_in[j], 16)
                norm_stats("mix", x_in_tok, j, squares0)
            act.wait_ge(raw_in[0], 16)
            nc.scalar.activation(tile_cols(w_hi, 0), tile_cols(w_raw, 0), ACT.Copy).then_inc(half_hi, 1)
            act.wait_ge(small_in, 16)
            norm_hi("mix", "mix_g", h_hi, S, range(4))
            nc.scalar.activation(tile_cols(w_hi, 1), tile_cols(w_raw, 1), ACT.Copy).then_inc(w_hi_ready, 1)
            norm_hi("mix", "mix_g", h_hi, S, range(4, 8))
            split_hi("xa", 1, ahead=0)
            act.wait_ge(x_in[2], 16)
            for j in range(2):
                norm_stats("mem", mem_tok, j, squares0)
            act.wait_ge(sp_e, 1)
            nc.scalar.activation(spt[:, 4:8], spt[:, 0:4], ACT.Exp, scale=-1.0).then_inc(sp_e, 1)
            act.wait_ge(lam_s, 1)
            nc.scalar.activation(lam_t[:, 2:4], lam_t[:, 0:2], ACT.Exp).then_inc(lam_e, 1)
            for c in range(4):
                tile_done("xa", c)
                copy_to(lambda k: xa_pad[:, k, 3:3 + S])(c, banks[c]).then_inc(acc_out[c], 1)
                if c == 1:
                    split_hi("xa", 0)
            norm_hi("mem", "mem_g", mem_hi, MEM, range(4))
            split_hi("xa", 1)
            norm_hi("mem", "mem_g", mem_hi, MEM, range(4, 8))
            pair_a("ga", lambda k, bank: nc.scalar.activation(ga_gelu[:, k, :], bank[:], ACT.Gelu_apprx_tanh))

            def lru():
                act.wait_ge(xc_ready, 4)
                for c in range(4):
                    for m, (dst, b) in enumerate(((lru_r, "b_a"), (lru_i, "b_x"))):
                        act.wait_ge(lru_mm, 2 * c + m + 1)
                        nc.scalar.activation(dst[:, c, :], banks[4 + 2 * (c % 2) + m][:], ACT.Sigmoid,
                                             bias=par_col(b, c)).then_inc(lru_ri, 1)
                    yield
                act.wait_ge(sp_ready, 1)
                act.wait_ge(lru_ri, 8)
                for c in range(4):
                    nc.scalar.activation(lru_t[:, c, :], lru_r[:, c, :], ACT.Tanh, scale=sp8[:, c:c + 1]).then_inc(lru_ta, 1)
                    if c % 2:
                        yield
                act.wait_ge(lru_ta, 4)
                for c in range(4):
                    nc.scalar.activation(lru_r[:, c, :], lru_r[:, c, :], ACT.Exp, scale=nsp8[:, c:c + 1]).then_inc(lru_ta, 1)
                    if c % 2:
                        yield

            steps = lru()
            side = pacer(steps, 1, 2)
            pair_a("memk", copy_to(lambda k: mkT[:, k, :]), side=side)
            group_b("memv", lambda k, bank: nc.scalar.activation(
                mv_tok[:, k // 2, k % 2 * 256:k % 2 * 256 + 256], bank[:, 0:256], ACT.Copy), side=side)
            finish(steps)
            pair_a("xq", copy_to(lambda k: xqT[:, k, :], P ** -0.5))
            for c in range(4):
                act.wait_ge(lru_m2, c + 1)
                nc.scalar.activation(lru_t[:, c, :], lru_t[:, c, :], ACT.Sqrt).then_inc(lru_mult, 1)
            pair_a("mq", copy_to(lambda k: qT[:, k, :], 64 ** -0.5))
            act.wait_ge(ya_ready, 4)
            steps = attend([MEM] * 16, U_X, 8)
            side = pacer(steps, *PACE["x"])
            pair_a("mk", copy_to(lambda k: kT[:, k, :]), side=side)
            group_b("mv", copy_to(lambda k: v_tok[:, k, :]), side=side)
            finish(steps)
            steps = attend([(t + 1) * P for h, t in MOBA_UNITS], U_M, 4)
            side = pacer(steps, *PACE["m"])
            act.wait_ge(oT_done, OT_AT["x"] + 4)
            for i in range(2):
                pair_a("gate0", lambda k, bank: half_tanh(merged[:, 4 * i + k, :], bank), i, side=side)
            for slot in range(2):
                for c in range(4):
                    side()
                tile_done("branch0", 4 * slot + 3)
                split_hi("branch0", slot)
            finish(steps)
            for n in (1, 2):
                act.wait_ge(m_ready, 8 * n)
                if n == 1:
                    act.wait_ge(o_out, U_D)
                with act.Fori(0, 2) as i:
                    pair_a(f"gate{n}", lambda k, bank: half_tanh(
                        gT[:, ds(i * 4 + k, 1), :].rearrange("p a s -> p (a s)"), bank), i)
                for slot in range(2):
                    for c in range(4) if n == 2 else ():
                        act.wait_ge(m_ready, 16 + 4 * slot + c + 1)
                        nc.scalar.activation(h_hi[:, 4 * slot + c, :], merged[:, 4 * slot + c, :], ACT.Copy,
                                             scale=0.5).then_inc(mhi_ready, 1)
                    tile_done(f"branch{n}", 4 * slot + 3)
                    split_hi(f"branch{n}", slot)
            group_b("wo")
            act.wait_ge(open_used, OPEN_AT["wo"] + 2)
            split_hi("wo", 0, 1)
            fetch_root_table()
            for j in range(NT):
                act.wait_ge(x1_ready, X1_AT["wo"] + j + 1)
                norm_stats("ffn", x_tok, j)
            norm_hi("ffn", "ffn_g", h_hi, S)
            split_hi("wo", 1, 1)
            for f in range(2):
                with act.Fori(0, 6) as i:
                    s0 = STRIP_AT[f"ffn{f}"]
                    for c in range(2):
                        tile_done(f"ffn{f}", c, i)
                        act.wait_ge(conv_ready, i * 2 + (12 * f + 1))
                        nc.scalar.activation(gpad[:, c, 2:2 + S], banks[c][:], ACT.Copy).then_inc(acc_out[c], 1)
                    split_hi(f"ffn{f}", 0, i)
                    for c in range(2):
                        act.wait_ge(conv_ready, i * 2 + (12 * f + c + 2))
                        nc.scalar.activation(gl[:, c, :], cv[:, c, :], ACT.Gelu_apprx_tanh).then_inc(gelu_ready, 1)
                    for c in range(2):
                        act.wait_ge(acc_out[2 + c], i + (TILE_AT[f"ffn{f}"] // 4 + 1))
                        nc.scalar.activation(y_hi[:, ds(i * 2 + c, 1), :].rearrange("p a s -> p (a s)"), pr[:, c, :],
                                             ACT.Copy).then_inc(ahi_ready, 1)
                    split_hi(f"ffn{f}", 1, i)
                name = f"down{f}"
                for half in range(2):
                    for k in range(3):
                        if k < 2:
                            act.wait_ge(open_used, OPEN_AT[name] + 2 * half + k + 1)
                        elif f == 0 or half == 0:
                            tile_done(name, 4 * half + 3)
                        if f == 0 or half == 0 or k < 2:
                            split_hi(name, 3 * half + k)
            fetch_root_table()
            for j in range(NT):
                act.wait_ge(x1_ready, X1_AT["down1"] + j + 1)
                norm_square("final", x_tok, j, ssq, [squares[:, k, :] for k in range(NT)])
                act.wait_ge(xg_ready, j + 1)
                norm_square("norm2", xn, j, ssq2, squares2)
                norm_sd("final", j, ssq, rstd)
                norm_sd("norm2", j, ssq2, rstd2)
            norm_hi("norm2", "norm2_g", h_hi, S)
            split_hi("down1", 5)
            def ret_qk(g):
                return lambda k, bank: nc.scalar.activation((rqT if k < 2 else rkT)[g][:, k % 2, :], bank[:], ACT.Copy,
                                                            scale=1.0 if k < 2 else 64 ** -0.5)

            def silu(k, bank):
                return nc.scalar.activation(gate[:, k, :], bank[:], ACT.Silu)

            pair_a("rqk0", ret_qk(0))
            group_b("rv0", copy_to(lambda k: rv[0][:, k, :]))
            steps = ret_attend(0)
            side = pacer(steps, *PACE["r"])
            act.wait_ge(xb_out, 16)
            pair_a("rqk1", ret_qk(1), side=side)
            group_b("rv1", copy_to(lambda k: rv[1][:, k, :]), side=side)
            finish(steps)
            group_root("r0", 16)
            hi = lambda *tiles: lambda: group_hi(0, tiles, 0, 0)
            pair_a("rg0", silu, hooks={1: hi(0), 2: hi(1), 3: hi(2, 3)})
            steps = ret_attend(1)
            side = pacer(steps, *PACE["r"])
            for i in range(2):
                pair_a("rmg", lambda k, bank: half_tanh(gT[:, 4 * i + k, :], bank), i, side=side)
            finish(steps)
            group_root("r1", 16)
            act.wait_ge(ylo_ready, OT_AT["r0"] + 4)
            hi = lambda *tiles: lambda: group_hi(4, tiles, 0, 4)
            pair_a("rg1", silu, hooks={1: hi(0), 2: hi(1), 3: hi(2, 3)})
            for i in range(2):
                for slot in range(2):
                    tile_done("rwo", 4 * i + 2 * slot + 1)
                    split_hi("rwo", slot, i)
            act.wait_ge(mret_out, 16)

            def raw_qk(g):
                def post(k, bank):
                    nc.scalar.activation((dqT if k < 2 else dkT)[g % 2][:, k % 2, :], bank[:], ACT.Copy)
                    if g:
                        act.wait_ge(dn_ready, 4 * (g - 1) + k + 1)
                    nc.scalar.activation(dsq[:, k, :], bank[:], ACT.Square).then_inc(dsq_ready, 1)
                return post

            def roots(g, tiles):
                for c in tiles:
                    act.wait_ge(dss_done, 4 * g + c + 1)
                    nc.scalar.activation(dsq[:, c, :], banks[c][:], ACT.Sqrt, scale=1 / 64 if c >= 2 else 1.0,
                                         bias=stats[:, 41 + c // 2:42 + c // 2]).then_inc(acc_out[c], 1)

            early = lambda g: {2: lambda: roots(g, (0, 1))}
            late = lambda g: {0: lambda: roots(g, (2, 3))}
            late_b = lambda g: {0: lambda: roots(g, (2, 3))}
            pair_a("dqk0", raw_qk(0), hooks=early(0))
            group_b("dv0", copy_to(lambda k: dv[0][:, k, :]), hooks=late_b(0))
            for g, beside in enumerate((("dqk1", "dg0"), ("dqk2", "dv1"), ("dqk3", "dg1"))):
                steps = both(*([diff_finish(g - 1)] if g else []), lead(LEAD[g]), diff_attend(g))
                side = pacer(steps, *PACE["d"])
                pair_a(beside[0], raw_qk(g + 1), side=side, hooks=early(g + 1))
                if beside[1] == "dv1":
                    group_b("dv1", copy_to(lambda k: dv[1][:, k, :]), side=side, hooks=late_b(g + 1))
                else:
                    if g == 2:
                        act.wait_ge(ylo_ready, OT_AT["d1"] + 2)

                    def tanh_only(k, bank):
                        half_tanh(gate[:, k, :], bank).then_inc(th_ready, 1)

                    pair_a(beside[1], tanh_only, side=side, hooks=late(g + 1))
                finish(steps)
            steps = both(diff_finish(2), lead(LEAD[3]), diff_attend(3), diff_finish(3))
            side = pacer(steps, *PACE["d"])
            for i in range(2):
                pair_a("dmg", lambda k, bank: half_tanh(gT[:, 4 * i + k, :], bank), i, side=side)
            finish(steps)
            for i in range(2):
                for slot in range(2):
                    for c in range(2):
                        k = 4 * i + 2 * slot + c
                        act.wait_ge(m_ready, 24 + k + 1)
                        nc.scalar.activation(h_hi[:, k, :], gT[:, k, :], ACT.Copy, scale=0.5).then_inc(mhi_ready, 1)
                    split_hi("dwo", slot, i)
            for i in range(2):
                group_b("wo2", None, i)

        @block.vector
        def _(dve):
            then = dve.drain

            def split_lo(name, slot, i=0, ahead=2):
                n = STRIP_AT[name] + slot + ahead
                if isinstance(i, int) and n + 2 * i >= STRIPS:
                    return
                if isinstance(i, int) and n + 2 * i in POOL_STRIPS:
                    return
                dve.wait_ge(w_hi_ready, i * 2 + (n + 1))
                nc.vector.tensor_tensor(w_lo[:, n % 2, :], w_raw[:, n % 2, :], w_hi[:, n % 2, :].bitcast(fp32),
                                        ALU.subtract).then_inc(w_lo_ready[n % 2], 1)

            def both_lo(name, i=0, side=None, hooks={}):
                for slot in range(2):
                    for k in range(4):
                        if side:
                            side()
                        if 4 * slot + k in hooks:
                            hooks[4 * slot + k]()
                    split_lo(name, slot, i)

            def norm_var(name, j):
                dve.wait_ge(ssq_ready, ssq_count(name, j))
                nc.vector.tensor_scalar(ssq[:, j:j + 1], ssq[:, j:j + 1], 1.0 / D, EPS, ALU.mult, ALU.add).then_inc(var_ready, 1)

            def norm_root(name, j):
                dve.wait_ge(sd_ready, ssq_count(name, j))
                nc.vector.reciprocal(rstd[:, j:j + 1], rstd[:, j:j + 1])
                then()

            def normed(src, j, xn=xn):
                nc.vector.tensor_scalar(xn[:, j, :], src[:, j, :], rstd[:, j:j + 1], None, ALU.mult).then_inc(xn_ready, 1)

            def norm_lo(name, gain, hi, lo, n, kts=range(KT)):
                for kt in kts:
                    dve.wait_ge(hhi_ready, HT_AT[name] + kt + 1)
                    bank = banks[4 + kt % 4 if name == "mem" else kt]
                    nc.vector.scalar_tensor_tensor(lo[:, kt, :], bank[:, 0:n], par_col(gain, kt),
                                                   hi[:, kt, :].bitcast(fp32), ALU.mult, ALU.subtract).then_inc(hlo_ready, 1)

            def gated(dst, tanh, bank):
                return nc.vector.scalar_tensor_tensor(dst, tanh, 1.0, bank[:], ALU.add, ALU.mult)

            def with_bias(bank, bias_cols, dst, col):
                return nc.vector.tensor_tensor_reduce(out=dst, in0=bank, in1=bias_cols, scale=-1.0, scalar=3e38,
                                                      op0=ALU.add, op1=ALU.min, accum_out=nmax[:, col:col + 1])

            def attend(units, key, base_u, y_at):
                def output(k):
                    dst = units[k][3]
                    dve.wait_ge(o_done, base_u + k + 1)
                    nc.vector.reciprocal(rsum[:, k % 4:k % 4 + 1], psum_p[:, k % 4:k % 4 + 1])
                    then()
                    nc.vector.tensor_scalar(dst, O_BANK[:, 0:dst.shape[-1]], rsum[:, k % 4:k % 4 + 1], None,
                                            ALU.mult).then_inc(o_out, 1)

                yield
                for k, (w, cols, number, _) in enumerate(units):
                    dve.wait_ge(sc_done, SC_AT[key] + k + 1)
                    dve.wait_ge(bias_ready, number)
                    if k >= 2:
                        dve.wait_ge(p_ready, base_u + k - 1)
                    with_bias(banks[4 + k % 2][:, 0:w], cols, z[:, k % 2, 0:w], k % 4).then_inc(z_ready, 1)
                    if k >= 2:
                        output(k - 2)
                    yield
                output(len(units) - 2)
                yield
                output(len(units) - 1)
                yield
                for c in range(4):
                    dve.wait_ge(yhi_ready, OT_AT[key] + c + 1)
                    nc.vector.tensor_tensor(y_lo[:, y_at + c, :], banks[4 + c][:], y_hi[:, y_at + c, :].bitcast(fp32),
                                            ALU.subtract).then_inc(ylo_ready, 1)

            def ret_attend(g):
                def head_sum(hh):
                    dve.wait_ge(so_out, 4 * g + hh + 1)
                    nc.vector.tensor_reduce(ossq.rearrange("p (j h) -> p j h", h=4)[:, :, hh],
                                            o_squares[:, :, hh * P:hh * P + P], AX.X, ALU.add)

                yield
                for hh in range(4):
                    head = 4 * g + hh
                    dve.wait_ge(dec_ready, head + 1)
                    if head >= 2:
                        dve.wait_ge(so_done, head - 1)
                    for c in range(NT):
                        r = 4 * head + c
                        dve.wait_ge(sc_done, SC_AT["r"] + r + 1)
                        n = S - c * P
                        nc.vector.tensor_tensor(st[:, hh % 2, ST_AT[c]:ST_AT[c] + n], banks[4 + r % 2][:, 0:n],
                                                decay[:, hh % 2, 0:n], ALU.mult).then_inc(st_ready, 1)
                        if c == 3 and hh >= 1:
                            head_sum(hh - 1)
                        yield
                head_sum(3)
                then()

            def group_scale(key, tokens, groups, const):
                n, sums, roots = O_NORM[key], ossq[:, 0:groups], orstd[:, 0:groups]
                nc.vector.tensor_scalar(sums, sums, 1.0 / P, EPS, ALU.mult, ALU.add).then_inc(ovar_ready, 1)
                dve.wait_ge(osd_ready, n + 1)
                nc.vector.reciprocal(roots, sums)
                then()
                if const != 1.0:
                    nc.vector.tensor_scalar(roots, roots, const, None, ALU.mult)
                    then()
                o3 = tokens.rearrange("p j (h e) -> p (j h) e", e=P)
                nc.vector.tensor_tensor(o3, o3, roots.rearrange("p (a b) -> p a b", b=1).to_broadcast([P, groups, P]),
                                        ALU.mult).then_inc(on_ready, 1)

            def group_gate(key, gains, gain_at, tiles, b0, g_at, y_at):
                for c in range(tiles):
                    gate_one(key, gains, gain_at, b0, g_at, c)
                for c in range(tiles):
                    gate_lo(key, g_at, y_at, c)

            def gate_one(key, gains, gain_at, b0, g_at, c):
                dve.wait_ge(oT_done, OT_AT[key] + c + 1)
                nc.vector.scalar_tensor_tensor(gate[:, g_at + c, :], banks[b0 + c][:], par_col(gains, gain_at + c),
                                               gate[:, g_at + c, :], ALU.mult, ALU.mult).then_inc(y_ready, 1)

            def gate_lo(key, g_at, y_at, c):
                dve.wait_ge(yhi_ready, OT_AT[key] + c + 1)
                nc.vector.tensor_tensor(y_lo[:, y_at + c, :], gate[:, g_at + c, :], y_hi[:, y_at + c, :].bitcast(fp32),
                                        ALU.subtract).then_inc(ylo_ready, 1)

            def gates_beside(g):
                def gated(c):
                    dve.wait_ge(acc_out[c], TILE_AT[f"rg{g}"] // 4 + 1)
                    gate_one(f"r{g}", "ret_g", 4 * g, 4, 0, c)

                def low(c):
                    gate_lo(f"r{g}", 0, 4 * g, c)

                def last():
                    gated(2)
                    low(1)
                    gated(3)
                    low(2)
                    low(3)

                return {3: lambda: gated(0), 5: lambda: (gated(1), low(0)), 7: last}

            def diff_attend(g):
                def mix(k):
                    w = (k % NT + 1) * P
                    a = 2 * (k % 2)
                    dve.wait_ge(p_ready, Z_AT["d"] + 16 * g + 2 * k + 2)
                    r1, ratio = rsum[:, 4 + k % 2:5 + k % 2], rsl[:, k % 2:k % 2 + 1]
                    nc.vector.reciprocal(r1, psum_p[:, a + 1:a + 2])
                    nc.vector.reciprocal(rsum[:, k % 4:k % 4 + 1], psum_p[:, a:a + 1])
                    then()
                    nc.vector.scalar_tensor_tensor(ratio, psum_p[:, a:a + 1], lam_col, r1, ALU.mult, ALU.mult)
                    then()
                    nc.vector.scalar_tensor_tensor(dprob[:, a, 0:w], dprob[:, a + 1, 0:w], ratio,
                                                   dprob[:, a, 0:w], ALU.mult, ALU.add).then_inc(a_ready, 1)

                yield
                for k in range(8):
                    hh, t = k // NT, k % NT
                    dve.wait_ge(bias_ready, 9 + 2 * g + hh + 1)
                    for m in range(2):
                        v = 2 * k + m
                        dve.wait_ge(sc_done, SC_AT["d"] + 16 * g + v + 1)
                        if k >= 2:
                            dve.wait_ge(pT_done, U_D + 8 * g + k - 1)
                        with_bias(banks[4 + m][:, 0:(t + 1) * P], bias2[:, hh % 2, (3 - t) * P:S],
                                  dprob[:, v % 4, 0:(t + 1) * P], v % 4).then_inc(z_ready, 1)
                    mix(k)
                    yield
                yield
                yield

            def diff_finish(g):
                dve.wait_ge(o_out, U_D + 8 * g + 8)
                group_scale(f"d{g}", do_tok[g % 2], 8, (1.0 - LAM_INIT) / 2)
                yield
                group_gate(f"d{g}", "sub_g", 2 * g, 2, 6, 2 * (g % 2), 2 * g)
                yield

            def both(*parts):
                for part in parts:
                    yield from part

            nc.vector.memset(stats[:, 41:42], 64 * EPS)
            nc.vector.memset(stats[:, 42:43], EPS).then_inc(eps_ready, 1)
            for j in range(NT):
                norm_var("mix", j)
                norm_root("mix", j)
                normed(x_in_tok, j, xn0)
            dve.wait_ge(half_hi, 1)
            nc.vector.tensor_tensor(tile_cols(w_lo, 0), tile_cols(w_raw, 0), tile_cols(w_hi, 0).bitcast(fp32),
                                    ALU.subtract).then_inc(half_lo, 1)
            norm_lo("mix", "mix_g", h_hi, h_lo, S)
            dve.wait_ge(w_hi_ready, 1)
            nc.vector.tensor_tensor(tile_cols(w_lo, 1), tile_cols(w_raw, 1), tile_cols(w_hi, 1).bitcast(fp32),
                                    ALU.subtract).then_inc(w_lo_ready[0], 1)
            split_lo("xa", 1, ahead=0)
            for j in range(2):
                norm_var("mem", j)
                norm_root("mem", j)
                if j == 0:
                    dve.wait_ge(hT_done, KT)
                normed(mem_tok, j, xn0)
            dve.wait_ge(small_in, 16)
            dve.wait_ge(lqk_ready, 16)
            lam4 = params[:, COLS["lam"]:COLS["lam"] + 4]
            neg, e, zz, z2, acc = (spt[:, 0:4], spt[:, 4:8], spt[:, 8:12], spt[:, 12:16], spt[:, 16:20])
            nc.vector.tensor_scalar(neg, lam4, -1.0, None, ALU.mult)
            then()
            nc.vector.tensor_tensor(neg, neg, lam4, ALU.max).then_inc(sp_e, 1)
            lprod = lqk[:, 0:2, :]
            nc.vector.tensor_tensor(lprod, lprod, lqk[:, 2:4, :], ALU.mult)
            then()
            nc.vector.tensor_reduce(lam_t[:, 0:2], lprod, AX.X, ALU.add).then_inc(lam_s, 1)
            nc.vector.memset(xa_pad[:, :, 0:3], 0.0)
            dve.wait_ge(sp_e, 2)
            nc.vector.tensor_scalar(acc, e, 2.0, None, ALU.add)
            then()
            nc.vector.reciprocal(acc, acc)
            then()
            nc.vector.tensor_tensor(zz, e, acc, ALU.mult)
            then()
            nc.vector.tensor_tensor(z2, zz, zz, ALU.mult)
            then()
            nc.vector.tensor_scalar(acc, z2, 1.0 / 15, None, ALU.mult)
            for k in (13, 11, 9, 7, 5, 3):
                then()
                nc.vector.scalar_tensor_tensor(acc, acc, 1.0 / k, z2, ALU.add, ALU.mult)
            then()
            nc.vector.scalar_tensor_tensor(acc, acc, 1.0, zz, ALU.add, ALU.mult)
            nc.vector.tensor_scalar(neg, lam4, -1.0, 0.0, ALU.mult, ALU.max)
            then()
            nc.vector.scalar_tensor_tensor(acc, acc, 2.0, neg, ALU.mult, ALU.add)
            then()
            nc.vector.tensor_scalar(sp8, acc, 8.0, None, ALU.mult)
            nc.vector.tensor_scalar(nsp8, acc, -8.0, None, ALU.mult).then_inc(sp_ready, 1)
            dve.wait_ge(lam_e, 1)
            nc.vector.tensor_tensor(lam_col, lam_t[:, 3:4], lam_t[:, 2:3], ALU.subtract)
            then()
            nc.vector.tensor_scalar(lam_col, lam_col, -LAM_INIT, None, ALU.add)
            then()
            def convolve(tiles):
                for c in tiles:
                    dve.wait_ge(acc_out[c], 1)
                    w = lambda k: par_col("lconv_w", 4 * c + k)
                    nc.vector.tensor_scalar(xc[:, c, :], xa_pad[:, c, 3:3 + S], w(3), par_col("lconv_b", c), ALU.mult, ALU.add)
                    for k in (2, 1, 0):
                        then()
                        done = nc.vector.scalar_tensor_tensor(xc[:, c, :], xa_pad[:, c, k:k + S], w(k), xc[:, c, :],
                                                              ALU.mult, ALU.add)
                    done.then_inc(xc_ready, 1)

            split_lo("xa", 0)
            convolve((0, 1))
            norm_lo("mem", "mem_g", mem_hi, mem_lo, MEM, range(4))
            split_lo("xa", 1)
            norm_lo("mem", "mem_g", mem_hi, mem_lo, MEM, range(4, 8))
            convolve((2,))
            split_lo("ga", 0)
            convolve((3,))
            split_lo("ga", 1)
            both_lo("memk")
            both_lo("memv")

            def lru_multiplier(c):
                dve.wait_ge(lru_ta, 4)
                s = c % 2
                nc.vector.tensor_scalar(lru_tmp[:, s, :], lru_t[:, c, :], 1.0, None, ALU.add)
                then()
                nc.vector.reciprocal(lru_tmp[:, s, :], lru_tmp[:, s, :])
                then()
                nc.vector.scalar_tensor_tensor(lru_t[:, c, :], lru_t[:, c, :], 2.0, lru_tmp[:, s, :],
                                               ALU.mult, ALU.mult).then_inc(lru_m2, 1)

            both_lo("xq", hooks={2 * c + 1: lambda c=c: lru_multiplier(c) for c in range(4)})

            def lru_outputs():
                for c in range(4):
                    dve.wait_ge(lru_ta, 8)
                    dve.wait_ge(lru_mult, c + 1)
                    dve.wait_ge(ixc_ready, c + 1)
                    nc.vector.tensor_tensor(lru_i[:, c, :], lru_i[:, c, :], lru_t[:, c, :], ALU.mult)
                    then()
                    nc.vector.tensor_tensor_scan(xc[:, c, :], lru_r[:, c, :], lru_i[:, c, :], 0.0, ALU.mult, ALU.add)
                    yield
                    then()
                    dve.wait_ge(acc_out[c], 2)
                    nc.vector.tensor_tensor(xc[:, c, :], xc[:, c, :], ga_gelu[:, c, :], ALU.mult)
                    then()
                    nc.vector.tensor_copy(y_hi[:, c, :], xc[:, c, :])
                    yield
                    then()
                    nc.vector.tensor_tensor(y_lo[:, c, :], xc[:, c, :], y_hi[:, c, :].bitcast(fp32),
                                            ALU.subtract).then_inc(ya_ready, 1)
                    yield

            steps = lru_outputs()
            both_lo("mq", side=pacer(steps, 3, 2))
            finish(steps)
            steps = attend([(MEM, bias1[:, k // NT % 2, 0:MEM], 1, o_tok1[:, k % NT, k // NT * P:k // NT * P + P])
                            for k in range(16)], "x", U_X, 8)
            side = pacer(steps, *PACE["x"])
            both_lo("mk", side=side)
            both_lo("mv", side=side)
            finish(steps)
            steps = attend([((t + 1) * P, bias1[:, h % 2, (3 - t) * P:S], h + 2, o_tok1[:, t, h * 64:h * 64 + 64])
                            for h, t in MOBA_UNITS], "m", U_M, 4)
            side = pacer(steps, *PACE["m"])
            for i in range(2):
                both_lo("gate0", i, side=side)
            for slot in range(2):
                for c in range(4):
                    k = 4 * slot + c
                    side()
                    dve.wait_ge(acc_done, TILE_AT["branch0"] + k + 1)
                    dve.wait_ge(acc_out[c], TILE_AT["gate0"] // 4 + slot + 1)
                    gated(merged[:, k, :], merged[:, k, :], banks[c]).then_inc(acc_out[c], 1)
                split_lo("branch0", slot)
            then()
            nc.vector.engine_nop().then_inc(m_ready, 8)
            finish(steps)
            def merged_lo(k):
                dve.wait_ge(mhi_ready, k + 1)
                nc.vector.scalar_tensor_tensor(h_lo[:, k, :], merged[:, k, :], 0.5, h_hi[:, k, :].bitcast(fp32),
                                               ALU.mult, ALU.subtract).then_inc(mlo_ready, 1)

            for n in (1, 2):
                with dve.Fori(0, 2) as i:
                    both_lo(f"gate{n}", i)
                t0 = TILE_AT[f"branch{n}"]
                for slot in range(2):
                    for c in range(4):
                        k = 4 * slot + c
                        dve.wait_ge(acc_done, t0 + k + 1)
                        dve.wait_ge(acc_out[k % 4], TILE_AT[f"gate{n}"] // 4 + k // 4 + 1)
                        gated(mtmp[:, c, :], gT[:, k, :], banks[c]).then_inc(acc_out[c], 1)
                        dve.wait_ge(acc_out[c], t0 // 4 + slot + 1)
                        nc.vector.tensor_tensor(merged[:, k, :], merged[:, k, :], mtmp[:, c, :], ALU.add).then_inc(m_ready, 1)
                        if n == 2 and k >= 1:
                            merged_lo(k - 1)
                    split_lo(f"branch{n}", slot)
            merged_lo(KT - 1)
            dve.wait_ge(x_in[1], 16)

            def add_residual(name, t_off, half, j):
                dve.wait_ge(acc_done, TILE_AT[name] + t_off + j + 1)
                xs = x_tok[:, j, half * S:half * S + S]
                return nc.vector.tensor_tensor(xs, xs, banks[j][:], ALU.add).then_inc(acc_out[j], 1)

            def residual_done():
                then()
                nc.vector.engine_nop().then_inc(x1_ready, 1)

            split_lo("wo", 0, 0)
            for j in range(NT):
                add_residual("wo", 0, 0, j)
            split_lo("wo", 1, 0)
            split_lo("wo", 0, 1)
            for j in range(NT):
                add_residual("wo", 4, 1, j)
                residual_done()
                if j:
                    norm_root("ffn", j - 1)
                    normed(x_tok, j - 1)
                norm_var("ffn", j)
            norm_root("ffn", NT - 1)
            normed(x_tok, NT - 1)
            norm_lo("ffn", "ffn_g", h_hi, h_lo, S)
            split_lo("wo", 1, 1)
            nc.vector.memset(gpad[:, :, 0:2], 0.0).then_inc(conv_ready, 1)
            for f in range(2):
                t0 = TILE_AT[f"ffn{f}"]
                with dve.Fori(0, 6) as i:
                    for c in range(2):
                        dve.wait_ge(acc_out[c], i + (t0 // 4 + 1))
                        col = lambda name, k: params[:, ds(i * 2 * k[1] + (COLS[name] + (12 * f + c) * k[1] + k[0]), 1)]
                        nc.vector.tensor_scalar(cv[:, c, :], gpad[:, c, 2:2 + S], col("fconv_w", (2, 3)), col("fconv_b", (0, 1)),
                                                ALU.mult, ALU.add)
                        then()
                        nc.vector.scalar_tensor_tensor(cv[:, c, :], gpad[:, c, 1:1 + S], col("fconv_w", (1, 3)), cv[:, c, :],
                                                       ALU.mult, ALU.add)
                        then()
                        nc.vector.scalar_tensor_tensor(cv[:, c, :], gpad[:, c, 0:S], col("fconv_w", (0, 3)), cv[:, c, :],
                                                       ALU.mult, ALU.add).then_inc(conv_ready, 1)
                    split_lo(f"ffn{f}", 0, i)
                    for c in range(2):
                        dve.wait_ge(gelu_ready, i * 2 + (12 * f + c + 1))
                        dve.wait_ge(acc_done, i * 4 + (t0 + 2 + c + 1))
                        nc.vector.tensor_tensor(pr[:, c, :], gl[:, c, :], banks[2 + c][:], ALU.mult).then_inc(acc_out[2 + c], 1)
                    for c in range(2):
                        dve.wait_ge(ahi_ready, i * 2 + (12 * f + c + 1))
                        nc.vector.tensor_tensor(y_lo[:, ds(i * 2 + c, 1), :].rearrange("p a s -> p (a s)"), pr[:, c, :],
                                                y_hi[:, ds(i * 2 + c, 1), :].rearrange("p a s -> p (a s)").bitcast(fp32),
                                                ALU.subtract).then_inc(alo_ready, 1)
                    split_lo(f"ffn{f}", 1, i)
                name = f"down{f}"
                for half in range(2):
                    for k in range(2):
                        split_lo(name, 3 * half + k)
                    if f == 0 or half == 0:
                        for j in range(NT):
                            add_residual(name, 4 * half, half, j)
                        split_lo(name, 3 * half + 2)
            dve.wait_ge(x_in[3], 16)

            def last_stats(j):
                norm_var("final", j)
                norm_root("final", j)
                r, m2, r2 = rstd[:, j:j + 1], ssq2[:, j:j + 1], rstd2[:, j:j + 1]
                dve.wait_ge(ssq_ready, ssq_count("norm2", j))
                nc.vector.scalar_tensor_tensor(m2, m2, 1.0 / D, r, ALU.mult, ALU.mult)
                then()
                nc.vector.tensor_scalar(m2, m2, r, EPS, ALU.mult, ALU.add).then_inc(var_ready, 1)
                dve.wait_ge(sd_ready, ssq_count("norm2", j))
                nc.vector.reciprocal(r2, r2)
                then()
                nc.vector.tensor_scalar(xn[:, j, :], xn[:, j, :], r, r2, ALU.mult, ALU.mult).then_inc(xn_ready, 1)

            for j in range(NT):
                add_residual("down1", 4, 1, j)
                residual_done()
                nc.vector.tensor_tensor(xn[:, j, :], x_tok[:, j, :], gain_row, ALU.mult).then_inc(xg_ready, 1)
                if j:
                    last_stats(j - 1)
            last_stats(NT - 1)
            norm_lo("norm2", "norm2_g", h_hi, h_lo, S)
            split_lo("down1", 5)
            for j in range(NT):
                nc.vector.scalar_tensor_tensor(x_tok[:, j, :], x_tok[:, j, :], rstd[:, j:j + 1], gain_row,
                                               ALU.mult, ALU.mult).then_inc(xb_ready, 1)
            both_lo("rqk0")
            both_lo("rv0")
            steps = ret_attend(0)
            side = pacer(steps, *PACE["r"])
            both_lo("rqk1", side=side)
            both_lo("rv1", side=side)
            finish(steps)
            group_scale("r0", o_tok, 16, 1.0)
            both_lo("rg0", hooks=gates_beside(0))
            steps = ret_attend(1)
            side = pacer(steps, *PACE["r"])
            for i in range(2):
                both_lo("rmg", i, side=side)
            finish(steps)
            group_scale("r1", o_tok, 16, 1.0)
            both_lo("rg1", hooks=gates_beside(1))

            def gate_tile(name, k):
                return TILE_AT[name] // 4 + k // 4 + 1
            for i in range(2):
                for slot in range(2):
                    for c in range(2):
                        b = 2 * slot + c
                        k = 4 * i + b
                        dve.wait_ge(acc_done, TILE_AT["rwo"] + k + 1)
                        dve.wait_ge(acc_out[b], gate_tile("rmg", k))
                        gated(gT[:, k, :], gT[:, k, :], banks[b]).then_inc(acc_out[b], 1)
                    split_lo("rwo", slot, i)
            then()
            nc.vector.engine_nop().then_inc(mret_ready, 8)
            def unit_norms(g):
                for c in range(4):
                    dve.wait_ge(acc_out[c], TILE_AT[f"dqk{g}"] // 4 + 1)
                    v = (dqT if c < 2 else dkT)[g % 2][:, c % 2, :]
                    for half in range(2):
                        cols = slice(half * S // 2, (half + 1) * S // 2)
                        nc.vector.reciprocal(dsq[:, c, cols], dsq[:, c, cols])
                        yield
                    then()
                    nc.vector.scalar_tensor_tensor(v, v, par_col("dq_g" if c < 2 else "dk_g"), dsq[:, c, :],
                                                   ALU.mult, ALU.mult).then_inc(dn_ready, 1)
                    yield

            def beside(g, attention, phases):
                norms = both(lead(7), unit_norms(g)) if g < 4 else lead(0)
                paces = [pacer(attention, *PACE["d"]), pacer(norms, 1, 1)]

                def side():
                    for slot in paces:
                        slot()

                def twice_silu(name, c):
                    dve.wait_ge(th_ready, (4 if name == "dg1" else 0) + c + 1)
                    gated(gate[:, c, :], gate[:, c, :], banks[c]).then_inc(acc_out[c], 1)

                for name, i in phases:
                    silus = {}
                    if name in ("dg0", "dg1"):
                        silus = {n: lambda c=c: twice_silu(name, c) for c, n in enumerate((3, 5, 7))}
                    elif (name, i) in (("dqk2", 0), ("dmg", 0)):
                        silus = {0: lambda: twice_silu("dg0" if name == "dqk2" else "dg1", 3)}
                    both_lo(name, i, side=side, hooks=silus)
                finish(attention)
                finish(norms)

            beside(0, lead(0), [("dqk0", 0), ("dv0", 0)])
            for g, phases in enumerate((("dqk1", "dg0"), ("dqk2", "dv1"), ("dqk3", "dg1"))):
                beside(g + 1, both(*([diff_finish(g - 1)] if g else []), lead(LEAD[g]), diff_attend(g)),
                       [(name, 0) for name in phases])
            beside(4, both(diff_finish(2), lead(LEAD[3]), diff_attend(3), diff_finish(3)), [("dmg", 0), ("dmg", 1)])
            dve.wait_ge(x_in[5], 16)
            for i in range(2):
                for slot in range(2):
                    for c in range(2):
                        b = 2 * slot + c
                        k = 4 * i + b
                        dve.wait_ge(acc_done, TILE_AT["dwo"] + k + 1)
                        dve.wait_ge(acc_out[b], gate_tile("dmg", k))
                        gated(gT[:, k, :], gT[:, k, :], banks[b]).then_inc(acc_out[b], 1)
                        dve.wait_ge(acc_out[b], gate_tile("dwo", k))
                        nc.vector.tensor_tensor(gT[:, k, :], gT[:, k, :], m_back[:, k, :], ALU.add).then_inc(m_ready, 1)
                        dve.wait_ge(mhi_ready, M_AT["two"] + k + 1)
                        nc.vector.scalar_tensor_tensor(h_lo[:, k, :], gT[:, k, :], 0.5, h_hi[:, k, :].bitcast(fp32),
                                                       ALU.mult, ALU.subtract).then_inc(mlo_ready, 1)
                    split_lo("dwo", slot, i)
            dve.wait_ge(x_in[4], 16)
            for half in range(2):
                split_lo("wo2", 0, half)
                for j in range(NT):
                    dve.wait_ge(acc_done, TILE_AT["wo2"] + 4 * half + j + 1)
                    cols = slice(half * S, half * S + S)
                    nc.vector.tensor_tensor(res[:, j, cols], xb[:, j, cols], banks[4 * half + j][:], ALU.add).then_inc(res_ready, 1)
                split_lo("wo2", 1, half)


_INPUTS = ("x", "mem", "par", "lru_w", "lqk", "final_g", "wstream")


def _laid_out(v):
    a = {k: np.asarray(t) for k, t in v.items()}

    def cols(t, n):
        return t.reshape(n, P).T

    def strip_a(w, c0):
        return w[:, c0:c0 + 256].reshape(KT, P, 256).transpose(1, 0, 2).reshape(P, STRIP)

    def strip_b(w, r0, c0):
        return w[r0:r0 + 512, c0:c0 + 512].reshape(4, P, 512).transpose(1, 0, 2).reshape(P, STRIP)

    w1, w2, kv = a["w_in"][0], a["w_in_2"][0], a["w_mem_kv"][0]
    strips = []

    def take_a(w, c0, n):
        strips.extend(strip_a(w, c0 + 256 * i) for i in range(n))

    def take_b(w, c0, halves, r0=0, k=2):
        strips.extend(strip_b(w, r0 + 512 * i, c0 + 512 * h) for h in range(halves) for i in range(k))

    for c0 in (0, 512):
        take_a(w1, c0, 2)
    take_a(kv, 0, 2)
    take_b(kv, 512, 1)
    take_a(w1, 2560, 2)
    take_a(w1, 1024, 2)
    take_a(w1, 1536, 2)
    take_b(w1, 2048, 1)
    for n in range(3):
        take_a(w1, 3072 + D * n, 4)
        take_b(a["w_branch"][0, n], 0, 2, k=1)
    take_b(a["w_out"][0], 0, 2)
    wg, wu, wd = a["w_ffn_gate"][0], a["w_ffn_up"][0], a["w_ffn_down"][0]
    for f in range(2):
        for i in range(6):
            take_a(wg, (6 * f + i) * 256, 1)
            take_a(wu, (6 * f + i) * 256, 1)
        take_b(wd, 0, 2, r0=f * FF // 2, k=3)
    for g in range(2):
        take_a(w2, 256 * g, 1)
        take_a(w2, 512 + 256 * g, 1)
        take_b(w2, 1024 + 512 * g, 1)
    take_a(w2, 2048, 2)
    take_a(w2, 7168, 4)
    take_a(w2, 2560, 2)
    take_a(a["ret_w_o_2"][0], 0, 4)
    for g in range(4):
        take_a(w2, 3072 + 256 * g, 1)
        take_a(w2, 4096 + 256 * g, 1)
        if g % 2 == 0:
            take_b(w2, 5120 + 256 * g, 1)
        else:
            take_a(w2, 6144 + 256 * (g - 1), 2)
    take_a(w2, 8192, 4)
    take_a(a["diff_w_o_2"][0], 0, 4)
    take_b(a["w_out_2"][0], 0, 2)
    assert len(strips) == STRIPS

    twice = lambda t: np.concatenate([t, t]).reshape(P, 1)
    small = np.concatenate([
        cols(a["mix_norm_gain"][0], 8), cols(a["mem_norm_gain"][0], 8), cols(a["ffn_norm_gain"][0], 8),
        cols(a["norm_g_2"][0], 8),
        a["lru_conv_w"][0].reshape(4, 4, P).transpose(2, 1, 0).reshape(P, 16), cols(a["lru_conv_b"][0], 4),
        cols(a["lru_b_a"][0].reshape(-1), 4), cols(a["lru_b_x"][0].reshape(-1), 4), cols(a["lru_lambda"][0], 4),
        a["ffn_conv_w"][0].reshape(3, FFT, P).transpose(2, 1, 0).reshape(P, 3 * FFT), cols(a["ffn_conv_b"][0], FFT),
        cols(a["ret_norm_g_2"][0], 8), twice(a["diff_q_norm_g_2"][0]), twice(a["diff_k_norm_g_2"][0]),
        cols(a["diff_sub_norm_g_2"][0], 8)], axis=1)
    lru = np.stack([a[k][0].reshape(4, P, 64).transpose(1, 0, 2) for k in ("lru_w_a", "lru_w_x")], axis=1)
    lq = np.stack([a[f"diff_{k}_2"][0] for k in ("lq1", "lq2", "lk1", "lk2")])
    return {
        "x": a["x"][0], "mem": a["mem"][0], "par": small, "lru_w": lru,
        "lqk": np.broadcast_to(lq, (P, 4, 64)), "final_g": np.broadcast_to(a["final_norm_gain"], (P, D)),
        "wstream": np.concatenate(strips, axis=0),
    }


def kernel(**inputs):
    import concourse.bacc as _bacc
    from concourse.bass_utils import run_bass_kernel_spmd as _run

    nc = _bacc.Bacc("TRN2", target_bir_lowering=False, num_devices=1)
    laid = _laid_out(inputs)
    arrays, args = {}, []
    for name in _INPUTS:
        arr = np.ascontiguousarray(laid[name])
        arrays[f"in_{name}"] = arr
        args.append(nc.dram_tensor(f"in_{name}", arr.shape, mybir.dt.from_np(arr.dtype), kind="ExternalInput").ap())
    out = nc.dram_tensor("out_dram", (S, D), mybir.dt.float32, kind="ExternalOutput").ap()
    xb = nc.dram_tensor("xb_dram", (S, D), mybir.dt.float32, kind="Internal").ap()
    mret = nc.dram_tensor("mret_dram", (P, KT * S), mybir.dt.float32, kind="Internal").ap()
    hybrid_block_kernel(nc, *args, out, xb, mret)
    r = _run(nc, [arrays], core_ids=[0])
    return r.results[0]["out_dram"].reshape(1, S, D)
```
